# Optimizing a Trainium2 kernel written in Bass

```python
import math
import jax, jax.numpy as jnp
from jax import lax
import numpy as np

D_MODEL = 1024
BATCH = 1
SEQ = 512
DEPTH = 2
DEC_BATCH = 8
DEC_SEQ = 8
PAST_LEN = 4096
PAGE_SIZE = 128

N_A_LAYERS = (DEPTH + 1) // 2
N_C_LAYERS = DEPTH // 2
A_HEADS = 4
A_DK = 128
A_DV = 128
A_CONV = 4
A_CHUNK = 64
A_QK = A_HEADS * A_DK
A_V = A_HEADS * A_DV
A_CONV_CH = 2 * A_QK + A_V
B_GROUPS = 4
B_GW = 128
B_WINDOWS = (2, 4, 8, 16)
B_HIST = max(B_WINDOWS) - 1
B_WIDTH = B_GROUPS * B_GW
EVEN_IN = A_CONV_CH + A_V + 2 * A_HEADS + B_WIDTH
EVEN_MIX = A_V + B_WIDTH
C_WIDTH = D_MODEL
C_HEADS = 4
C_HW = C_WIDTH // C_HEADS
C_CONV = 4
C_GATE = 8.0
ODD_IN = 2 * C_WIDTH
N_EXPERTS = 16
N_GROUPS = 4
EPG = N_EXPERTS // N_GROUPS
TOP_GROUPS = 1
TOP_K = 2
D_EXPERT = 512
ALPHA = (2 * DEPTH) ** 0.25
BETA_INIT = (8 * DEPTH) ** -0.25
LN_EPS = 1e-5
RMS_EPS = 1e-6
F32 = jnp.float32

kernel_name = 'hybrid_deltanet_pool_rglru_moe_step'

def layer_norm(x, g, b):
    xf = x.astype(F32)
    mu = xf.mean(-1, keepdims=True)
    var = jnp.square(xf - mu).mean(-1, keepdims=True)
    return ((xf - mu) * lax.rsqrt(var + LN_EPS) * g + b).astype(x.dtype)

def l2norm(t):
    tf = t.astype(F32)
    return tf * lax.rsqrt(jnp.sum(tf * tf, -1, keepdims=True) + 1e-6)

def causal_conv(u, hist, w, b=None):
    T = u.shape[1]
    ext = jnp.concatenate([hist.astype(u.dtype), u], axis=1)
    out = sum(ext[:, j:j + T] * w[j] for j in range(w.shape[0]))
    if b is not None:
        out = out + b
    return out, ext[:, T:]

def gated_delta_rule(q, k, v, g, beta, s0):
    bsz, T, H, dk = q.shape
    dv = v.shape[-1]
    C = min(A_CHUNK, T)
    n = -(-T // C)
    pad = n * C - T

    def blocks(t):
        t = jnp.pad(t.astype(F32), [(0, 0), (0, pad)] + [(0, 0)] * (t.ndim - 2))
        t = t.reshape((bsz, n, C) + t.shape[2:])
        return jnp.moveaxis(t, 3, 1)

    q, k, v, g, beta = blocks(q), blocks(k), blocks(v), blocks(g), blocks(beta)
    q = q * dk ** -0.5
    gc = jnp.cumsum(g, axis=-1)
    incl = jnp.tril(jnp.ones((C, C), bool))
    strict = jnp.tril(jnp.ones((C, C), bool), -1)
    diff = gc[..., :, None] - gc[..., None, :]
    decay = jnp.where(incl, jnp.exp(jnp.where(incl, diff, 0.0)), 0.0)
    kb = k * beta[..., None]
    m = jnp.where(strict, jnp.einsum('bhnid,bhnjd->bhnij', kb, k) * decay, 0.0)
    neg = -m
    tinv = jnp.eye(C, dtype=F32) + neg
    power = neg
    for _ in range(max((C - 1).bit_length() - 1, 0)):
        power = power @ power
        tinv = tinv + tinv @ power
    u_in = tinv @ (v * beta[..., None])
    w_in = tinv @ (kb * jnp.exp(gc)[..., None])
    a_intra = jnp.where(incl, jnp.einsum('bhnid,bhnjd->bhnij', q, k) * decay, 0.0)
    q_dec = q * jnp.exp(gc)[..., None]
    g_last = gc[..., -1]
    k_dec = k * jnp.exp(g_last[..., None] - gc)[..., None]

    def step(s, xs):
        u_c, w_c, a_c, qd_c, kd_c, gl_c = xs
        u_new = u_c - w_c @ s
        o = qd_c @ s + a_c @ u_new
        s = s * jnp.exp(gl_c)[..., None, None] + jnp.swapaxes(kd_c, -1, -2) @ u_new
        return s, o

    xs = tuple(jnp.moveaxis(t, 2, 0) for t in (u_in, w_in, a_intra, q_dec, k_dec, g_last))
    s_fin, o = lax.scan(step, s0.astype(F32), xs)
    o = jnp.moveaxis(o, 0, 2).reshape(bsz, H, n * C, dv)[:, :, :T]
    return jnp.swapaxes(o, 1, 2), s_fin

def multiscale_pool(u, hist, hist_valid):
    bsz, T, _ = u.shape
    ext = jnp.concatenate([hist.astype(u.dtype), u], axis=1)
    extf = ext.astype(F32)
    cs = jnp.concatenate([jnp.zeros((bsz, 1, B_WIDTH), F32), jnp.cumsum(extf, axis=1)], axis=1)
    end = cs[:, B_HIST + 1:]
    cur = extf[:, B_HIST:]
    pos = jnp.arange(T) + 1 + hist_valid
    parts = []
    for gi, w in enumerate(B_WINDOWS):
        lo, hi = gi * B_GW, (gi + 1) * B_GW
        start = cs[:, B_HIST + 1 - w:B_HIST + 1 - w + T, lo:hi]
        cnt = jnp.minimum(pos, w).astype(F32)[None, :, None]
        parts.append((end[..., lo:hi] - start) / cnt - cur[..., lo:hi])
    return jnp.concatenate(parts, axis=-1), ext[:, T:]

def delta_pool_mixer(x, conv_hist, s0, pool_hist, hist_valid, w_in, conv_w, log_decay, dt_bias, norm_w, w_group, scale, w_out):
    bsz, T, _ = x.shape
    proj = x @ w_in
    c0 = A_CONV_CH
    c1 = c0 + A_V
    c2 = c1 + A_HEADS
    c3 = c2 + A_HEADS
    qkv, z, b_raw, a_raw, u = jnp.split(proj, [c0, c1, c2, c3], axis=-1)
    qkv, conv_new = causal_conv(qkv, conv_hist, conv_w)
    qkv = jax.nn.silu(qkv)
    q, k, v = jnp.split(qkv, [A_QK, 2 * A_QK], axis=-1)
    q = l2norm(q.reshape(bsz, T, A_HEADS, A_DK))
    k = l2norm(k.reshape(bsz, T, A_HEADS, A_DK))
    v = v.reshape(bsz, T, A_HEADS, A_DV)
    beta = jax.nn.sigmoid(b_raw.astype(F32))
    g = -jnp.exp(log_decay.astype(F32)) * jax.nn.softplus(a_raw.astype(F32) + dt_bias.astype(F32))
    o, s_new = gated_delta_rule(q, k, v, g, beta, s0)
    o = o * lax.rsqrt(jnp.mean(o * o, -1, keepdims=True) + RMS_EPS) * norm_w.astype(F32)
    o = o * jax.nn.silu(z.astype(F32)).reshape(bsz, T, A_HEADS, A_DV)
    o_a = o.reshape(bsz, T, A_V).astype(x.dtype)
    pooled, pool_new = multiscale_pool(u, pool_hist, hist_valid)
    o_b = jnp.einsum('btgc,gcd->btgd', pooled.reshape(bsz, T, B_GROUPS, B_GW), w_group.astype(F32))
    o_b = (o_b.reshape(bsz, T, B_WIDTH) * scale.astype(F32)).astype(x.dtype)
    y = jnp.concatenate([o_a, o_b], axis=-1) @ w_out
    return y, conv_new.astype(conv_hist.dtype), s_new.astype(s0.dtype), pool_new.astype(pool_hist.dtype)

def rglru_mixer(x, conv_hist, h0, w_in, conv_w, conv_b, w_r, b_r, w_i, b_i, lam, w_out):
    bsz, T, _ = x.shape
    proj = x @ w_in
    y_br, x_br = jnp.split(proj, 2, axis=-1)
    y_br = jax.nn.gelu(y_br, approximate=True)
    xc, conv_new = causal_conv(x_br, conv_hist, conv_w, conv_b)
    xh = xc.reshape(bsz, T, C_HEADS, C_HW)
    r = jax.nn.sigmoid((jnp.einsum('bthi,hij->bthj', xh, w_r).reshape(bsz, T, C_WIDTH) + b_r).astype(F32))
    gi = jax.nn.sigmoid((jnp.einsum('bthi,hij->bthj', xh, w_i).reshape(bsz, T, C_WIDTH) + b_i).astype(F32))
    log_a = -C_GATE * r * jax.nn.softplus(-lam.astype(F32))
    a = jnp.exp(log_a)
    bt = jnp.sqrt(-jnp.expm1(2.0 * log_a)) * gi * xc.astype(F32)

    def step(h, ab):
        a_t, b_t = ab
        h = a_t * h + b_t
        return h, h

    h_last, hs = lax.scan(step, h0.astype(F32), (jnp.swapaxes(a, 0, 1), jnp.swapaxes(bt, 0, 1)))
    hs = jnp.swapaxes(hs, 0, 1).astype(x.dtype)
    y = (hs * y_br) @ w_out
    return y, conv_new.astype(conv_hist.dtype), h_last.astype(h0.dtype)

def moe(x, router_w, router_bias, w_gate, w_up, w_down):
    shp = x.shape
    xt = x.reshape(-1, D_MODEL)
    n = xt.shape[0]
    scores = jax.nn.sigmoid(xt.astype(F32) @ router_w.astype(F32))
    biased = scores + router_bias.astype(F32)
    grp_score = lax.top_k(biased.reshape(n, N_GROUPS, EPG), TOP_K)[0].sum(-1)
    _, g_idx = lax.top_k(grp_score, TOP_GROUPS)
    g_mask = jax.nn.one_hot(g_idx, N_GROUPS, dtype=F32).sum(-2)
    e_mask = jnp.repeat(g_mask, EPG, axis=-1) > 0
    _, e_idx = lax.top_k(jnp.where(e_mask, biased, -jnp.inf), TOP_K)
    w_sel = jnp.take_along_axis(scores, e_idx, axis=-1)
    w_sel = w_sel / jnp.sum(w_sel, -1, keepdims=True)
    combine = jnp.einsum('nk,nke->ne', w_sel, jax.nn.one_hot(e_idx, N_EXPERTS, dtype=F32)).astype(x.dtype)
    y = jnp.zeros_like(xt)
    for e in range(N_EXPERTS):
        h = jax.nn.silu(xt @ w_gate[e]) * (xt @ w_up[e])
        y = y + combine[:, e:e + 1] * (h @ w_down[e])
    return y.reshape(shp)

def trunk(x, states, hist_valid, weights):
    st_delta, st_dconv, st_pool, st_lru, st_lconv = states
    (ab_w_in, a_conv_w, a_log_decay, a_dt_bias, a_norm_w, b_w_group, b_scale, ab_w_out,
     c_w_in, c_conv_w, c_conv_b, c_w_r, c_b_r, c_w_i, c_b_i, c_lambda, c_w_out,
     ln_mix_g, ln_mix_b, ln_ffn_g, ln_ffn_b, router_w, router_bias, moe_w_gate, moe_w_up, moe_w_down) = weights
    n_delta, n_dconv, n_pool, n_lru, n_lconv = [], [], [], [], []
    for layer in range(DEPTH):
        j = layer // 2
        if layer % 2 == 0:
            h, dconv, delta, pool = delta_pool_mixer(
                x, st_dconv[j], st_delta[j], st_pool[j], hist_valid, ab_w_in[j], a_conv_w[j],
                a_log_decay[j], a_dt_bias[j], a_norm_w[j], b_w_group[j], b_scale[j], ab_w_out[j])
            n_delta.append(delta)
            n_dconv.append(dconv)
            n_pool.append(pool)
        else:
            h, lconv, lru = rglru_mixer(
                x, st_lconv[j], st_lru[j], c_w_in[j], c_conv_w[j], c_conv_b[j], c_w_r[j], c_b_r[j],
                c_w_i[j], c_b_i[j], c_lambda[j], c_w_out[j])
            n_lru.append(lru)
            n_lconv.append(lconv)
        x = layer_norm(ALPHA * x + h, ln_mix_g[layer], ln_mix_b[layer])
        f = moe(x, router_w, router_bias, moe_w_gate[layer], moe_w_up[layer], moe_w_down[layer])
        x = layer_norm(ALPHA * x + f, ln_ffn_g[layer], ln_ffn_b[layer])
    return (x, jnp.stack(n_delta), jnp.stack(n_dconv), jnp.stack(n_pool), jnp.stack(n_lru), jnp.stack(n_lconv))

def setup_inputs(seed: int = 0) -> dict:
    key = jax.random.key(seed)
    ks = iter(jax.random.split(key, 48))

    def nrm(shape, s):
        return jax.random.normal(next(ks), shape, F32) * s

    def gain(shape):
        return 1.0 + nrm(shape, 0.02)

    dt = jnp.exp(jax.random.uniform(next(ks), (N_A_LAYERS, A_HEADS), F32, math.log(1e-3), math.log(0.1)))
    a_base = jax.random.uniform(next(ks), (N_C_LAYERS, C_WIDTH), F32, 0.81, 0.998) ** (1.0 / C_GATE)
    return {
        'x_prompt': nrm((BATCH, SEQ, D_MODEL), 1.0),
        'x_sample': nrm((DEC_BATCH, DEC_SEQ, D_MODEL), 1.0),
        'state_delta': nrm((N_A_LAYERS, DEC_BATCH, A_HEADS, A_DK, A_DV), 0.2),
        'state_delta_conv': nrm((N_A_LAYERS, DEC_BATCH, A_CONV - 1, A_CONV_CH), 1.0),
        'state_pool': nrm((N_A_LAYERS, DEC_BATCH, B_HIST, B_WIDTH), 1.0),
        'state_lru': nrm((N_C_LAYERS, DEC_BATCH, C_WIDTH), 0.3),
        'state_lru_conv': nrm((N_C_LAYERS, DEC_BATCH, C_CONV - 1, C_WIDTH), 1.0),
        'ab_w_in': nrm((N_A_LAYERS, D_MODEL, EVEN_IN), D_MODEL ** -0.5),
        'a_conv_w': nrm((N_A_LAYERS, A_CONV, A_CONV_CH), A_CONV ** -0.5),
        'a_log_decay': jnp.log(jax.random.uniform(next(ks), (N_A_LAYERS, A_HEADS), F32, 1.0, 16.0)),
        'a_dt_bias': dt + jnp.log(-jnp.expm1(-dt)),
        'a_norm_w': gain((N_A_LAYERS, A_DV)),
        'b_w_group': nrm((N_A_LAYERS, B_GROUPS, B_GW, B_GW), B_GW ** -0.5),
        'b_scale': gain((N_A_LAYERS, B_WIDTH)),
        'ab_w_out': nrm((N_A_LAYERS, EVEN_MIX, D_MODEL), EVEN_MIX ** -0.5 * BETA_INIT),
        'c_w_in': nrm((N_C_LAYERS, D_MODEL, ODD_IN), D_MODEL ** -0.5),
        'c_conv_w': nrm((N_C_LAYERS, C_CONV, C_WIDTH), C_CONV ** -0.5),
        'c_conv_b': nrm((N_C_LAYERS, C_WIDTH), 0.02),
        'c_w_r': nrm((N_C_LAYERS, C_HEADS, C_HW, C_HW), C_HW ** -0.5),
        'c_b_r': nrm((N_C_LAYERS, C_WIDTH), 0.02),
        'c_w_i': nrm((N_C_LAYERS, C_HEADS, C_HW, C_HW), C_HW ** -0.5),
        'c_b_i': nrm((N_C_LAYERS, C_WIDTH), 0.02),
        'c_lambda': jnp.log(a_base) - jnp.log1p(-a_base),
        'c_w_out': nrm((N_C_LAYERS, C_WIDTH, D_MODEL), C_WIDTH ** -0.5 * BETA_INIT),
        'ln_mix_g': gain((DEPTH, D_MODEL)),
        'ln_mix_b': nrm((DEPTH, D_MODEL), 0.02),
        'ln_ffn_g': gain((DEPTH, D_MODEL)),
        'ln_ffn_b': nrm((DEPTH, D_MODEL), 0.02),
        'router_w': nrm((D_MODEL, N_EXPERTS), D_MODEL ** -0.5),
        'router_bias': nrm((N_EXPERTS,), 0.01),
        'moe_w_gate': nrm((DEPTH, N_EXPERTS, D_MODEL, D_EXPERT), D_MODEL ** -0.5),
        'moe_w_up': nrm((DEPTH, N_EXPERTS, D_MODEL, D_EXPERT), D_MODEL ** -0.5),
        'moe_w_down': nrm((DEPTH, N_EXPERTS, D_EXPERT, D_MODEL), D_EXPERT ** -0.5 * BETA_INIT),
    }

def reference(x_prompt, x_sample, state_delta, state_delta_conv, state_pool, state_lru, state_lru_conv,
              ab_w_in, a_conv_w, a_log_decay, a_dt_bias, a_norm_w, b_w_group, b_scale, ab_w_out,
              c_w_in, c_conv_w, c_conv_b, c_w_r, c_b_r, c_w_i, c_b_i, c_lambda, c_w_out,
              ln_mix_g, ln_mix_b, ln_ffn_g, ln_ffn_b, router_w, router_bias, moe_w_gate, moe_w_up, moe_w_down):
    weights = (ab_w_in, a_conv_w, a_log_decay, a_dt_bias, a_norm_w, b_w_group, b_scale, ab_w_out,
               c_w_in, c_conv_w, c_conv_b, c_w_r, c_b_r, c_w_i, c_b_i, c_lambda, c_w_out,
               ln_mix_g, ln_mix_b, ln_ffn_g, ln_ffn_b, router_w, router_bias, moe_w_gate, moe_w_up, moe_w_down)
    bp = x_prompt.shape[0]
    zero_states = (
        jnp.zeros((N_A_LAYERS, bp) + state_delta.shape[2:], state_delta.dtype),
        jnp.zeros((N_A_LAYERS, bp) + state_delta_conv.shape[2:], state_delta_conv.dtype),
        jnp.zeros((N_A_LAYERS, bp) + state_pool.shape[2:], state_pool.dtype),
        jnp.zeros((N_C_LAYERS, bp) + state_lru.shape[2:], state_lru.dtype),
        jnp.zeros((N_C_LAYERS, bp) + state_lru_conv.shape[2:], state_lru_conv.dtype),
    )
    y_prompt, p_delta, p_dconv, p_pool, p_lru, p_lconv = trunk(x_prompt, zero_states, 0, weights)
    sample_states = (state_delta, state_delta_conv, state_pool, state_lru, state_lru_conv)
    y_sample, s_delta, s_dconv, s_pool, s_lru, s_lconv = trunk(x_sample, sample_states, B_HIST, weights)
    return (y_prompt, y_sample, p_delta, p_dconv, p_pool, p_lru, p_lconv, s_delta, s_dconv, s_pool, s_lru, s_lconv)


_drawn_inputs = setup_inputs


def setup_inputs(seed=0):
    import zlib

    import numpy as np

    out = dict(_drawn_inputs(seed))
    spreads = {}
    factors = {'c_b_r': 8.0, 'c_b_i': 6.766}
    for name, (base, spread) in spreads.items():
        noise = np.random.default_rng([zlib.crc32(name.encode()), seed]).standard_normal(out[name].shape)
        drawn = base * np.exp(spread * noise) if base else spread * noise
        out[name] = __import__('jax').numpy.asarray(drawn.astype(out[name].dtype))
    for name, factor in factors.items():
        out[name] = (out[name] * factor).astype(out[name].dtype)
    return out
```

```python
import concourse.bass as bass
from concourse import mybir

F32 = mybir.dt.float32
I32 = mybir.dt.int32
ALU = mybir.AluOpType
ACT = mybir.ActivationFunctionType
AX = mybir.AxisListType

P = 128
D = 1024
KD = D // P
TP, NS, LS = 512, 8, 8
TS = NS * LS
T = TP + TS
NT = 5
ROWS = [P] * (TP // P) + [TS]
NCHUNK = 12
NH = 4
HIST = 15
CONV = 4
NPROJ = 20
FF = 512
NE = 16
BLOCKS = NT
SLOTS = BLOCKS * P * NE
WINDOWS = (2, 4, 8, 16)
ALPHA = 4.0 ** 0.25
LN_EPS, RMS_EPS, L2_EPS = 1e-5, 1e-6, 1e-6
BIG = 1.0e30
EXT_P, EXT_S = CONV - 1 + TP, CONV - 1 + LS
EXT = EXT_P + NS * EXT_S
UEP, UES = HIST + TP, HIST + LS
UE = UEP + NS * UES
WORK = 35340


class Steps:

    def __init__(self, sem, names):
        self.sem, self.names, self.made = sem, names, 0

    def at(self, n, name):
        return n * len(self.names) + self.names.index(name) + 1

    def end(self, instruction, n, name):
        self.made += 1
        assert self.made == self.at(n, name), (self.made, n, name)
        return instruction.then_inc(self.sem, 1)

    def wait(self, engine, n, name):
        engine.wait_ge(self.sem, self.at(n, name))


def hybrid_trunk(nc, x_prompt, x_sample, state_delta, state_delta_conv, state_pool, state_lru, state_lru_conv,
                 ab_w_in, a_conv_w, a_log_decay, a_dt_bias, a_norm_w, b_w_group, b_scale, ab_w_out,
                 c_w_in, c_conv_w, c_conv_b, c_w_r, c_b_r, c_w_i, c_b_i, c_lambda, c_w_out,
                 ln_mix_g, ln_mix_b, ln_ffn_g, ln_ffn_b, router_w, router_bias,
                 moe_w_gate, moe_w_up, moe_w_down,
                 y_prompt, y_sample, p_delta, p_dconv, p_pool, p_lru, p_lconv,
                 s_delta, s_dconv, s_pool, s_lru, s_lconv):
    from contextlib import ExitStack
    ctx = ExitStack()
    with ctx:
        def sb(name, shape, dt=F32):
            return ctx.enter_context(nc.sbuf_tensor(name, shape, dt))

        def sem(name):
            return ctx.enter_context(nc.semaphore(name))

        def steps(name, names):
            return Steps(sem(name), names)

        x_rows = [nc.dram_tensor(f"x_rows{l}", [T, D], F32).ap() for l in range(2)]
        slot_list = [nc.dram_tensor(f"slot_list{l}", [SLOTS, 1], I32).ap() for l in range(2)]
        y_rows = [nc.dram_tensor(f"y_rows{l}", [SLOTS, D], F32).ap() for l in range(2)]

        X = sb("X", [P, NT, D])
        XT = sb("XT", [P, KD, T])
        LNP = sb("LNP", [P, 2, 2, D])
        work = sb("work", [P, WORK])
        ident = sb("ident", [P, P])
        ones = sb("ones", [P, P])
        m_strict_bd = sb("m_strict_bd", [P, P])
        m_strict_off = sb("m_strict_off", [P, P])
        m_strict_s = sb("m_strict_s", [TS, TS])
        m_incl = sb("m_incl", [P, P])
        m_incl_s = sb("m_incl_s", [TS, TS])
        m_before = sb("m_before", [P, P])
        sel_gc = sb("sel_gc", [68, NH, P])
        sel_row = sb("sel_row", [NH, NH, P])
        own_sample = sb("own_sample", [TS, NS])
        ms_col = sb("ms_col", [P, NH, NH])
        inv_cnt = sb("inv_cnt", [P, 16])
        iota16 = sb("iota16", [P, NE])
        tok_id = sb("tok_id", [P, NT], I32)
        zero_i = sb("zero_i", [P, SLOTS // P], I32)
        rw = sb("rw", [P, KD, NE])
        rbias = sb("rbias", [P, NE])
        par = sb("par", [P, 88])
        COL = sb("COL", [P, NT, 68])
        ecol = sb("ecol", [P, NT, NH])
        kdc = sb("kdc", [P, NT, NH])
        kbgc = sb("kbgc", [P, NT, NH])
        egl = sb("egl", [P, NH, 12])
        lnw = sb("lnw", [P, NT, 16])
        scores = sb("scores", [P, NT, NE])
        wsel = sb("wsel", [P, 4, NT])
        pos_i = sb("pos_i", [P, 2, NT], I32)
        idx_all = sb("idx_all", [P, BLOCKS, NE], I32)
        gpar = sb("gpar", [36, 2])
        iota_i = sb("iota_i", [P, 16], I32)
        idx_cur = sb("idx_cur", [P, 2], I32)
        over_i = sb("over_i", [1, 1], I32)

        bank = [ctx.enter_context(nc.psum_tensor(f"bank{i}", [P, 512], F32)) for i in range(8)]

        def heads_of(b, n=P, m=P):
            return bank[b][:, :].rearrange("p (h c) -> p h c", h=4)[0:n, :, 0:m]

        def view(off, shape):
            n = 1
            for s in shape:
                n *= s
            v = work[:, off:off + n]
            if len(shape) == 2:
                v = v.rearrange("p (a b) -> p a b", a=shape[0])
            elif len(shape) == 3:
                v = v.rearrange("p (a b c) -> p a b c", a=shape[0], b=shape[1])
            return v

        W0 = [view(2048 * s, (KD, 256)) for s in range(4)]
        QKV = view(8192, (NCHUNK, T))
        Z = view(15104, (NH, T))
        U = view(17408, (NH, UE))
        gB = view(20252, (NH, T))
        INV = view(22556, (8, T))
        SS = view(22556, (NS * NH, P))
        chist_rows = work[:, 22556:22556 + 1536]
        phist_rows = work[:, 24092:24092 + 512]
        par_rows = work[:, 24604:24604 + P]
        wab_in = view(24732, (KD, 8))
        wab = view(24796, (KD, 68))
        EXTB = [work[:, 27164 + EXT * s:27164 + EXT * (s + 1)] for s in range(3)]
        CV = view(28973, (2, T))
        SQ = view(30125, (2, T))
        PT_ = view(31277, (2, UE))
        POOLED = view(32699, (NH, T))
        chistT = view(31277, (NCHUNK, 24))
        RT, RA, RB, keep = (work[:, 15104 + T * i:15104 + T * i + T] for i in range(4))
        slot = [view(512 * s, (NH, P)) for s in range(16)] + \
               [view(27164 + 512 * s, (NH, P)) for s in range(8)]
        (kbg, kd, vb, dif, dmx, dmn, Dbd, Doff, DTm, aT, Pa, Pb, PTa, PTb, TT, Noff,
         TB, Yo, nwT, un, egB, SP_, UB0, UB1) = slot
        UB = view(27164 + 512 * 6, (NS, P))
        WO0 = view(0, (KD, D))
        WG = view(31277, (NH, P))
        tails = view(35003, (27, NCHUNK))
        utail = view(30125, (NH, NS * HIST))
        rows_out = LNP[:, 1, :, :].rearrange("p n d -> p (n d)")
        W1 = W0
        WRI = view(8192, (2, 8, 256))
        YB = view(12288, (KD, T))
        XC = view(16896, (KD, T))
        R_ = view(21504, (KD, T))
        GI = view(26112, (KD, T))
        EXT1 = [work[:, 30720 + EXT * s:30720 + EXT * (s + 1)] for s in range(3)]
        TMP = view(32529, (2, T))
        lhistT = view(33681, (KD, 24))
        lstateT = view(33873, (KD, NS))
        lhist_rows = work[:, 26112:26112 + D]
        lstate_rows = work[:, 27136:27136 + D]
        par_rows1 = work[:, 28160:28160 + P]
        tails1 = view(34073, (27, KD))
        lru_last = work[:, 33937:33937 + 72]
        lru_init = work[:, 34009:34009 + 64].rearrange("p (c s) -> p c s", c=KD)
        WGT = [view(8192 + 4096 * s, (KD, FF)) for s in range(2)]
        WUP = [view(16384 + 4096 * s, (KD, FF)) for s in range(2)]
        WDN = [view(4096 * s, (FF // P, D)) for s in range(2)]
        XG = [work[:, 24576 + D * s:24576 + D * (s + 1)] for s in range(2)]
        XGT = view(26624, (KD, P))
        SG = [work[:, 27648 + FF * s:27648 + FF * (s + 1)] for s in range(2)]
        HB = [work[:, 28672 + FF * s:28672 + FF * (s + 1)] for s in range(2)]
        HT = view(29696, (FF // P, P))
        YO = [work[:, 30208 + D * s:30208 + D * (s + 1)] for s in range(2)]
        rt = view(30208, (12, NT * NE))
        oh = view(31168, (2, NT * NE)).rearrange("p k (t e) -> p k t e", t=NT)
        Y1 = [work[:, 16384 + D * s:16384 + D * (s + 1)] for s in range(2)]
        Y2 = [work[:, 18432 + D * s:18432 + D * (s + 1)] for s in range(2)]
        own = {e: sem(f"{e}_own") for e in ("dve", "pool")}

        class Own:

            def __init__(self, engine, s):
                self.engine, self.s, self.n = engine, s, 0

            def __call__(self, instruction):
                self.n += 1
                return instruction.then_inc(self.s, 1)

            def settle(self):
                self.engine.wait_ge(self.s, self.n)

        x_in, hist_in, gates_in, wab_sem = sem("x_in"), sem("hist_in"), sem("gates_in"), sem("wab_in_s")
        w_in = [sem(f"w_in{s}") for s in range(4)]
        w1_in = [sem(f"w1_in{s}") for s in range(4)]
        lnp_in = [sem(f"lnp_in{s}") for s in range(2)]
        router_in, lists_zeroed = sem("router_in"), sem("lists_zeroed")
        ss_in, wg_in, wo_in, wri_in, hist1_in = sem("ss_in"), sem("wg_in"), sem("wo_in"), sem("wri_in"), sem("hist1_in")
        state_out, y_out = sem("state_out"), sem("y_out")
        xrows_out, tok_scattered, idx_in = sem("xrows_out"), sem("tok_scattered"), sem("idx_in")
        consts_ready = sem("consts_ready")
        xt_ps, xt_lo, xt_hi = sem("xt_ps"), sem("xt_lo"), sem("xt_hi")
        hist_ps, hist_out, ab_ps, rows_ready = sem("hist_ps"), sem("hist_out"), sem("ab_ps"), sem("rows_ready")
        wab_ready, gate_act, gate_dve = sem("wab_ready"), sem("gate_act"), sem("gate_dve")
        proj_ps, proj_out, conv_done, silu_done = sem("proj_ps"), sem("proj_out"), sem("conv_done"), sem("silu_done")
        sq_done, ssq_ps, inv_done, tail_done = sem("sq_done"), sem("ssq_ps"), sem("inv_done"), sem("tail_done")
        gcb_ps, gcb_out, col_ps, col_out, egl_done = sem("gcb_ps"), sem("gcb_out"), sem("col_ps"), sem("col_out"), sem("egl_done")
        roots_done, q_scaled, k_scaled = sem("roots_done"), sem("q_scaled"), sem("k_scaled")
        psum_done, pooled_done = sem("pool_sum_done"), sem("pooled_done")
        gained = sem("gained")
        utail_done = sem("utail_done")
        strow_ps, strow_out = sem("strow_ps"), sem("strow_out")
        d_pe = steps("delta_pe", ["ktr", "vtr", "gram", "qk", "pt"] +
                     [f"{a}{r}" for r in range(1, 6) for a in ("p", "pt", "x")][:-2] + ["x5"] +
                     ["tb", "y", "x6", "nw", "un", "o", "sn"])
        d_dve = steps("delta_dve", ["dif", "kbg", "kd", "p0", "off", "a", "tt0"] +
                      [f"{a}{r}" for r in range(1, 6) for a in ("p", "tt")] + ["y", "tt6", "un", "s"])
        d_act = steps("delta_act", ["vb", "dbd", "dt", "eg", "pt0", "pt1", "pt2", "pt3", "pt4", "tb", "nw", "o"])
        d_pool = steps("delta_pool", ["max", "min", "bd", "off", "incl", "qd"])
        e_pe = steps("sample_pe", ["ktr", "vtr", "gram", "qk", "pt", "p1", "pt1", "x1", "p2", "x2", "nw", "ut", "un",
                                   "o"] + [f"sn{h}" for h in range(NH)])
        e_dve = steps("sample_dve", ["dif", "kbg", "kd", "p0", "a", "tt0", "p1", "tt1", "p2", "tt2", "un", "o"] +
                      [f"s{h}" for h in range(NH)])
        e_act = steps("sample_act", ["vb", "dbd", "dt", "eg", "pt0", "pt1", "nw", "ut"])
        e_pool = steps("sample_pool", ["max", "min", "bd", "incl", "qd"] + [f"ub{h}" for h in range(NH)])
        s_zeroed = sem("s_zeroed")
        rms_sq, rms_ps, rms_eps, rms_root, rms_inv = sem("rms_sq"), sem("rms_ps"), sem("rms_eps"), sem("rms_root"), sem("rms_inv")
        rmsb_ps, rmsb_out, mix_a, group_ps, mix_b = sem("rmsb_ps"), sem("rmsb_out"), sem("mix_a"), sem("group_ps"), sem("mix_b")
        out_ps = sem("out_ps")
        norm_sum, norm_stats, norm_coef = sem("norm_sum"), sem("norm_stats"), sem("norm_coef")
        norm_root, norm_scaled, norm_done = sem("norm_root"), sem("norm_scaled"), sem("norm_done")
        logits_ps, scores_done, onehot_ready, rank_ps, pos_ready = \
            sem("logits_ps"), sem("scores_done"), sem("onehot_ready"), sem("rank_ps"), sem("pos_ready")
        gate_in, up_in, down_in, xg_in, y_stored, ysel_in = (
            [sem(f"{n}{u}") for u in range(2)]
            for n in ("gate_in", "up_in", "down_in", "xg_in", "y_stored", "ysel_in"))
        xg_ps, xgt_ready, gate_ps, up_ps, sg_done, h_ready = \
            sem("xg_ps"), sem("xgt_ready"), sem("gate_ps"), sem("up_ps"), sem("sg_done"), sem("h_ready")
        h_ps, ht_ready, y1_ps, y0_ps, y1_out, y0_out = \
            sem("h_ps"), sem("ht_ready"), sem("y1_ps"), sem("y0_ps"), sem("y1_out"), sem("y0_out")
        ysel_scaled = sem("ysel_scaled")
        OV = {"x_ps": ("pe", 4, 1), "gu_ps": ("pe", 4, 2), "h_ps": ("pe", 4, 3), "y_ps": ("pe", 4, 4),
              "sg": ("act", 3, 1), "ht": ("act", 3, 2), "y_a": ("act", 3, 3),
              "xgt": ("dve", 3, 1), "h": ("dve", 3, 2), "y_d": ("dve", 3, 3),
              "w": ("w", 48, 48), "xg": ("xg", 16, 16), "stored": ("stored", 16, 16)}
        ov = [{n: sem(f"ov{l}_{n}") for n in ("pe", "act", "dve", "w", "xg", "stored")} for l in range(2)]

        def ov_wait(engine, l, n, part):
            who, per_step, at = OV[part]
            start = 4 if who == "pe" else 0
            engine.wait_ge(ov[l][who], n * per_step + (at - per_step + start))

        def ov_buffers_free(engine, l, n):
            engine.wait_ge(ov[l]["pe"], n * 4)

        lru_gate_ps, lru_gates_done = sem("lru_gate_ps"), sem("lru_gates_done")
        lru_hist_ps, lru_hist_out, lru_par = sem("lru_hist_ps"), sem("lru_hist_out"), sem("lru_par")
        proj1_ps, proj1_out, conv1_done, tail1_done = sem("proj1_ps"), sem("proj1_out"), sem("conv1_done"), sem("tail1_done")
        lru_a, lru_a2, lru_t, lru_w, lru_root, lru_x, lru_h, ext1_zeroed = (
            sem(f"lru_{n}") for n in ("a", "a2", "t", "w", "root", "x", "h", "ext_zeroed"))
        st1_ps, st1_out = sem("st1_ps"), sem("st1_out")

        def tile_cols(t):
            return slice(P * t, P * t + ROWS[t])

        def bc(ap, shape):
            return ap.broadcast_to(shape)

        def xrow_dram(t, prompt, sample):
            return prompt[0, P * t:P * t + P, :] if t < TP // P else sample.rearrange("s l d -> (s l) d")

        ext_prompt = slice(CONV - 1, EXT_P)

        def ext_samples(buf):
            return buf[:, EXT_P:EXT].rearrange("p (s l) -> p s l", s=NS)

        def samples(ap):
            return ap[:, TP:T].rearrange("p (s l) -> p s l", s=NS)

        def at_least(engine, s, value):
            if not isinstance(value, int) or value > 0:
                engine.wait_ge(s, value)

        def arrivals(l, pairs):
            return pairs * 16 + P * l if not isinstance(pairs, int) else 16 * pairs + P * l

        block = ctx.enter_context(nc.Block())
        TILE_BANK = lambda t: 4 + 2 * (t % 2)

        @block.sync
        def _(sp):
            def lnp(slot_, l, gains, biases):
                for n, src in enumerate((gains, biases)):
                    sp.dma_start(LNP[:, slot_, n, :], src[l, :].partition_broadcast(P)).then_inc(lnp_in[slot_], 16)

            def gate_up(l, e, u):
                sp.dma_start(WGT[u], moe_w_gate[l, e].rearrange("(k p) f -> p k f", p=P)).then_inc(gate_in[u], 16)
                sp.dma_start(WUP[u], moe_w_up[l, e].rearrange("(k p) f -> p k f", p=P)).then_inc(up_in[u], 16)

            def down(l, e, u):
                sp.dma_start(WDN[u], moe_w_down[l, e].rearrange("(k p) d -> p k d", p=P)).then_inc(down_in[u], 16)

            def store_rows(l, q, t):
                sp.wait_ge(norm_done, q * NT + t + 1)
                sp.dma_start(x_rows[l][P * t:P * t + ROWS[t], :], X[0:ROWS[t], t, :]).then_inc(xrows_out, 16)

            def experts(l):
                sp.wait_ge(mix_a, NH + KD * l)
                sp.wait_ge(mix_b, NH)
                for u in range(2):
                    gate_up(l, u, u)
                for t in range(NT):
                    store_rows(l, 2 * l, t)
                for u in range(2):
                    down(l, u, u)
                sp.wait_ge(tok_scattered, 160 * (l + 1))
                sp.dma_start(idx_all[:, :, :], slot_list[l].rearrange("(b s e) o -> s b (e o)", b=BLOCKS, s=P))\
                  .then_inc(idx_in, 16)
                base = NE * l
                with sp.Fori(0, NE // 2 - 1) as i:
                    for u in range(2):
                        sp.wait_ge(gate_ps, i * 2 + (base + u + 1))
                        sp.dma_start(WGT[u], moe_w_gate[l, bass.ds(i * 2 + (2 + u), 1)]
                                     .rearrange("o (k p) f -> p (o k) f", p=P)).then_inc(gate_in[u], 16)
                        sp.wait_ge(up_ps, i * 2 + (base + u + 1))
                        sp.dma_start(WUP[u], moe_w_up[l, bass.ds(i * 2 + (2 + u), 1)]
                                     .rearrange("o (k p) f -> p (o k) f", p=P)).then_inc(up_in[u], 16)
                        sp.wait_ge(y0_ps, i * 2 + (base + u + 1))
                        sp.dma_start(WDN[u], moe_w_down[l, bass.ds(i * 2 + (2 + u), 1)]
                                     .rearrange("o (k p) d -> p (o k) d", p=P)).then_inc(down_in[u], 16)
                sp.wait_ge(y0_ps, base + NE)
                overflow(l)

            def overflow(l):
                s = ov[l]
                sp.wait_ge(pos_ready, l + 1)
                most = sp.value_load(over_i[0:1, 0:1], min_val=0, max_val=T)
                with sp.If(most > P):
                    with sp.Fori(1, BLOCKS) as b:
                        with sp.Fori(0, NE) as e:
                            ov_buffers_free(sp, l, b * NE + e - (NE - 1))
                            for buf, w in ((WGT, moe_w_gate), (WUP, moe_w_up), (WDN, moe_w_down)):
                                sp.dma_start(buf[0], w[l, bass.ds(e, 1)].rearrange("o (k p) f -> p (o k) f", p=P))\
                                  .then_inc(s["w"], 16)
                    ov_buffers_free(sp, l, (BLOCKS - 1) * NE + 1)

            def mixer1():
                sp.dma_start(lhist_rows[0:24, :], state_lru_conv[0].rearrange("s j c -> (s j) c")).then_inc(hist1_in, 16)
                sp.dma_start(lstate_rows[0:NS, :], state_lru[0]).then_inc(hist1_in, 16)
                sp.dma_start(par_rows1[0:32, :], c_conv_w[0].rearrange("j (c p) -> (j c) p", p=P)).then_inc(hist1_in, 16)
                for n, src in enumerate((c_conv_b, c_b_r, c_b_i, c_lambda)):
                    sp.dma_start(par_rows1[32 + 8 * n:40 + 8 * n, :], src[0].rearrange("(c p) -> c p", p=P))\
                      .then_inc(hist1_in, 16)
                for n, src in enumerate((c_w_r, c_w_i)):
                    sp.dma_start(WRI[:, n, :, :], src[0].rearrange("h (k p) j -> p (h k) j", p=P)).then_inc(wri_in, 16)
                win = c_w_in[0].rearrange("(k p) c -> p k c", p=P)
                for n in range(8):
                    if n >= 4:
                        sp.wait_ge(proj1_ps, 2 * (n - 4) + 2)
                    sp.dma_start(W0[n % 4], win[:, :, 256 * n:256 * n + 256]).then_inc(w1_in[n % 4], 16)
                sp.wait_ge(proj1_ps, 16)
                sp.dma_start(WO0, c_w_out[0].rearrange("(k p) d -> p k d", p=P)).then_inc(wo_in, 16)
                sp.wait_ge(st1_out, 1)
                sd = s_lconv[0].rearrange("s j (c p) -> (s j c) p", p=P)
                sp.dma_start(p_lconv[0, 0].rearrange("j (c p) -> (j c) p", p=P), rows_out[0:24, 0:128])\
                  .then_inc(state_out, 16)
                sp.dma_start(sd[0:84, :], rows_out[24:108, 0:128]).then_inc(state_out, 16)
                sp.dma_start(sd[84:192, :], rows_out[0:108, 128:256]).then_inc(state_out, 16)
                sp.wait_ge(st1_out, 2)
                sp.dma_start(p_lru[0, 0].rearrange("(c p) -> c p", p=P), rows_out[0:8, 256:384]).then_inc(state_out, 16)
                sp.dma_start(s_lru[0].rearrange("s (c p) -> (s c) p", p=P), rows_out[8:72, 256:384]).then_inc(state_out, 16)
            sp.dma_start(X[:, 0:4, :], x_prompt[0].rearrange("(t p) d -> p t d", p=P)).then_inc(x_in, 16)
            sp.dma_start(X[0:TS, 4, :], x_sample.rearrange("s l d -> (s l) d")).then_inc(x_in, 16)
            lnp(0, 0, ln_mix_g, ln_mix_b)
            sp.dma_start(rw[:, :, :], router_w.rearrange("(k p) e -> p k e", p=P)).then_inc(router_in, 16)
            sp.dma_start(rbias[:, :], router_bias.partition_broadcast(P)).then_inc(router_in, 16)
            win = ab_w_in[0].rearrange("(k p) c -> p k c", p=P)
            sp.dma_start(wab_in, win[:, :, 2048:2056]).then_inc(wab_sem, 16)
            sp.dma_start(chist_rows[0:24, :], state_delta_conv[0].rearrange("s j c -> (s j) c")).then_inc(hist_in, 16)
            sp.dma_start(phist_rows[0:120, :], state_pool[0].rearrange("s j c -> (s j) c")).then_inc(hist_in, 16)
            sp.dma_start(par_rows[0:48, :], a_conv_w[0].rearrange("j (c p) -> (j c) p", p=P)).then_inc(hist_in, 16)
            sp.dma_start(par_rows[48:52, :], b_scale[0].rearrange("(c p) -> c p", p=P)).then_inc(hist_in, 16)
            sp.dma_start(par_rows[52:53, :], a_norm_w).then_inc(hist_in, 16)
            cols = [256 * i for i in range(6)] + [2056, 2312] + [1536, 1792]
            for n, c in enumerate(cols):
                if n >= 4:
                    sp.wait_ge(proj_ps, 2 * (n - 4) + 2)
                sp.dma_start(W0[n % 4], win[:, :, c:c + 256]).then_inc(w_in[n % 4], 16)
                if n == 3:
                    sp.wait_ge(consts_ready, 1)
                    for l in range(2):
                        sp.dma_start(slot_list[l].rearrange("(p n) o -> p (n o)", p=P), zero_i[:, :])\
                          .then_inc(lists_zeroed, 16)
            sp.wait_ge(q_scaled, 4)
            sp.wait_ge(k_scaled, 4)
            sp.dma_start(SS, state_delta[0].rearrange("s h k v -> k (s h) v")).then_inc(ss_in, 16)
            sp.wait_ge(strow_out, 1)
            sp.dma_start(p_pool[0, 0].rearrange("j c -> j c"), rows_out[0:HIST, 0:512]).then_inc(state_out, 16)
            sp.dma_start(s_pool[0].rearrange("s j c -> (s j) c"), rows_out[0:120, 512:1024]).then_inc(state_out, 16)
            sd = s_dconv[0].rearrange("s j (c p) -> (s j c) p", p=P)
            sp.dma_start(p_dconv[0, 0].rearrange("j (c p) -> (j c) p", p=P), rows_out[0:36, 1024:1152])\
              .then_inc(state_out, 16)
            for g, (lo, hi) in enumerate(((36, 108), (0, 108), (0, 108))):
                at = 108 * g + lo - 36
                sp.dma_start(sd[at:at + hi - lo, :], rows_out[lo:hi, 1024 + P * g:1152 + P * g]).then_inc(state_out, 16)
            sp.wait_ge(state_out, 16 * 6)
            lnp(1, 0, ln_ffn_g, ln_ffn_b)
            sp.wait_ge(pooled_done, 4)
            sp.dma_start(WG, b_w_group[0].rearrange("g c d -> c g d")).then_inc(wg_in, 16)
            d_dve.wait(sp, 3, "s")
            sp.dma_start(p_delta[0, 0].rearrange("h k v -> k h v"), SP_).then_inc(state_out, 16)
            e_dve.wait(sp, 0, "s3")
            sp.dma_start(s_delta[0].rearrange("s h k v -> k (s h) v"), SS).then_inc(state_out, 16)
            e_pe.wait(sp, 0, "sn3")
            sp.dma_start(WO0, ab_w_out[0].rearrange("(k p) d -> p k d", p=P)).then_inc(wo_in, 16)
            sp.wait_ge(state_out, 16 * 8)
            experts(0)
            lnp(0, 1, ln_mix_g, ln_mix_b)
            mixer1()
            sp.wait_ge(state_out, 16 * 13)
            lnp(1, 1, ln_ffn_g, ln_ffn_b)
            experts(1)
            for t in range(NT):
                sp.wait_ge(norm_done, 3 * NT + t + 1)
                dst = xrow_dram(t, y_prompt, y_sample)
                sp.dma_start(dst, X[0:ROWS[t], t, :]).then_inc(y_out, 16)
            sp.wait_ge(y_out, 16 * NT)
            sp.wait_ge(state_out, 16 * 13)

        @block.tensor
        def _(pe):
            mm, tr = nc.tensor.matmul, nc.tensor.transpose

            def to_channels(n):
                for t in range(NT):
                    r, b = ROWS[t], TILE_BANK(t)
                    if n:
                        pe.wait_ge(norm_done, (n - 1) * NT + t + 1)
                    elif t == 0:
                        pe.wait_ge(x_in, 32)
                        pe.wait_ge(consts_ready, 1)
                    if n == 3 and t == 0:
                        pe.wait_ge(st1_out, 2)
                    if n * NT + t >= 2:
                        pe.wait_ge(xt_lo, n * NT + t - 1)
                        pe.wait_ge(xt_hi, n * NT + t - 1)
                    for k in range(KD):
                        last = tr(heads_of(b + k // 4, P, r)[:, k % 4, :], X[0:r, t, P * k:P * k + P], ident[0:r, 0:r])
                    last.then_inc(xt_ps, 1)

            def project(c, arrived, done, out_done):
                pe.wait_ge(arrived[(c // 2) % 4], 16 * (c // 8 + 1))
                if c >= 3:
                    pe.wait_ge(out_done, c - 2)
                w = W0[(c // 2) % 4][:, :, P * (c % 2):P * (c % 2) + P]
                for k in range(KD):
                    mm(bank[c % 3][:, :], w[:, k, :], XT[:, k, 0:TP], start=(k == 0), stop=(k == KD - 1))
                    last = mm(bank[(3, 6, 7)[c % 3]][:, 0:TS], w[:, k, :], XT[:, k, TP:T],
                              start=(k == 0), stop=(k == KD - 1))
                last.then_inc(done, 1)

            def delta_prompt(b):
                cols = tile_cols(b)
                kT, qT, vT = (lambda h, o=o: QKV[:, o + h, cols] for o in (4, 0, 8))
                if b:
                    d_dve.wait(pe, b - 1, "un")
                for h in range(NH):
                    last = tr(heads_of(0)[:, h, :], kT(h), ident[:, :])
                d_pe.end(last, b, "ktr")
                if b:
                    d_act.wait(pe, b - 1, "o")
                for h in range(NH):
                    last = tr(heads_of(1)[:, h, :], vT(h), ident[:, :])
                d_pe.end(last, b, "vtr")
                if b:
                    d_dve.wait(pe, b - 1, "s")
                for h in range(NH):
                    last = mm(heads_of(2)[:, h, :], kT(h), kT(h), start=True, stop=True)
                d_pe.end(last, b, "gram")
                for h in range(NH):
                    last = mm(heads_of(3)[:, h, :], kT(h), qT(h), start=True, stop=True)
                d_pe.end(last, b, "qk")
                d_dve.wait(pe, b, "p0")
                for h in range(NH):
                    last = tr(heads_of(4)[:, h, :], Pa[:, h, :], ident[:, :])
                d_pe.end(last, b, "pt")
                pw, pwt = (Pa, Pb), (PTa, PTb)
                for r in range(1, 6):
                    a, o = (r - 1) % 2, r % 2
                    d_act.wait(pe, b, f"pt{r - 1}")
                    d_dve.wait(pe, b, f"p{r - 1}")
                    for h in range(NH):
                        last = mm(heads_of(5)[:, h, :], pwt[a][:, h, :], pw[a][:, h, :], start=True, stop=True)
                    d_pe.end(last, b, f"p{r}")
                    if r < 5:
                        for h in range(NH):
                            last = mm(heads_of(6)[:, h, :], pw[a][:, h, :], pwt[a][:, h, :], start=True, stop=True)
                        d_pe.end(last, b, f"pt{r}")
                    d_dve.wait(pe, b, f"p{r}")
                    for h in range(NH):
                        last = mm(heads_of(7)[:, h, :], pw[o][:, h, :], TT[:, h, :], start=True, stop=True)
                    d_pe.end(last, b, f"x{r}")
                d_dve.wait(pe, b, "tt5")
                for h in range(NH):
                    last = tr(heads_of(4)[:, h, :], TT[:, h, :], ident[:, :])
                d_pe.end(last, b, "tb")
                for h in range(NH):
                    last = mm(heads_of(5)[:, h, :], Noff[:, h, :], TT[:, h, :], start=True, stop=True)
                d_pe.end(last, b, "y")
                d_act.wait(pe, b, "tb")
                d_dve.wait(pe, b, "y")
                for h in range(NH):
                    last = mm(heads_of(7)[:, h, :], TB[:, h, :], Yo[:, h, :], start=True, stop=True)
                d_pe.end(last, b, "x6")
                d_dve.wait(pe, b, "tt6")
                for h in range(NH):
                    last = mm(heads_of(6)[:, h, :], kbg[:, h, :], TT[:, h, :], start=True, stop=True)
                d_pe.end(last, b, "nw")
                d_act.wait(pe, b, "nw")
                if b == 0:
                    pe.wait_ge(s_zeroed, 1)
                else:
                    d_dve.wait(pe, b - 1, "s")
                for h in range(NH):
                    mm(heads_of(0)[:, h, :], TT[:, h, :], vb[:, h, :], start=True, stop=False)
                    last = mm(heads_of(0)[:, h, :], nwT[:, h, :], SP_[:, h, :], start=False, stop=True)
                d_pe.end(last, b, "un")
                d_dve.wait(pe, b, "un")
                d_pool.wait(pe, b, "qd")
                for h in range(NH):
                    mm(heads_of(1)[:, h, :], SP_[:, h, :], qT(h), start=True, stop=False)
                    last = mm(heads_of(1)[:, h, :], un[:, h, :], aT[:, h, :], start=False, stop=True)
                d_pe.end(last, b, "o")
                for h in range(NH):
                    last = mm(heads_of(2)[:, h, :], kd[:, h, :], un[:, h, :], start=True, stop=True)
                d_pe.end(last, b, "sn")

            def delta_samples():
                b, n = NT - 1, TS
                cols = tile_cols(b)
                kT, qT, vT = (lambda h, o=o: QKV[:, o + h, cols] for o in (4, 0, 8))
                d_dve.wait(pe, 3, "un")
                for h in range(NH):
                    last = tr(heads_of(0, n)[:, h, :], kT(h), ident[:, :])
                e_pe.end(last, 0, "ktr")
                d_act.wait(pe, 3, "o")
                for h in range(NH):
                    last = tr(heads_of(1, n)[:, h, :], vT(h), ident[:, :])
                e_pe.end(last, 0, "vtr")
                d_dve.wait(pe, 3, "s")
                for h in range(NH):
                    last = mm(heads_of(2, n, n)[:, h, :], kT(h), kT(h), start=True, stop=True)
                e_pe.end(last, 0, "gram")
                for h in range(NH):
                    last = mm(heads_of(3, n, n)[:, h, :], kT(h), qT(h), start=True, stop=True)
                e_pe.end(last, 0, "qk")
                e_dve.wait(pe, 0, "p0")
                for h in range(NH):
                    last = tr(heads_of(4, n, n)[:, h, :], Pa[0:n, h, 0:n], ident[0:n, 0:n])
                e_pe.end(last, 0, "pt")
                pw, pwt = (Pa, Pb), (PTa, PTb)
                for r in (1, 2):
                    a, o = (r - 1) % 2, r % 2
                    e_act.wait(pe, 0, f"pt{r - 1}")
                    for h in range(NH):
                        last = mm(heads_of(5, n, n)[:, h, :], pwt[a][0:n, h, 0:n], pw[a][0:n, h, 0:n],
                                  start=True, stop=True)
                    e_pe.end(last, 0, f"p{r}")
                    if r < 2:
                        for h in range(NH):
                            last = mm(heads_of(6, n, n)[:, h, :], pw[a][0:n, h, 0:n], pwt[a][0:n, h, 0:n],
                                      start=True, stop=True)
                        e_pe.end(last, 0, f"pt{r}")
                    e_dve.wait(pe, 0, f"p{r}")
                    for h in range(NH):
                        last = mm(heads_of(7, n, n)[:, h, :], pw[o][0:n, h, 0:n], TT[0:n, h, 0:n],
                                  start=True, stop=True)
                    e_pe.end(last, 0, f"x{r}")
                e_dve.wait(pe, 0, "tt2")
                for h in range(NH):
                    last = mm(heads_of(6, P, n)[:, h, :], kbg[0:n, h, :], TT[0:n, h, 0:n], start=True, stop=True)
                e_pe.end(last, 0, "nw")
                e_act.wait(pe, 0, "nw")
                pe.wait_ge(ss_in, 16)
                for h in range(NH):
                    mm(heads_of(0, P, n)[:, h, :], vb[0:n, h, :], TT[0:n, h, 0:n], start=True, stop=False)
                    for s in range(NS):
                        c = slice(LS * s, LS * s + LS)
                        last = mm(heads_of(0, P, n)[:, h, c], SS[:, NH * s + h, :], nwT[:, h, c],
                                  start=False, stop=(s == NS - 1))
                e_pe.end(last, 0, "ut")
                e_act.wait(pe, 0, "ut")
                for h in range(NH):
                    last = tr(heads_of(4, n)[:, h, :], Yo[:, h, 0:n], ident[:, :])
                e_pe.end(last, 0, "un")
                e_dve.wait(pe, 0, "un")
                e_pool.wait(pe, 0, "qd")
                for h in range(NH):
                    for s in range(NS):
                        c = slice(LS * s, LS * s + LS)
                        mm(heads_of(1, P, n)[:, h, c], SS[:, NH * s + h, :], qT(h)[:, c], start=(s == 0), stop=False)
                    last = mm(heads_of(1, P, n)[:, h, :], un[0:n, h, :], aT[0:n, h, 0:n], start=False, stop=True)
                e_pe.end(last, 0, "o")
                for h in range(NH):
                    e_pool.wait(pe, 0, f"ub{h}")
                    if h:
                        e_dve.wait(pe, 0, f"s{h - 1}")
                    for half in range(2):
                        last = mm(heads_of(2 + half)[:, :, :], kd[0:n, h, :], UB[0:n, 4 * half:4 * half + 4, :],
                                  start=True, stop=True)
                    e_pe.end(last, 0, f"sn{h}")

            def mixer0():
                pe.wait_ge(hist_in, 16 * 5)
                for c in range(NCHUNK):
                    last = tr(bank[0][:, 24 * c:24 * c + 24], chist_rows[0:24, P * c:P * c + P], ident[0:24, 0:24])
                last.then_inc(hist_ps, 1)
                for g in range(NH):
                    last = tr(bank[1][:, 120 * g:120 * g + 120], phist_rows[0:120, P * g:P * g + P],
                              ident[0:120, 0:120])
                last.then_inc(hist_ps, 1)
                tr(bank[2][:, 0:53], par_rows[0:53, :], ident[0:53, 0:53]).then_inc(hist_ps, 1)
                pe.wait_ge(xt_lo, NT)
                pe.wait_ge(xt_hi, NT)
                pe.wait_ge(wab_ready, 1)
                for k in range(KD):
                    mm(bank[4][0:68, :], wab[:, k, :], XT[:, k, 0:TP], start=(k == 0), stop=(k == KD - 1))
                    last = mm(bank[5][0:68, 0:TS], wab[:, k, :], XT[:, k, TP:T], start=(k == 0), stop=(k == KD - 1))
                last.then_inc(ab_ps, 1)
                pe.wait_ge(hist_out, 3)
                for c in range(NPROJ):
                    project(c, w_in, proj_ps, proj_out)
                    if 2 <= c < 10:
                        n = c - 2
                        pe.wait_ge(sq_done, n + 1)
                        if n:
                            pe.wait_ge(inv_done, n)
                        else:
                            pe.wait_ge(rows_ready, 1)
                        mm(bank[4][:, :], ones[:, :], SQ[:, n % 2, 0:TP], start=True, stop=True)
                        mm(bank[5][:, 0:TS], ones[:, :], SQ[:, n % 2, TP:T], start=True, stop=True).then_inc(ssq_ps, 1)
                    if 10 <= c < 14:
                        h = c - 10
                        if h:
                            pe.wait_ge(gcb_out, h)
                        else:
                            pe.wait_ge(inv_done, 8)
                        mm(bank[4][:, :], sel_gc[:, h, :], RT[0:68, 0:TP], start=True, stop=True)
                        mm(bank[5][:, 0:TS], sel_gc[:, h, :], RT[0:68, TP:T], start=True, stop=True).then_inc(gcb_ps, 1)
                    if c == 14:
                        pe.wait_ge(gcb_out, 4)
                        for t in range(NT):
                            last = tr(bank[4][0:ROWS[t], 68 * t:68 * t + 68], RT[0:68, tile_cols(t)], ident[0:68, 0:68])
                        last.then_inc(col_ps, 1)
                pe.wait_ge(proj_out, NPROJ)
                pe.wait_ge(col_out, 1)
                pe.wait_ge(tail_done, NCHUNK)
                pe.wait_ge(utail_done, 1)
                for g in range(NH):
                    tr(bank[4][0:HIST, P * g:P * g + P], U[:, g, TP:TP + HIST], ident[:, :])
                for g in range(NH):
                    tr(bank[5][0:120, P * g:P * g + P], utail[:, g, :], ident[:, :])
                for g in range(3):
                    last = tr(bank[6][0:108, P * g:P * g + P], tails[:, 9 * g:9 * g + 9, :].rearrange("p j c -> p (j c)"), ident[:, :])
                last.then_inc(strow_ps, 1)
                pe.wait_ge(q_scaled, NH)
                pe.wait_ge(k_scaled, NH)
                pe.wait_ge(silu_done, NCHUNK)
                pe.wait_ge(strow_out, 1)
                for b in range(NT - 1):
                    delta_prompt(b)
                delta_samples()
                pe.wait_ge(rms_sq, 1)
                for h in range(NH):
                    mm(bank[6][0:NH, :], ms_col[:, h, :], gB[:, h, 0:TP], start=(h == 0), stop=(h == 3))
                    last = mm(bank[7][0:NH, 0:TS], ms_col[:, h, :], gB[:, h, TP:T], start=(h == 0), stop=(h == 3))
                last.then_inc(rms_ps, 1)
                pe.wait_ge(wg_in, 16)
                pe.wait_ge(pooled_done, NH)
                e_dve.wait(pe, 0, "s3")
                for g in range(NH):
                    if g:
                        pe.wait_ge(mix_b, g)
                    mm(bank[2][:, :], WG[:, g, :], POOLED[:, g, 0:TP], start=True, stop=True)
                    mm(bank[3][:, 0:TS], WG[:, g, :], POOLED[:, g, TP:T], start=True, stop=True).then_inc(group_ps, 1)
                pe.wait_ge(rms_inv, 1)
                for h in range(NH):
                    if h >= 2:
                        pe.wait_ge(rmsb_out, h - 1)
                    bb = (4, 0)[h % 2]
                    mm(bank[bb][:, :], sel_row[:, h, :], gB[0:NH, 0, 0:TP], start=True, stop=True)
                    mm(bank[bb + 1][:, 0:TS], sel_row[:, h, :], gB[0:NH, 0, TP:T], start=True, stop=True)\
                        .then_inc(rmsb_ps, 1)

            def out_projection(l):
                pe.wait_ge(mix_a, NH + KD * l)
                if l == 0:
                    pe.wait_ge(mix_b, NH)
                pe.wait_ge(wo_in, 16 * (l + 1))
                for t in range(NT):
                    if t >= 2:
                        pe.wait_ge(norm_sum, 2 * l * NT + t - 1)
                    for half in range(2):
                        for k in range(KD):
                            last = mm(bank[2 * (t % 2) + half][0:ROWS[t], :], XT[:, k, tile_cols(t)],
                                      WO0[:, k, 512 * half:512 * half + 512], start=(k == 0), stop=(k == KD - 1))
                    last.then_inc(out_ps, 1)

            def route(l):
                pe.wait_ge(router_in, 32)
                n = 1 + 2 * l
                pe.wait_ge(norm_sum, 2 * l * NT + NT)
                for t in range(NT):
                    pe.wait_ge(xt_lo, n * NT + t + 1)
                    pe.wait_ge(xt_hi, n * NT + t + 1)
                    for k in range(KD):
                        last = mm(bank[0][0:ROWS[t], NE * t:NE * t + NE], XT[:, k, tile_cols(t)], rw[:, k, :],
                                  start=(k == 0), stop=(k == KD - 1))
                last.then_inc(logits_ps, 1)
                pe.wait_ge(onehot_ready, l + 1)
                hot = rt[:, 11, :]
                mm(bank[1][:, 0:80], m_before[:, :], hot, start=True, stop=True)
                mm(bank[2][:, 0:80], ones[:, :], hot, start=True, stop=True).then_inc(rank_ps, 1)

            def gather_transposed(l, pairs, u, g):
                pe.wait_ge(xg_in[u], arrivals(l, pairs))
                at_least(pe, xgt_ready, g * 2)
                for k in range(KD):
                    last = tr(heads_of(4 + k // 4)[:, k % 4, :], XG[u][:, P * k:P * k + P], ident[:, :])
                last.then_inc(xg_ps, 1)

            def gate_up(l, pairs, u, g):
                pe.wait_ge(xgt_ready, g * 2 + 2)
                pe.wait_ge(gate_in[u], arrivals(l, pairs))
                at_least(pe, sg_done, g - 1)
                for k in range(KD):
                    last = mm(bank[u][:, :], XGT[:, k, :], WGT[u][:, k, :], start=(k == 0), stop=(k == KD - 1))
                last.then_inc(gate_ps, 1)
                pe.wait_ge(up_in[u], arrivals(l, pairs))
                at_least(pe, h_ready, g - 1)
                for k in range(KD):
                    last = mm(bank[2 + u][:, :], XGT[:, k, :], WUP[u][:, k, :], start=(k == 0), stop=(k == KD - 1))
                last.then_inc(up_ps, 1)

            def h_transposed(u, g):
                pe.wait_ge(h_ready, g + 1)
                at_least(pe, y0_out, g)
                for f in range(4):
                    last = tr(heads_of(7)[:, f, :], HB[u][:, P * f:P * f + P], ident[:, :])
                last.then_inc(h_ps, 1)

            def down(l, pairs, u, g):
                pe.wait_ge(ht_ready, g + 1)
                pe.wait_ge(down_in[u], arrivals(l, pairs))
                at_least(pe, y1_out, g)
                for half, done in ((1, y1_ps), (0, y0_ps)):
                    for f in range(4):
                        last = mm(bank[7 - half][:, :], HT[:, f, :], WDN[u][:, f, 512 * half:512 * half + 512],
                                  start=(f == 0), stop=(f == 3))
                    last.then_inc(done, 1)

            def experts(l):
                base = NE * l

                def step(i, v):
                    u, g = (1 + v) % 2, i * 2 + (base + 1 + v)
                    gate_up(l, i + (v + 1), u, g)
                    h_transposed(1 - u, g - 1)
                    gather_transposed(l, i + 2, 1 - u, g + 1)
                    down(l, i + 1, 1 - u, g - 1)

                pe.wait_ge(pos_ready, l + 1)
                pe.wait_ge(xt_hi, (2 * l + 2) * NT)
                gather_transposed(l, 1, 0, base)
                gate_up(l, 1, 0, base)
                gather_transposed(l, 1, 1, base + 1)
                step(0, 0)
                step(0, 1)
                with pe.Fori(1, NE // 2 - 1) as i:
                    step(i, 0)
                    step(i, 1)
                gate_up(l, 8, 1, base + 15)
                h_transposed(0, base + 14)
                down(l, 8, 0, base + 14)
                h_transposed(1, base + 15)
                down(l, 8, 1, base + 15)
                overflow(l)

            def overflow(l):
                s = ov[l]
                most = pe.value_load(over_i[0:1, 0:1], min_val=0, max_val=T)
                with pe.If(most > P):
                    pe.wait_ge(y0_out, NE * (l + 1))
                    pe.wait_ge(y1_out, NE * (l + 1))
                    pe.sem_inc(s["pe"], 4)
                    with pe.Fori(1, BLOCKS) as b:
                        with pe.Fori(0, NE) as e:
                            n = b * NE + e - (NE - 1)
                            ov_wait(pe, l, n, "xg")
                            for k in range(KD):
                                last = tr(heads_of(4 + k // 4)[:, k % 4, :], XG[0][:, P * k:P * k + P], ident[:, :])
                            last.then_inc(s["pe"], 1)
                            ov_wait(pe, l, n, "xgt")
                            ov_wait(pe, l, n, "w")
                            for to, w in ((0, WGT), (2, WUP)):
                                for k in range(KD):
                                    last = mm(bank[to][:, :], XGT[:, k, :], w[0][:, k, :],
                                              start=(k == 0), stop=(k == KD - 1))
                            last.then_inc(s["pe"], 1)
                            ov_wait(pe, l, n, "h")
                            for f in range(4):
                                last = tr(heads_of(7)[:, f, :], HB[0][:, P * f:P * f + P], ident[:, :])
                            last.then_inc(s["pe"], 1)
                            ov_wait(pe, l, n, "ht")
                            for half in (1, 0):
                                for f in range(4):
                                    last = mm(bank[7 - half][:, :], HT[:, f, :],
                                              WDN[0][:, f, 512 * half:512 * half + 512],
                                              start=(f == 0), stop=(f == 3))
                            last.then_inc(s["pe"], 1)

            def mixer1():
                pe.wait_ge(hist1_in, 16 * 7)
                pe.wait_ge(y0_out, NE)
                for c in range(KD):
                    last = tr(bank[0][:, 24 * c:24 * c + 24], lhist_rows[0:24, P * c:P * c + P], ident[0:24, 0:24])
                last.then_inc(lru_hist_ps, 1)
                for c in range(KD):
                    last = tr(bank[1][:, NS * c:NS * c + NS], lstate_rows[0:NS, P * c:P * c + P], ident[0:NS, 0:NS])
                last.then_inc(lru_hist_ps, 1)
                tr(bank[2][:, 0:64], par_rows1[0:64, :], ident[0:64, 0:64]).then_inc(lru_hist_ps, 1)
                pe.wait_ge(lru_hist_out, 3)
                pe.wait_ge(xt_lo, 3 * NT)
                pe.wait_ge(xt_hi, 3 * NT)
                for c in range(16):
                    project(c, w1_in, proj1_ps, proj1_out)
                pe.wait_ge(wri_in, 32)
                pe.wait_ge(proj1_out, 16)
                for m in range(KD):
                    for n in range(2):
                        j = 2 * m + n
                        pe.wait_ge(conv1_done, 2 * (m // 2) + 2)
                        at_least(pe, lru_gates_done, j - 3)
                        b0 = (4, 0, 2, 6)[j % 4]
                        for k in range(2):
                            w = WRI[:, n, 2 * (m // 2) + k, P * (m % 2):P * (m % 2) + P]
                            x = XC[:, 2 * (m // 2) + k, :]
                            mm(bank[b0][:, :], w, x[:, 0:TP], start=(k == 0), stop=(k == 1))
                            last = mm(bank[b0 + 1][:, 0:TS], w, x[:, TP:T], start=(k == 0), stop=(k == 1))
                        last.then_inc(lru_gate_ps, 1)
                pe.wait_ge(lru_gates_done, 16)
                pe.wait_ge(tail1_done, KD)
                for g in range(2):
                    last = tr(bank[4][0:108, P * g:P * g + P], tails1[:, :, :]
                              .rearrange("p j c -> p (j c)")[:, 108 * g:108 * g + 108], ident[:, :])
                last.then_inc(st1_ps, 1)
                pe.wait_ge(lru_h, KD)
                tr(bank[5][0:72, 0:P], lru_last, ident[:, :]).then_inc(st1_ps, 1)

            to_channels(0)
            mixer0()
            for l in range(2):
                out_projection(l)
                to_channels(1 + 2 * l)
                route(l)
                experts(l)
                if l == 0:
                    to_channels(2)
                    mixer1()

        @block.scalar
        def _(act):
            def copy(out, in_, scale=1.0):
                return nc.scalar.activation(out, in_, ACT.Copy, scale=scale)

            def to_channels(n):
                for t in range(NT):
                    act.wait_ge(xt_ps, n * NT + t + 1)
                    copy(XT[:, 4:8, tile_cols(t)], heads_of(TILE_BANK(t) + 1, P, ROWS[t])).then_inc(xt_hi, 1)

            def gates():
                act.wait_ge(consts_ready, 1)
                act.wait_ge(ab_ps, 1)
                nc.scalar.activation(RT[0:4, 0:TP], bank[4][0:4, :], ACT.Sigmoid).then_inc(gate_act, 1)
                nc.scalar.activation(RT[0:4, TP:T], bank[5][0:4, 0:TS], ACT.Sigmoid).then_inc(gate_act, 1)
                act.wait_ge(gates_in, 32)
                nc.scalar.activation(gpar[32:36, 1:2], gpar[32:36, 1:2], ACT.Exp).then_inc(gate_act, 1)
                act.wait_ge(gate_dve, 1)
                nc.scalar.activation(RB[32:36, :], RB[32:36, :], ACT.Exp).then_inc(gate_act, 1)
                act.wait_ge(gate_act, 4)
                nc.scalar.activation(RB[32:36, :], RB[32:36, :], ACT.Ln, bias=ones[32:36, 0:1]).then_inc(gate_act, 1)

            def delta_prompt(b):
                d_pe.wait(act, b, "vtr")
                for h in range(NH):
                    last = copy(vb[:, h, :], heads_of(1)[:, h, :], COL[:, b, h:h + 1])
                d_act.end(last, b, "vb")
                d_pool.wait(act, b, "max")
                d_act.end(nc.scalar.activation(dmx, dmx, ACT.Exp, scale=-1.0), b, "dbd")
                d_pool.wait(act, b, "min")
                d_act.end(nc.scalar.activation(dmn, dmn, ACT.Exp), b, "dt")
                d_act.end(nc.scalar.activation(egB, gB[:, :, tile_cols(b)], ACT.Exp), b, "eg")
                for r in range(5):
                    d_pe.wait(act, b, "pt" if r == 0 else f"pt{r}")
                    d_act.end(copy((PTa, PTb)[r % 2], heads_of(4 if r == 0 else 6)), b, f"pt{r}")
                d_pe.wait(act, b, "tb")
                d_act.end(copy(TB, heads_of(4)), b, "tb")
                d_pe.wait(act, b, "nw")
                d_act.end(copy(nwT, heads_of(6), -1.0), b, "nw")
                d_pe.wait(act, b, "o")
                d_act.end(copy(QKV[:, 8:12, tile_cols(b)], heads_of(1)), b, "o")

            def delta_samples():
                b, n = NT - 1, TS
                e_pe.wait(act, 0, "vtr")
                for h in range(NH):
                    last = copy(vb[0:n, h, :], heads_of(1, n)[:, h, :], COL[0:n, b, h:h + 1])
                e_act.end(last, 0, "vb")
                e_pool.wait(act, 0, "max")
                e_act.end(nc.scalar.activation(dmx[0:n, :, 0:n], dmx[0:n, :, 0:n], ACT.Exp, scale=-1.0), 0, "dbd")
                e_pool.wait(act, 0, "min")
                e_act.end(nc.scalar.activation(dmn[0:n, :, 0:n], dmn[0:n, :, 0:n], ACT.Exp), 0, "dt")
                e_act.end(nc.scalar.activation(egB[:, :, 0:n], gB[:, :, tile_cols(b)], ACT.Exp), 0, "eg")
                for r in range(2):
                    e_pe.wait(act, 0, "pt" if r == 0 else "pt1")
                    e_act.end(copy((PTa, PTb)[r][0:n, :, 0:n], heads_of(4 if r == 0 else 6, n, n)), 0, f"pt{r}")
                e_pe.wait(act, 0, "nw")
                e_act.end(copy(nwT[:, :, 0:n], heads_of(6, P, n), -1.0), 0, "nw")
                e_pe.wait(act, 0, "ut")
                e_act.end(copy(Yo[:, :, 0:n], heads_of(0, P, n)), 0, "ut")

            def mixer0():
                gates()
                for c in range(NPROJ):
                    pb, sbk = bank[c % 3], bank[(3, 6, 7)[c % 3]]
                    act.wait_ge(proj_ps, c + 1)
                    if c < NCHUNK:
                        if c >= 3:
                            act.wait_ge(conv_done, c - 2)
                            act.wait_ge(tail_done, c - 2)
                        buf = EXTB[c % 3]
                        copy(buf[:, CONV - 1:EXT_P], pb[:, :])
                        copy(ext_samples(buf)[:, :, CONV - 1:], sbk[:, 0:TS].rearrange("p (s l) -> p s l", s=NS))\
                            .then_inc(proj_out, 1)
                    elif c < 16:
                        g = c - NCHUNK
                        copy(U[:, g, HIST:UEP], pb[:, :])
                        copy(U[:, g, UEP:UE].rearrange("p (s l) -> p s l", s=NS)[:, :, HIST:],
                             sbk[:, 0:TS].rearrange("p (s l) -> p s l", s=NS)).then_inc(proj_out, 1)
                    else:
                        nc.scalar.activation(Z[:, c - 16, 0:TP], pb[:, :], ACT.Silu)
                        nc.scalar.activation(Z[:, c - 16, TP:T], sbk[:, 0:TS], ACT.Silu).then_inc(proj_out, 1)
                    if 1 <= c <= NCHUNK:
                        n = c - 1
                        act.wait_ge(conv_done, n + 1)
                        nc.scalar.activation(QKV[:, n, :], CV[:, n % 2, :], ACT.Silu).then_inc(silu_done, 1)
                        if n < 8:
                            if n >= 2:
                                act.wait_ge(ssq_ps, n - 1)
                            act.wait_ge(silu_done, n + 1)
                            nc.scalar.activation(SQ[:, n % 2, :], QKV[:, n, :], ACT.Square).then_inc(sq_done, 1)
                    if 10 <= c < 14:
                        h = c - 10
                        act.wait_ge(gcb_ps, h + 1)
                        copy(gB[:, h, 0:TP], bank[4][:, :])
                        copy(gB[:, h, TP:T], bank[5][:, 0:TS]).then_inc(gcb_out, 1)
                act.wait_ge(gcb_out, 4)
                act.wait_ge(inv_done, 8)
                for n in range(2):
                    nc.scalar.activation(INV[:, 4 * n:4 * n + 4, :], INV[:, 4 * n:4 * n + 4, :], ACT.Sqrt)\
                        .then_inc(roots_done, 1)
                act.wait_ge(col_out, 1)
                nc.scalar.activation(ecol[:, :, :], COL[:, :, 32:36], ACT.Exp).then_inc(egl_done, 1)
                nc.scalar.activation(kdc[:, :, :], COL[:, :, 64:68], ACT.Exp).then_inc(egl_done, 1)
                nc.scalar.activation(egl[:, :, 0:4], gB[:, :, 0:TP].rearrange("p h (c l) -> p h c l", l=P)[:, :, :, P - 1],
                                     ACT.Exp).then_inc(egl_done, 1)
                nc.scalar.activation(egl[:, :, 4:12], gB[:, :, TP:T].rearrange("p h (c l) -> p h c l", l=LS)[:, :, :, LS - 1],
                                     ACT.Exp).then_inc(egl_done, 1)
                for b in range(NT - 1):
                    delta_prompt(b)
                delta_samples()
                e_dve.wait(act, 0, "o")
                nc.scalar.activation(gB, QKV[:, 8:12, :], ACT.Square).then_inc(rms_sq, 1)
                for g in range(NH):
                    act.wait_ge(group_ps, g + 1)
                    sc = par[:, 48 + g:49 + g]
                    copy(XT[:, NH + g, 0:TP], bank[2][:, :], sc)
                    copy(XT[:, NH + g, TP:T], bank[3][:, 0:TS], sc).then_inc(mix_b, 1)
                act.wait_ge(rms_eps, 1)
                nc.scalar.activation(gB[0:NH, 0, :], gB[0:NH, 0, :], ACT.Sqrt).then_inc(rms_root, 1)

            def norm(q):
                def scaled(t):
                    act.wait_ge(norm_coef, q * NT + t + 1)
                    r = ROWS[t]
                    nc.scalar.activation(X[0:r, t, :], X[0:r, t, :], ACT.Identity, bias=lnw[0:r, t, 15:16],
                                         scale=lnw[0:r, t, 14:15]).then_inc(norm_scaled, 1)

                for t in range(NT):
                    if q % 2:
                        u = t % 2
                        act.wait_ge(ysel_in[u], 32 * ((q // 2) * (3 - u) + t // 2 + 1))
                        copy(Y1[u][0:ROWS[t], :], Y1[u][0:ROWS[t], :], wsel[0:ROWS[t], 0, t:t + 1])\
                            .then_inc(ysel_scaled, 1)
                    act.wait_ge(norm_stats, q * NT + t + 1)
                    r = ROWS[t]
                    nc.scalar.activation(lnw[0:r, t, 14:15], lnw[0:r, t, 13:14], ACT.Sqrt).then_inc(norm_root, 1)
                    if t:
                        scaled(t - 1)
                scaled(NT - 1)

            def route(l):
                act.wait_ge(logits_ps, l + 1)
                nc.scalar.activation(scores[:, 0:4, :], bank[0][:, 0:64].rearrange("p (t e) -> p t e", t=4), ACT.Sigmoid)
                nc.scalar.activation(scores[0:TS, 4, :], bank[0][0:TS, 64:80], ACT.Sigmoid).then_inc(scores_done, 1)

            def y_view(l):
                return y_rows[l].rearrange("(b s e) d -> b s e d", b=BLOCKS, s=P)

            def experts(l):
                base = NE * l

                def h_copied(g):
                    act.wait_ge(h_ps, g + 1)
                    copy(HT, heads_of(7)).then_inc(ht_ready, 1)

                def silu(u, g):
                    act.wait_ge(gate_ps, g + 1)
                    at_least(act, h_ready, g - 1)
                    nc.scalar.activation(SG[u], bank[u][:, :], ACT.Silu).then_inc(sg_done, 1)

                def result(pairs, u, g, e):
                    act.wait_ge(y0_ps, g + 1)
                    at_least(act, y_stored[u], arrivals(l, pairs - 1))
                    copy(YO[u][:, 0:512], bank[7][:, :]).then_inc(y0_out, 1)
                    act.wait_ge(y0_out, g + 1)
                    act.wait_ge(y1_out, g + 1)
                    act.dma_start(y_view(l)[0, :, bass.ds(e, 1), :].rearrange("s o d -> s (o d)"), YO[u])\
                       .then_inc(y_stored[u], 16)

                def step(i, v):
                    u, g = (1 + v) % 2, i * 2 + (base + 1 + v)
                    silu(u, g)
                    h_copied(g - 1)
                    result(i + 1, 1 - u, g - 1, i * 2 + v)

                silu(0, base)
                step(0, 0)
                step(0, 1)
                with act.Fori(1, NE // 2 - 1) as i:
                    step(i, 0)
                    step(i, 1)
                silu(1, base + 15)
                h_copied(base + 14)
                result(8, 0, base + 14, 14)
                h_copied(base + 15)
                result(8, 1, base + 15, 15)
                overflow(l)

            def overflow(l):
                s = ov[l]
                act.wait_ge(pos_ready, l + 1)
                most = act.value_load(over_i[0:1, 0:1], min_val=0, max_val=T)
                with act.If(most > P):
                    for u in range(2):
                        act.wait_ge(y_stored[u], arrivals(l, 8))
                    with act.Fori(1, BLOCKS) as b:
                        with act.Fori(0, NE) as e:
                            n = b * NE + e - (NE - 1)
                            ov_wait(act, l, n, "gu_ps")
                            nc.scalar.activation(SG[0], bank[0][:, :], ACT.Silu).then_inc(s["act"], 1)
                            ov_wait(act, l, n, "h_ps")
                            copy(HT, heads_of(7)).then_inc(s["act"], 1)
                            ov_wait(act, l, n, "y_ps")
                            copy(YO[0][:, 0:512], bank[7][:, :]).then_inc(s["act"], 1)
                            ov_wait(act, l, n, "y_a")
                            ov_wait(act, l, n, "y_d")
                            act.dma_start(y_view(l)[bass.ds(b, 1), :, bass.ds(e, 1), :]
                                          .rearrange("q s o d -> (q s) (o d)"), YO[0]).then_inc(s["stored"], 16)
                            ov_wait(act, l, n, "stored")

            def mixer1():
                act.wait_ge(lru_par, 1)
                nc.scalar.activation(par[:, 80:88], par[:, 80:88], ACT.Exp).then_inc(lru_par, 1)
                act.wait_ge(lru_par, 2)
                nc.scalar.activation(par[:, 80:88], par[:, 80:88], ACT.Ln, bias=ones[:, 0:1]).then_inc(lru_par, 1)
                for c in range(16):
                    pb, sbk = bank[c % 3], bank[(3, 6, 7)[c % 3]]
                    act.wait_ge(proj1_ps, c + 1)
                    if c < KD:
                        nc.scalar.activation(YB[:, c, 0:TP], pb[:, :], ACT.Gelu_apprx_tanh)
                        nc.scalar.activation(YB[:, c, TP:T], sbk[:, 0:TS], ACT.Gelu_apprx_tanh).then_inc(proj1_out, 1)
                    else:
                        m = c - KD
                        if m >= 3:
                            act.wait_ge(conv1_done, m - 2)
                            act.wait_ge(tail1_done, m - 2)
                        buf = EXT1[m % 3]
                        copy(buf[:, CONV - 1:EXT_P], pb[:, :])
                        copy(ext_samples(buf)[:, :, CONV - 1:], sbk[:, 0:TS].rearrange("p (s l) -> p s l", s=NS))\
                            .then_inc(proj1_out, 1)
                for m in range(KD):
                    for n, (to, b_at) in enumerate(((R_, 40), (GI, 48))):
                        j = 2 * m + n
                        act.wait_ge(lru_gate_ps, j + 1)
                        b0 = (4, 0, 2, 6)[j % 4]
                        bias = par[:, b_at + m:b_at + m + 1]
                        nc.scalar.activation(to[:, m, 0:TP], bank[b0][:, :], ACT.Sigmoid, bias=bias)
                        nc.scalar.activation(to[:, m, TP:T], bank[b0 + 1][:, 0:TS], ACT.Sigmoid, bias=bias)\
                            .then_inc(lru_gates_done, 1)
                act.wait_ge(lru_gates_done, 16)
                act.wait_ge(lru_par, 4)
                for m in range(KD):
                    nc.scalar.activation(XT[:, m, :], R_[:, m, :], ACT.Exp, scale=par[:, 72 + m:73 + m])\
                        .then_inc(lru_a, 1)
                    act.wait_ge(lru_a, m + 1)
                    nc.scalar.activation(R_[:, m, :], R_[:, m, :], ACT.Tanh, scale=par[:, 64 + m:65 + m])\
                        .then_inc(lru_t, 1)
                for m in range(KD):
                    act.wait_ge(lru_w, m + 1)
                    nc.scalar.activation(R_[:, m, :], R_[:, m, :], ACT.Sqrt).then_inc(lru_root, 1)

            to_channels(0)
            mixer0()
            for l in range(2):
                norm(2 * l)
                to_channels(1 + 2 * l)
                route(l)
                experts(l)
                norm(2 * l + 1)
                if l == 0:
                    to_channels(2)
                    mixer1()

        @block.vector
        def _(dve):
            mine = Own(dve, own["dve"])
            V = nc.vector

            def to_channels(n):
                for t in range(NT):
                    dve.wait_ge(xt_ps, n * NT + t + 1)
                    V.tensor_copy(XT[:, 0:4, tile_cols(t)], heads_of(TILE_BANK(t), P, ROWS[t])).then_inc(xt_lo, 1)

            def gates():
                g = slice(32, 36)
                dve.wait_ge(gates_in, 32)
                dve.wait_ge(ab_ps, 1)
                dve.wait_ge(gate_act, 2)
                mine(V.tensor_scalar(RA[g, 0:TP], bank[4][g, :], gpar[g, 0:1], None, ALU.add))
                mine(V.tensor_scalar(RA[g, TP:T], bank[5][g, 0:TS], gpar[g, 0:1], None, ALU.add))
                mine.settle()
                V.scalar_tensor_tensor(RB[g, :], RA[g, :], -1.0, RA[g, :], ALU.mult, ALU.min).then_inc(gate_dve, 1)
                dve.wait_ge(gate_dve, 1)
                mine(V.tensor_scalar(RA[g, :], RA[g, :], 0.0, None, ALU.max))
                dve.wait_ge(gate_act, 5)
                mine.settle()
                mine(V.tensor_tensor(RB[g, :], RB[g, :], RA[g, :], ALU.add))
                mine.settle()
                mine(V.tensor_scalar(RB[g, :], RB[g, :], gpar[g, 1:2], -1.0, ALU.mult, ALU.mult))
                mine.settle()
                mine(V.tensor_tensor_scan(RT[g, :], keep[g, :], RB[g, :], 0.0, ALU.mult, ALU.add))
                mine.settle()
                for lo, n, l in ((0, TP // P, P), (TP, NS, LS)):
                    gc = RT[g, lo:lo + n * l].rearrange("p (c l) -> p c l", l=l)
                    last = V.tensor_tensor(RT[64:68, lo:lo + n * l].rearrange("p (c l) -> p c l", l=l),
                                           gc[:, :, l - 1:l].broadcast_to([4, n, l]), gc, ALU.subtract)
                last.then_inc(rows_ready, 1)

            def conv(c, buf, hist, out, taps, bias):
                mine(V.tensor_copy(ext_samples(buf)[:, :, 0:CONV - 1], hist.rearrange("p (s j) -> p s j", s=NS)))
                mine.settle()
                for j in range(CONV):
                    w = par[:, taps * j + c:taps * j + c + 1]
                    srcs = ((out[:, 0:TP], buf[:, j:j + TP]), (samples(out), ext_samples(buf)[:, :, j:j + LS]))
                    for dst, src in srcs:
                        if j == 0 and bias is not None:
                            last = V.tensor_scalar(dst, src, w, bias, ALU.mult, ALU.add)
                        elif j == 0:
                            last = V.tensor_scalar(dst, src, w, None, ALU.mult)
                        else:
                            last = V.scalar_tensor_tensor(dst, src, w, dst, ALU.mult, ALU.add)
                        if j < CONV - 1:
                            mine(last)
                    if j < CONV - 1:
                        mine.settle()
                return last

            def delta_prompt(b):
                cols = tile_cols(b)
                for h in range(NH):
                    last = V.tensor_scalar(dif[:, h, :], gB[:, h, cols], COL[:, b, 32 + h:33 + h], None, ALU.subtract)
                d_dve.end(last, b, "dif")
                d_pe.wait(dve, b, "ktr")
                for name, to, by in (("kbg", kbg, kbgc), ("kd", kd, kdc)):
                    for h in range(NH):
                        last = V.tensor_scalar(to[:, h, :], heads_of(0)[:, h, :], by[:, b, h:h + 1], None, ALU.mult)
                    d_dve.end(last, b, name)
                d_pe.wait(dve, b, "gram")
                for name, to, mask, ready in (("p0", Pa, Dbd, "bd"), ("off", Noff, Doff, "off")):
                    d_pool.wait(dve, b, ready)
                    for h in range(NH):
                        last = V.scalar_tensor_tensor(to[:, h, :], heads_of(2)[:, h, :], COL[:, b, h:h + 1],
                                                      mask[:, h, :], ALU.mult, ALU.mult)
                    d_dve.end(last, b, name)
                d_pe.wait(dve, b, "qk")
                d_pool.wait(dve, b, "incl")
                d_dve.end(V.tensor_tensor(aT, heads_of(3), DTm, ALU.mult), b, "a")
                d_act.wait(dve, b, "pt0")
                d_dve.end(V.tensor_tensor(TT, PTa, ident[:, :].unsqueeze(1).broadcast_to([P, NH, P]), ALU.add), b, "tt0")
                for r in range(1, 6):
                    d_pe.wait(dve, b, f"p{r}")
                    d_dve.end(V.tensor_copy((Pa, Pb)[r % 2], heads_of(5)), b, f"p{r}")
                    d_pe.wait(dve, b, f"x{r}")
                    d_dve.wait(dve, b, f"tt{r - 1}")
                    d_dve.end(V.tensor_tensor(TT, TT, heads_of(7), ALU.add), b, f"tt{r}")
                d_pe.wait(dve, b, "y")
                d_dve.end(V.tensor_copy(Yo, heads_of(5)), b, "y")
                d_pe.wait(dve, b, "x6")
                d_dve.wait(dve, b, "tt5")
                d_dve.end(V.tensor_tensor(TT, TT, heads_of(7), ALU.add), b, "tt6")
                d_pe.wait(dve, b, "un")
                d_dve.end(V.tensor_copy(un, heads_of(0)), b, "un")
                d_pe.wait(dve, b, "sn")
                if b:
                    d_dve.wait(dve, b - 1, "s")
                for h in range(NH):
                    last = V.scalar_tensor_tensor(SP_[:, h, :], SP_[:, h, :], egl[:, h, b:b + 1], heads_of(2)[:, h, :],
                                                  ALU.mult, ALU.add)
                d_dve.end(last, b, "s")

            def delta_samples():
                b, n = NT - 1, TS
                cols = tile_cols(b)
                for h in range(NH):
                    last = V.tensor_scalar(dif[0:n, h, 0:n], gB[0:n, h, cols], COL[0:n, b, 32 + h:33 + h], None,
                                           ALU.subtract)
                e_dve.end(last, 0, "dif")
                e_pe.wait(dve, 0, "ktr")
                for name, to, by in (("kbg", kbg, kbgc), ("kd", kd, kdc)):
                    for h in range(NH):
                        last = V.tensor_scalar(to[0:n, h, :], heads_of(0, n)[:, h, :], by[0:n, b, h:h + 1], None,
                                               ALU.mult)
                    e_dve.end(last, 0, name)
                e_pe.wait(dve, 0, "gram")
                e_pool.wait(dve, 0, "bd")
                for h in range(NH):
                    last = V.scalar_tensor_tensor(Pa[0:n, h, 0:n], heads_of(2, n, n)[:, h, :], COL[0:n, b, h:h + 1],
                                                  Dbd[0:n, h, 0:n], ALU.mult, ALU.mult)
                e_dve.end(last, 0, "p0")
                e_pe.wait(dve, 0, "qk")
                e_pool.wait(dve, 0, "incl")
                e_dve.end(V.tensor_tensor(aT[0:n, :, 0:n], heads_of(3, n, n), DTm[0:n, :, 0:n], ALU.mult), 0, "a")
                e_act.wait(dve, 0, "pt0")
                tt = TT[0:n, :, 0:n]
                e_dve.end(V.tensor_tensor(tt, PTa[0:n, :, 0:n], ident[0:n, 0:n].unsqueeze(1).broadcast_to([n, NH, n]),
                                          ALU.add), 0, "tt0")
                for r in (1, 2):
                    e_pe.wait(dve, 0, f"p{r}")
                    e_dve.end(V.tensor_copy((Pa, Pb)[r % 2][0:n, :, 0:n], heads_of(5, n, n)), 0, f"p{r}")
                    e_pe.wait(dve, 0, f"x{r}")
                    e_dve.wait(dve, 0, f"tt{r - 1}")
                    e_dve.end(V.tensor_tensor(tt, tt, heads_of(7, n, n), ALU.add), 0, f"tt{r}")
                e_pe.wait(dve, 0, "un")
                e_dve.end(V.tensor_copy(un[0:n, :, :], heads_of(4, n)), 0, "un")
                e_pe.wait(dve, 0, "o")
                e_dve.end(V.tensor_copy(QKV[:, 8:12, cols], heads_of(1, P, n)), 0, "o")
                for h in range(NH):
                    e_pe.wait(dve, 0, f"sn{h}")
                    for s in range(NS):
                        st = SS[:, NH * s + h, :]
                        last = V.scalar_tensor_tensor(st, st, egl[:, h, 4 + s:5 + s], heads_of(2 + s // 4)[:, s % 4, :],
                                                      ALU.mult, ALU.add)
                    e_dve.end(last, 0, f"s{h}")

            def mixer0():
                dve.wait_ge(consts_ready, 1)
                V.reciprocal(inv_cnt[:, :], inv_cnt[:, :])
                dve.wait_ge(wab_sem, 16)
                V.tensor_copy(wab[:, :, 0:4], wab_in[:, :, 0:4])
                V.tensor_copy(wab[:, :, 32:36], wab_in[:, :, 4:8]).then_inc(wab_ready, 1)
                dve.wait_ge(hist_ps, 1)
                V.tensor_copy(chistT, bank[0][:, 0:288].rearrange("p (c j) -> p c j", c=NCHUNK)).then_inc(hist_out, 1)
                dve.wait_ge(hist_ps, 2)
                V.tensor_copy(U[:, :, UEP:UE].rearrange("p g (s l) -> p g s l", s=NS)[:, :, :, 0:HIST],
                              bank[1][:, 0:480].rearrange("p (g s l) -> p g s l", g=NH, s=NS)).then_inc(hist_out, 1)
                dve.wait_ge(hist_ps, 3)
                V.tensor_copy(par[:, 0:53], bank[2][:, 0:53]).then_inc(hist_out, 1)
                gates()
                dve.wait_ge(hist_out, 3)
                for c in range(NCHUNK):
                    dve.wait_ge(proj_out, c + 1)
                    if c >= 2:
                        dve.wait_ge(silu_done, c - 1)
                    conv(c, EXTB[c % 3], chistT[:, c, :], CV[:, c % 2, :], NCHUNK, None).then_inc(conv_done, 1)
                    if 3 <= c < 11:
                        n = c - 3
                        dve.wait_ge(ssq_ps, n + 1)
                        mine(V.tensor_scalar(INV[:, n, 0:TP], bank[4][:, :], L2_EPS, None, ALU.add))
                        mine(V.tensor_scalar(INV[:, n, TP:T], bank[5][:, 0:TS], L2_EPS, None, ALU.add))
                        mine.settle()
                        V.reciprocal(INV[:, n, :], INV[:, n, :]).then_inc(inv_done, 1)
                dve.wait_ge(col_ps, 1)
                V.tensor_copy(COL[:, 0:4, :], bank[4][:, 0:272].rearrange("p (t c) -> p t c", t=4))
                V.tensor_copy(COL[0:TS, 4, :], bank[4][0:TS, 272:340]).then_inc(col_out, 1)
                for g, w in enumerate(WINDOWS):
                    dve.wait_ge(psum_done, g + 1)
                    s, u = PT_[:, g % 2, :], U[:, g, :]
                    mine(V.scalar_tensor_tensor(POOLED[:, g, w:TP], s[:, HIST + w:UEP], 1.0 / w, u[:, HIST + w:UEP],
                                                ALU.mult, ALU.subtract))
                    ss, us = (x[:, UEP:UE].rearrange("p (s l) -> p s l", s=NS)[:, :, HIST:] for x in (s, u))
                    mine(V.scalar_tensor_tensor(samples(POOLED[:, g, :]), ss, 1.0 / w, us, ALU.mult, ALU.subtract))
                    mine(V.tensor_tensor(POOLED[:, g, 0:w], s[:, HIST:HIST + w], inv_cnt[:, 0:w], ALU.mult))
                    mine.settle()
                    V.tensor_tensor(POOLED[:, g, 0:w], POOLED[:, g, 0:w], u[:, HIST:HIST + w], ALU.subtract)\
                        .then_inc(pooled_done, 1)
                dve.wait_ge(strow_ps, 1)
                V.tensor_copy(rows_out[0:HIST, 0:512], bank[4][0:HIST, :])
                V.tensor_copy(rows_out[0:120, 512:1024], bank[5][0:120, :])
                V.tensor_copy(rows_out[0:108, 1024:1408], bank[6][0:108, 0:384]).then_inc(strow_out, 1)
                dve.wait_ge(roots_done, 2)
                dve.wait_ge(silu_done, NCHUNK)
                for h in range(NH):
                    V.scalar_tensor_tensor(QKV[:, h, :], QKV[:, h, :], float(P) ** -0.5, INV[:, h, :], ALU.mult,
                                           ALU.mult).then_inc(q_scaled, 1)
                dve.wait_ge(egl_done, 4)
                mine(V.tensor_tensor(kbgc[:, :, :], COL[:, :, 0:4], ecol[:, :, :], ALU.mult))
                mine.settle()
                dve.wait_ge(proj_ps, NPROJ)
                for b in range(NT - 1):
                    delta_prompt(b)
                delta_samples()
                dve.wait_ge(rms_ps, 1)
                V.tensor_scalar(gB[0:NH, 0, 0:TP], bank[6][0:NH, :], RMS_EPS, None, ALU.add)
                V.tensor_scalar(gB[0:NH, 0, TP:T], bank[7][0:NH, 0:TS], RMS_EPS, None, ALU.add).then_inc(rms_eps, 1)
                dve.wait_ge(rms_root, 1)
                V.reciprocal(gB[0:NH, 0, :], gB[0:NH, 0, :]).then_inc(rms_inv, 1)
                for h in range(NH):
                    dve.wait_ge(rmsb_ps, h + 1)
                    bb, o = (4, 0)[h % 2], QKV[:, 8 + h, :]
                    V.scalar_tensor_tensor(XT[:, h, 0:TP], o[:, 0:TP], par[:, 52:53], bank[bb][:, :], ALU.mult, ALU.mult)
                    V.scalar_tensor_tensor(XT[:, h, TP:T], o[:, TP:T], par[:, 52:53], bank[bb + 1][:, 0:TS], ALU.mult,
                                           ALU.mult).then_inc(rmsb_out, 1)

            def norm(q):
                l = q // 2

                def stats(t):
                    r, n = ROWS[t], q * NT + t
                    x, w = X[0:r, t, :], lnw[0:r, t, :]
                    if q % 2 == 0:
                        dve.wait_ge(out_ps, l * NT + t + 1)
                        for half in range(2):
                            c = slice(512 * half, 512 * half + 512)
                            last = V.scalar_tensor_tensor(x[:, c], x[:, c], ALPHA, bank[2 * (t % 2) + half][0:r, :],
                                                          ALU.mult, ALU.add)
                    else:
                        dve.wait_ge(ysel_scaled, l * NT + t + 1)
                        y1, y2 = Y1[t % 2][0:r, :], Y2[t % 2][0:r, :]
                        mine(V.scalar_tensor_tensor(y1, y2, wsel[0:r, 1, t:t + 1], y1, ALU.mult, ALU.add))
                        mine.settle()
                        last = V.scalar_tensor_tensor(x, x, ALPHA, y1, ALU.mult, ALU.add)
                    last.then_inc(norm_sum, 1)
                    dve.wait_ge(norm_sum, n + 1)
                    for half in range(2):
                        mine(V.bn_stats(w[:, 6 * half:6 * half + 6], x[:, 512 * half:512 * half + 512]))
                    mine.settle()
                    mine(V.bn_aggr(w[:, 12:14], w[:, 0:12]))
                    mine.settle()
                    V.tensor_scalar(w[:, 13:14], w[:, 13:14], LN_EPS, None, ALU.add).then_inc(norm_stats, 1)

                def coefficients(t):
                    w = lnw[0:ROWS[t], t, :]
                    dve.wait_ge(norm_root, q * NT + t + 1)
                    mine(V.reciprocal(w[:, 14:15], w[:, 14:15]))
                    mine.settle()
                    V.scalar_tensor_tensor(w[:, 15:16], w[:, 12:13], -1.0, w[:, 14:15], ALU.mult, ALU.mult)\
                        .then_inc(norm_coef, 1)

                if q % 2:
                    dve.wait_ge(xrows_out, 16 * NT * (l + 1))
                stats(0)
                for t in range(NT):
                    if t + 1 < NT:
                        stats(t + 1)
                    coefficients(t)

            def route(l):
                def do(instruction):
                    mine(instruction)
                    mine.settle()

                def per(i, n):
                    return rt[:, i, 0:NT * n].rearrange("p (t g) -> p t g", t=NT)

                def first_max(values, i, n, out):
                    top = rt[:, 10, 0:NT]
                    do(V.tensor_reduce(top, values, AX.X, ALU.max))
                    do(V.tensor_tensor(per(i, n), values, top.unsqueeze(2).broadcast_to([P, NT, n]), ALU.is_equal))
                    io = iota16[:, 0:n].unsqueeze(1).broadcast_to([P, NT, n])
                    do(V.scalar_tensor_tensor(per(i, n), per(i, n), -100.0, io, ALU.mult, ALU.add))
                    do(V.tensor_reduce(top, per(i, n), AX.X, ALU.min))
                    do(V.tensor_tensor(out, per(i, n), top.unsqueeze(2).broadcast_to([P, NT, n]), ALU.is_equal))

                dve.wait_ge(router_in, 32)
                dve.wait_ge(scores_done, l + 1)
                biased, masked = per(0, NE), per(9, NE)
                do(V.tensor_tensor(biased, scores[:, :, :], rbias[:, :].unsqueeze(1).broadcast_to([P, NT, NE]), ALU.add))
                of4 = rt[:, 0, :].rearrange("p (g e) -> p g e", e=4)
                r = [rt[:, i, 0:20] for i in range(12)]
                mine(V.tensor_tensor(r[1], of4[:, :, 0], of4[:, :, 1], ALU.max))
                mine(V.tensor_tensor(r[2], of4[:, :, 0], of4[:, :, 1], ALU.min))
                mine(V.tensor_tensor(r[3], of4[:, :, 2], of4[:, :, 3], ALU.max))
                do(V.tensor_tensor(r[4], of4[:, :, 2], of4[:, :, 3], ALU.min))
                mine(V.tensor_tensor(r[5], r[1], r[3], ALU.max))
                mine(V.tensor_tensor(r[6], r[1], r[3], ALU.min))
                do(V.tensor_tensor(r[7], r[2], r[4], ALU.max))
                do(V.tensor_tensor(r[6], r[6], r[7], ALU.max))
                do(V.tensor_tensor(r[5], r[5], r[6], ALU.add))
                first_max(per(5, 4), 7, 4, per(8, 4))
                group = r[8].unsqueeze(2).broadcast_to([P, 20, 4])
                m4 = rt[:, 9, :].rearrange("p (g e) -> p g e", e=4)
                mine(V.tensor_tensor(m4, of4, group, ALU.mult))
                do(V.tensor_scalar(r[7], r[8], BIG, -BIG, ALU.mult, ALU.add))
                do(V.tensor_tensor(m4, m4, r[7].unsqueeze(2).broadcast_to([P, 20, 4]), ALU.add))
                first_max(masked, 1, NE, oh[:, 0, :, :])
                do(V.scalar_tensor_tensor(masked, oh[:, 0, :, :], -BIG, masked, ALU.mult, ALU.add))
                first_max(masked, 1, NE, oh[:, 1, :, :])
                for k in range(2):
                    do(V.tensor_tensor(per(1, NE), scores[:, :, :], oh[:, k, :, :], ALU.mult))
                    do(V.tensor_reduce(wsel[:, k, :], per(1, NE), AX.X, ALU.add))
                do(V.tensor_tensor(wsel[:, 2, :], wsel[:, 0, :], wsel[:, 1, :], ALU.add))
                do(V.reciprocal(wsel[:, 3, :], wsel[:, 2, :]))
                for k in range(2):
                    mine(V.tensor_tensor(wsel[:, k, :], wsel[:, k, :], wsel[:, 3, :], ALU.mult))
                do(V.memset(oh[TS:P, :, NT - 1, :], 0.0))
                V.tensor_tensor(per(11, NE), oh[:, 0, :, :], oh[:, 1, :, :], ALU.add).then_inc(onehot_ready, 1)
                dve.wait_ge(rank_ps, l + 1)
                do(V.tensor_copy(rt[:, 2, :], bank[2][:, 0:80]))
                before, total = per(3, NE), per(2, NE)
                do(V.memset(before[:, 0, :], 0.0))
                for t in range(1, NT):
                    do(V.tensor_tensor(before[:, t, :], before[:, t - 1, :], total[:, t - 1, :], ALU.add))
                do(V.tensor_tensor(rt[:, 4, 0:NE], before[:, NT - 1, :], total[:, NT - 1, :], ALU.add))
                do(V.tensor_reduce(rt[:, 5, 0:1], rt[:, 4, 0:NE], AX.X, ALU.max))
                do(V.tensor_copy(over_i[:, :], rt[0:1, 5, 0:1]))
                do(V.tensor_tensor(rt[:, 3, :], rt[:, 3, :], bank[1][:, 0:80], ALU.add))
                do(V.scalar_tensor_tensor(per(3, NE), per(3, NE), float(NE),
                                          iota16[:, :].unsqueeze(1).broadcast_to([P, NT, NE]), ALU.mult, ALU.add))
                for k in range(2):
                    do(V.tensor_tensor(per(1, NE), per(3, NE), oh[:, k, :, :], ALU.mult))
                    do(V.tensor_reduce(rt[:, 6 + k, 0:NT], per(1, NE), AX.X, ALU.add))
                    last = V.tensor_copy(pos_i[:, k, :], rt[:, 6 + k, 0:NT])
                    if k == 0:
                        do(last)
                last.then_inc(pos_ready, 1)

            def experts(l):
                base = NE * l

                def x_copied(g):
                    dve.wait_ge(xg_ps, g + 1)
                    V.tensor_copy(XGT[:, 0:4, :], heads_of(4)).then_inc(xgt_ready, 1)
                    V.tensor_copy(XGT[:, 4:8, :], heads_of(5)).then_inc(xgt_ready, 1)

                def h_product(u, g):
                    dve.wait_ge(up_ps, g + 1)
                    dve.wait_ge(sg_done, g + 1)
                    at_least(dve, h_ps, g - 1)
                    V.tensor_tensor(HB[u], SG[u], bank[2 + u][:, :], ALU.mult).then_inc(h_ready, 1)

                def result(pairs, u, g):
                    dve.wait_ge(y1_ps, g + 1)
                    at_least(dve, y_stored[u], arrivals(l, pairs - 1))
                    V.tensor_copy(YO[u][:, 512:1024], bank[6][:, :]).then_inc(y1_out, 1)

                def step(i, v):
                    u, g = (1 + v) % 2, i * 2 + (base + 1 + v)
                    h_product(u, g)
                    x_copied(g + 1)
                    result(i + 1, 1 - u, g - 1)

                x_copied(base)
                h_product(0, base)
                x_copied(base + 1)
                step(0, 0)
                step(0, 1)
                with dve.Fori(1, NE // 2 - 1) as i:
                    step(i, 0)
                    step(i, 1)
                h_product(1, base + 15)
                result(8, 0, base + 14)
                result(8, 1, base + 15)
                overflow(l)

            def overflow(l):
                s = ov[l]
                dve.wait_ge(pos_ready, l + 1)
                most = dve.value_load(over_i[0:1, 0:1], min_val=0, max_val=T)
                with dve.If(most > P):
                    with dve.Fori(1, BLOCKS) as b:
                        with dve.Fori(0, NE) as e:
                            n = b * NE + e - (NE - 1)
                            ov_wait(dve, l, n, "x_ps")
                            V.tensor_copy(XGT[:, 0:4, :], heads_of(4))
                            V.tensor_copy(XGT[:, 4:8, :], heads_of(5)).then_inc(s["dve"], 1)
                            ov_wait(dve, l, n, "gu_ps")
                            ov_wait(dve, l, n, "sg")
                            V.tensor_tensor(HB[0], SG[0], bank[2][:, :], ALU.mult).then_inc(s["dve"], 1)
                            ov_wait(dve, l, n, "y_ps")
                            V.tensor_copy(YO[0][:, 512:1024], bank[6][:, :]).then_inc(s["dve"], 1)

            def mixer1():
                dve.wait_ge(lru_hist_ps, 1)
                V.tensor_copy(lhistT, bank[0][:, 0:192].rearrange("p (c j) -> p c j", c=KD)).then_inc(lru_hist_out, 1)
                dve.wait_ge(lru_hist_ps, 2)
                V.tensor_copy(lstateT, bank[1][:, 0:64].rearrange("p (c s) -> p c s", c=KD)).then_inc(lru_hist_out, 1)
                dve.wait_ge(lru_hist_ps, 3)
                V.tensor_copy(par[:, 0:64], bank[2][:, 0:64]).then_inc(lru_hist_out, 1)
                dve.wait_ge(lru_hist_out, 3)
                lam, c, nc_, tmp = par[:, 56:64], par[:, 64:72], par[:, 72:80], par[:, 80:88]
                V.scalar_tensor_tensor(tmp, lam, -1.0, lam, ALU.mult, ALU.min).then_inc(lru_par, 1)
                mine(V.tensor_scalar(c, lam, -1.0, 0.0, ALU.mult, ALU.max))
                dve.wait_ge(lru_par, 3)
                mine.settle()
                mine(V.tensor_tensor(c, c, tmp, ALU.add))
                mine.settle()
                mine(V.tensor_scalar(nc_, c, -8.0, None, ALU.mult))
                mine.settle()
                V.tensor_scalar(c, c, 8.0, None, ALU.mult).then_inc(lru_par, 1)
                for m in range(KD):
                    dve.wait_ge(proj1_out, KD + m + 1)
                    if m < 3:
                        dve.wait_ge(ext1_zeroed, 1)
                    conv(m, EXT1[m % 3], lhistT[:, m, :], XC[:, m, :], KD, par[:, 32 + m:33 + m]).then_inc(conv1_done, 1)
                for m in range(KD):
                    dve.wait_ge(lru_t, m + 1)
                    dve.wait_ge(lru_a2, m + 1)
                    V.scalar_tensor_tensor(R_[:, m, :], TMP[:, m % 2, :], 1.0, R_[:, m, :], ALU.add, ALU.mult)\
                        .then_inc(lru_w, 1)
                for m in range(KD):
                    a, bt, h = XT[:, m, :], GI[:, m, :], XC[:, m, :]
                    dve.wait_ge(lru_root, m + 1)
                    dve.wait_ge(lru_x, m + 1)
                    mine(V.tensor_tensor(bt, R_[:, m, :], bt, ALU.mult))
                    mine(V.tensor_tensor(lru_init[:, m, :], samples(a)[:, :, 0], lstateT[:, m, :], ALU.mult))
                    mine.settle()
                    mine(V.tensor_tensor(samples(bt)[:, :, 0], samples(bt)[:, :, 0], lru_init[:, m, :], ALU.add))
                    mine(V.memset(samples(a)[:, :, 0], 0.0))
                    mine.settle()
                    mine(V.tensor_tensor_scan(h, a, bt, 0.0, ALU.mult, ALU.add))
                    mine.settle()
                    V.tensor_copy(lru_last[:, m:m + 1], h[:, TP - 1:TP])
                    V.tensor_copy(lru_last[:, 8:72].rearrange("p (s c) -> p s c", s=NS)[:, :, m],
                                  samples(h)[:, :, LS - 1]).then_inc(lru_h, 1)
                dve.wait_ge(norm_done, 2 * NT)
                dve.wait_ge(st1_ps, 1)
                V.tensor_copy(rows_out[0:108, 0:256], bank[4][0:108, 0:256]).then_inc(st1_out, 1)
                dve.wait_ge(st1_ps, 2)
                V.tensor_copy(rows_out[0:72, 256:384], bank[5][0:72, 0:128]).then_inc(st1_out, 1)

            to_channels(0)
            mixer0()
            for l in range(2):
                norm(2 * l)
                to_channels(1 + 2 * l)
                route(l)
                experts(l)
                norm(2 * l + 1)
                if l == 0:
                    to_channels(2)
                    mixer1()

        @block.gpsimd
        def _(pool):
            mine = Own(pool, own["pool"])
            G = nc.gpsimd

            def do(instruction):
                mine(instruction)
                mine.settle()

            def keep_where(m, pattern, base, mult, fill=0.0, op=ALU.is_ge):
                do(G.affine_select(out=m, in_=m, compare_op=op, fill=fill, base=base, pattern=pattern,
                                   channel_multiplier=mult))

            def constants():
                for m, v in ((ident, 0.0), (ones, 1.0), (m_strict_bd, -1.0), (m_strict_off, -1.0), (m_strict_s, -1.0),
                             (m_incl, 1.0), (m_incl_s, 1.0), (m_before, 1.0), (own_sample, 1.0), (ms_col, 0.0),
                             (sel_gc, 0.0), (sel_row, 0.0), (COL, 0.0), (scores, 0.5)):
                    mine(G.memset(m[:], v))
                mine(G.memset(zero_i[:, :], 0))
                mine(G.memset(RT, 0.0))
                mine(G.memset(keep, 1.0))
                mine(G.memset(wab, 0.0))
                mine(G.memset(U[:, :, 0:HIST], 0.0))
                for buf in EXTB:
                    mine(G.memset(buf[:, 0:CONV - 1], 0.0))
                do(G.iota(tok_id[:, :], pattern=[[P, NT]], base=0, channel_multiplier=1))
                mine(G.memset(keep[:, 0:TP].rearrange("p (c l) -> p c l", l=P)[:, :, 0], 0.0))
                mine(G.memset(keep[:, TP:T].rearrange("p (c l) -> p c l", l=LS)[:, :, 0], 0.0))
                keep_where(ident[:, :], [[-1, P]], 0, 1, 1.0, ALU.not_equal)
                keep_where(m_strict_bd[:, :], [[-1, P]], -1, 1)
                keep_where(m_strict_bd[:, :].rearrange("p (b c) -> p b c", b=2), [[-64, 2], [0, 64]], 0, 1)
                keep_where(m_strict_bd[:, :].rearrange("p (b c) -> p b c", b=2), [[64, 2], [0, 64]], 63, -1)
                keep_where(m_strict_off[:, :], [[0, P]], -64, 1)
                keep_where(m_strict_off[:, :], [[-1, P]], 63, 0)
                by_sample = m_strict_s[:, :].rearrange("p (s l) -> p s l", s=NS)
                keep_where(m_strict_s[:, :], [[-1, TS]], -1, 1)
                keep_where(by_sample, [[-LS, NS], [0, LS]], 0, 1)
                keep_where(by_sample, [[LS, NS], [0, LS]], LS - 1, -1)
                by_sample = m_incl_s[:, :].rearrange("p (s l) -> p s l", s=NS)
                keep_where(m_incl[:, :], [[1, P]], 0, -1)
                keep_where(m_incl_s[:, :], [[1, TS]], 0, -1)
                keep_where(by_sample, [[-LS, NS], [0, LS]], 0, 1)
                keep_where(by_sample, [[LS, NS], [0, LS]], LS - 1, -1)
                keep_where(m_before[:, :], [[1, P]], -1, -1)
                keep_where(own_sample[:, :], [[-LS, NS]], 0, 1)
                keep_where(own_sample[:, :], [[LS, NS]], LS - 1, -1)
                keep_where(sel_gc[:, :, :], [[-1, NH], [0, P]], -32, 1, 1.0, ALU.not_equal)
                keep_where(sel_row[:, :, :], [[-1, NH], [0, P]], 0, 1, 1.0, ALU.not_equal)
                keep_where(ms_col[:, :, :], [[1, NH], [-1, NH]], 0, 0, 1.0 / P, ALU.not_equal)
                do(G.iota(iota_i[:, :], pattern=[[1, NE]], base=0, channel_multiplier=0))
                do(G.tensor_copy(iota16[:, :], iota_i[:, :]))
                do(G.iota(iota_i[:, :], pattern=[[1, 16]], base=1, channel_multiplier=0))
                G.tensor_copy(inv_cnt[:, :], iota_i[:, :]).then_inc(consts_ready, 1)

            def tail(ready, n, buf, to, c, done):
                pool.wait_ge(ready, n)
                G.tensor_copy(to[:, 0:3, c], buf[:, TP:TP + 3])
                G.tensor_copy(to[:, 3:27, c].rearrange("p (s j) -> p s j", s=NS), ext_samples(buf)[:, :, LS:LS + 3])\
                    .then_inc(done, 1)

            def spread(mask, n):
                return mask[0:n, 0:n].unsqueeze(1).broadcast_to([n, NH, n])

            def delta(st, b, n, dv, ac, pe_, i, strict, incl, off):
                cols = tile_cols(b)
                cut = lambda x: x[0:n, :, 0:n]
                dv.wait(pool, i, "dif")
                st.end(G.tensor_scalar(cut(dmx), cut(dif), 0.0, None, ALU.max), i, "max")
                st.end(G.tensor_scalar(cut(dmn), cut(dif), 0.0, None, ALU.min), i, "min")
                ac.wait(pool, i, "dbd")
                st.end(G.tensor_tensor(cut(Dbd), cut(dmx), spread(strict, n), ALU.mult), i, "bd")
                if off is not None:
                    st.end(G.tensor_tensor(cut(Doff), cut(dmx), spread(off, n), ALU.mult), i, "off")
                ac.wait(pool, i, "dt")
                st.end(G.tensor_tensor(cut(DTm), cut(dmn), spread(incl, n), ALU.mult), i, "incl")
                ac.wait(pool, i, "eg")
                pe_.wait(pool, i, "qk")
                st.end(G.tensor_tensor(QKV[:, 0:4, cols], QKV[:, 0:4, cols], egB[:, :, 0:n], ALU.mult), i, "qd")

            def mixer0():
                for n, src in enumerate((a_dt_bias, a_log_decay)):
                    pool.dma_start(gpar[32:36, n:n + 1], src.rearrange("o h -> h o")).then_inc(gates_in, 16)
                for c in range(NCHUNK):
                    tail(proj_out, c + 1, EXTB[c % 3], tails, c, tail_done)
                pool.wait_ge(conv_done, NCHUNK)
                for g in range(NH):
                    pool.wait_ge(proj_out, NCHUNK + g + 1)
                    if g:
                        pool.wait_ge(pooled_done, g)
                    src = U[:, g, :]
                    for k in range(g + 1):
                        sh, lo = 1 << k, (2 << k) - 1
                        last = G.tensor_tensor(PT_[:, k % 2, lo:UE], src[:, lo:UE], src[:, lo - sh:UE - sh], ALU.add)
                        if k < g:
                            do(last)
                        src = PT_[:, k % 2, :]
                    last.then_inc(psum_done, 1)
                pool.wait_ge(ssq_ps, 8)
                for g in range(NH):
                    last = G.tensor_copy(utail[:, g, :].rearrange("p (s l) -> p s l", s=NS),
                                         U[:, g, UEP:UE].rearrange("p (s l) -> p s l", s=NS)[:, :, LS:LS + HIST])
                last.then_inc(utail_done, 1)
                pool.wait_ge(roots_done, 2)
                for h in range(NH):
                    G.tensor_tensor(QKV[:, 4 + h, :], QKV[:, 4 + h, :], INV[:, 4 + h, :], ALU.mult).then_inc(k_scaled, 1)
                pool.wait_ge(silu_done, NCHUNK)
                pool.wait_ge(strow_out, 1)
                G.memset(SP_, 0.0).then_inc(s_zeroed, 1)
                for b in range(NT - 1):
                    delta(d_pool, b, P, d_dve, d_act, d_pe, b, m_strict_bd, m_incl, m_strict_off)
                delta(e_pool, NT - 1, TS, e_dve, e_act, e_pe, 0, m_strict_s, m_incl_s, None)
                e_dve.wait(pool, 0, "un")
                for h in range(NH):
                    if h:
                        e_pe.wait(pool, 0, f"sn{h - 1}")
                    e_pool.end(G.tensor_tensor(UB[0:TS, :, :], un[0:TS, h, :].unsqueeze(1).broadcast_to([TS, NS, P]),
                                               own_sample[:, :].unsqueeze(2).broadcast_to([TS, NS, P]), ALU.mult),
                               0, f"ub{h}")
                for h in range(NH):
                    pool.wait_ge(rmsb_out, h + 1)
                    G.tensor_tensor(XT[:, h, :], XT[:, h, :], Z[:, h, :], ALU.mult).then_inc(mix_a, 1)

            def norm(q):
                l = q // 2

                def select(t, rows):
                    u, r = t % 2, ROWS[t]
                    if t >= 2:
                        pool.wait_ge(norm_sum, q * NT + t - 1)
                    for k, to in enumerate((Y1, Y2)):
                        pool.indirect_dma_start(
                            out=to[u][0:r, :], out_offset=None, in_=rows,
                            in_offset=bass.IndirectOffsetOnAxis(ap=pos_i[0:r, k, t:t + 1], axis=0),
                        ).then_inc(ysel_in[u], 16)

                def tiles(rows):
                    if rows is not None:
                        select(0, rows)
                        select(1, rows)
                    for t in range(NT):
                        r = ROWS[t]
                        pool.wait_ge(norm_scaled, q * NT + t + 1)
                        G.tensor_tensor(X[0:r, t, :], X[0:r, t, :], LNP[0:r, q % 2, 0, :], ALU.mult)\
                            .then_inc(gained, 1)
                        pool.wait_ge(gained, q * NT + t + 1)
                        G.tensor_tensor(X[0:r, t, :], X[0:r, t, :], LNP[0:r, q % 2, 1, :], ALU.add)\
                            .then_inc(norm_done, 1)
                        if rows is not None and t + 2 < NT:
                            select(t + 2, rows)

                pool.wait_ge(lnp_in[q % 2], 32 * (l + 1))
                if q % 2 == 0:
                    tiles(None)
                else:
                    for u in range(2):
                        pool.wait_ge(y_stored[u], arrivals(l, 8))
                    with pool.If(most_tokens() > P):
                        overflow(l)
                        tiles(y_rows[l])
                    with pool.Else():
                        tiles(y_rows[l][0:P * NE, :])

            def experts(l):
                base = NE * l

                def gather(u, g, e):
                    at_least(pool, xg_ps, g - 1)
                    G.tensor_copy(idx_cur[:, u:u + 1], idx_all[:, 0, bass.ds(e, 1)])
                    pool.drain()
                    pool.indirect_dma_start(
                        out=XG[u], out_offset=None, in_=x_rows[l],
                        in_offset=bass.IndirectOffsetOnAxis(ap=idx_cur[:, u:u + 1], axis=0)).then_inc(xg_in[u], 16)

                pool.wait_ge(lists_zeroed, 32)
                pool.wait_ge(pos_ready, l + 1)
                for t in range(NT):
                    for k in range(2):
                        pool.indirect_dma_start(
                            out=slot_list[l], in_=tok_id[0:ROWS[t], t:t + 1], in_offset=None,
                            out_offset=bass.IndirectOffsetOnAxis(ap=pos_i[0:ROWS[t], k, t:t + 1], axis=0),
                        ).then_inc(tok_scattered, 16)
                pool.wait_ge(state_out, 16 * 8)
                pool.wait_ge(idx_in, 16 * (l + 1))
                pool.wait_ge(xrows_out, 16 * NT * (l + 1))
                gather(0, base, 0)
                gather(1, base + 1, 1)
                with pool.Fori(1, NE // 2) as i:
                    for u in range(2):
                        gather(u, i * 2 + (base + u), i * 2 + u)

            def most_tokens():
                return pool.value_load(over_i[0:1, 0:1], min_val=0, max_val=T)

            def overflow(l):
                s = ov[l]
                with pool.Fori(1, BLOCKS) as b:
                    with pool.Fori(0, NE) as e:
                        n = b * NE + e - (NE - 1)
                        ov_buffers_free(pool, l, n)
                        G.tensor_copy(idx_cur[:, 0:1], idx_all[:, bass.ds(b, 1), bass.ds(e, 1)]
                                      .rearrange("p b e -> p (b e)"))
                        pool.drain()
                        pool.indirect_dma_start(
                            out=XG[0], out_offset=None, in_=x_rows[l],
                            in_offset=bass.IndirectOffsetOnAxis(ap=idx_cur[:, 0:1], axis=0)).then_inc(s["xg"], 16)
                ov_wait(pool, l, NE * (BLOCKS - 1), "stored")

            def mixer1():
                for buf in EXT1:
                    last = G.memset(buf[:, 0:CONV - 1], 0.0)
                last.then_inc(ext1_zeroed, 1)
                for m in range(KD):
                    tail(proj1_out, KD + m + 1, EXT1[m % 3], tails1, m, tail1_done)
                pool.wait_ge(lru_gates_done, 16)
                pool.wait_ge(conv1_done, KD)
                for m in range(KD):
                    pool.wait_ge(lru_a, m + 1)
                    if m >= 2:
                        pool.wait_ge(lru_w, m - 1)
                    G.tensor_tensor(TMP[:, m % 2, :], XT[:, m, :], XT[:, m, :], ALU.mult).then_inc(lru_a2, 1)
                    G.tensor_tensor(GI[:, m, :], GI[:, m, :], XC[:, m, :], ALU.mult).then_inc(lru_x, 1)
                for m in range(KD):
                    pool.wait_ge(lru_h, m + 1)
                    G.tensor_tensor(XT[:, m, :], XC[:, m, :], YB[:, m, :], ALU.mult).then_inc(mix_a, 1)

            constants()
            mixer0()
            for l in range(2):
                norm(2 * l)
                experts(l)
                norm(2 * l + 1)
                if l == 0:
                    mixer1()


_INS = ['x_prompt', 'x_sample', 'state_delta', 'state_delta_conv', 'state_pool', 'state_lru', 'state_lru_conv',
        'ab_w_in', 'a_conv_w', 'a_log_decay', 'a_dt_bias', 'a_norm_w', 'b_w_group', 'b_scale', 'ab_w_out',
        'c_w_in', 'c_conv_w', 'c_conv_b', 'c_w_r', 'c_b_r', 'c_w_i', 'c_b_i', 'c_lambda', 'c_w_out',
        'ln_mix_g', 'ln_mix_b', 'ln_ffn_g', 'ln_ffn_b', 'router_w', 'router_bias',
        'moe_w_gate', 'moe_w_up', 'moe_w_down']
_OUTS = [(1, 512, 1024), (8, 8, 1024), (1, 1, 4, 128, 128), (1, 1, 3, 1536), (1, 1, 15, 512), (1, 1, 1024),
         (1, 1, 3, 1024), (1, 8, 4, 128, 128), (1, 8, 3, 1536), (1, 8, 15, 512), (1, 8, 1024), (1, 8, 3, 1024)]


def kernel(**inputs):
    import numpy as _np
    import concourse.bacc as _bacc
    from concourse import mybir as _mybir
    from concourse.bass_utils import run_bass_kernel_spmd as _run

    nc = _bacc.Bacc("TRN2", target_bir_lowering=False, num_devices=1)
    arrays, args = {}, []
    for name in _INS:
        a = _np.ascontiguousarray(inputs[name])
        arrays[f"in_{name}_dram"] = a
        args.append(nc.dram_tensor(f"in_{name}_dram", a.shape, _mybir.dt.from_np(a.dtype), kind="ExternalInput").ap())
    for i, shape in enumerate(_OUTS):
        args.append(nc.dram_tensor(f"out_{i}_dram", shape, _mybir.dt.float32, kind="ExternalOutput").ap())
    hybrid_trunk(nc, *args)
    r = _run(nc, [arrays], core_ids=[0])
    return tuple(r.results[0][f"out_{i}_dram"] for i in range(len(_OUTS)))
```

```python
import concourse.bass as bass
from concourse import mybir

F32 = mybir.dt.float32
I32 = mybir.dt.int32
F32R = mybir.dt.float32r
ALU = mybir.AluOpType
ACT = mybir.ActivationFunctionType
AX = mybir.AxisListType

P = 128
D = 1024
KD = D // P
TP, NS, LS = 512, 8, 8
TS = NS * LS
T = TP + TS
TH = T // 2
NT = 5
ROWS = [P] * (TP // P) + [TS]
NCHUNK = 12
NH = 4
HIST = 15
CONV = 4
NPROJ = 20
FF = 512
NE = 16
BLOCKS = NT
SLOTS = BLOCKS * P * NE
WINDOWS = (2, 4, 8, 16)
ALPHA = 4.0 ** 0.25
LN_EPS, RMS_EPS, L2_EPS = 1e-5, 1e-6, 1e-6
EXT_P, EXT_S = CONV - 1 + TP, CONV - 1 + LS
EXT = EXT_P + NS * EXT_S
UEP, UES = HIST + TP, HIST + LS
UE = UEP + NS * UES
WORK = 35340


class Steps:

    def __init__(self, sem, names, rounds=1, ahead=()):
        self.sem, self.made = sem, 0
        order = [(0, name) for name in names if name in ahead]
        for n in range(rounds):
            order += [(n + 1 if name in ahead else n, name) for name in names if name not in ahead or n + 1 < rounds]
        self.count = {step: i + 1 for i, step in enumerate(order)}

    def at(self, n, name):
        return self.count[n, name]

    def end(self, instruction, n, name):
        self.made += 1
        assert self.made == self.at(n, name), (self.made, n, name)
        return instruction.then_inc(self.sem, 1)

    def wait(self, engine, n, name):
        engine.wait_ge(self.sem, self.at(n, name))


def hybrid_trunk(nc, x_prompt, x_sample, state_delta, state_delta_conv, state_pool, state_lru, state_lru_conv,
                 ab_w_in, a_conv_w, a_log_decay, a_dt_bias, a_norm_w, b_w_group, b_scale, ab_w_out,
                 c_w_in, c_conv_w, c_conv_b, c_w_r, c_b_r, c_w_i, c_b_i, c_lambda, c_w_out,
                 ln_mix_g, ln_mix_b, ln_ffn_g, ln_ffn_b, router_w, router_bias,
                 moe_w_gate, moe_w_up, moe_w_down,
                 y_prompt, y_sample, p_delta, p_dconv, p_pool, p_lru, p_lconv,
                 s_delta, s_dconv, s_pool, s_lru, s_lconv):
    from contextlib import ExitStack
    ctx = ExitStack()
    with ctx:
        def sb(name, shape, dt=F32):
            return ctx.enter_context(nc.sbuf_tensor(name, shape, dt))

        def sem(name):
            return ctx.enter_context(nc.semaphore(name))

        def steps(name, names, rounds=1, ahead=()):
            return Steps(sem(name), names, rounds, ahead)

        x_rows = [nc.dram_tensor(f"x_rows{l}", [T, D], F32).ap() for l in range(2)]
        slot_list = [nc.dram_tensor(f"slot_list{l}", [SLOTS, 1], I32).ap() for l in range(2)]
        y_rows = [nc.dram_tensor(f"y_rows{l}", [SLOTS, D], F32).ap() for l in range(2)]

        def next_address():
            return -(-nc.sbuf_base // 32) * 32

        X = sb("X", [P, NT, D])
        XT_AT = next_address()
        XT = sb("XT", [P, KD, T])
        LNP = sb("LNP", [P, 2, 2, D])
        WORK_AT = next_address()
        work = sb("work", [P, WORK])
        ident = sb("ident", [P, P])
        ones = sb("ones", [P, P])
        m_strict_bd = sb("m_strict_bd", [P, P])
        m_strict_off = sb("m_strict_off", [P, P])
        m_strict_s = sb("m_strict_s", [TS, TS])
        m_incl = sb("m_incl", [P, P])
        m_incl_s = sb("m_incl_s", [TS, TS])
        m_before = sb("m_before", [P, P])
        sel_gc = sb("sel_gc", [68, NH, P])
        sel_row = sb("sel_row", [NH, NH, P])
        own_sample = sb("own_sample", [TS, NS])
        ms_col = sb("ms_col", [P, NH, NH])
        inv_cnt = sb("inv_cnt", [P, 16])
        iota16 = sb("iota16", [P, NE])
        m_lower4 = sb("m_lower4", [P, 4, 4])
        tok_id = sb("tok_id", [P, NT], I32)
        zero_i = sb("zero_i", [P, SLOTS // P], I32)
        rw = sb("rw", [P, KD, NE])
        rbias = sb("rbias", [P, NE])
        par = sb("par", [P, 88])
        COL = sb("COL", [P, NT, 68])
        ecol = sb("ecol", [P, NT, NH])
        kdc = sb("kdc", [P, NT, NH])
        kbgc = sb("kbgc", [P, NT, NH])
        egl = sb("egl", [P, NH, 12])
        lnw = sb("lnw", [P, NT, 16])
        scores = sb("scores", [P, NT, NE])
        wsel = sb("wsel", [P, 4, NT])
        pos_i = sb("pos_i", [P, 2, NT], I32)
        idx_all = sb("idx_all", [P, BLOCKS, NE], I32)
        gpar = sb("gpar", [36, 2])
        iota_i = sb("iota_i", [P, 16], I32)
        idx_cur = sb("idx_cur", [P, 2], I32)
        over_i = sb("over_i", [1, 1], I32)

        bank = [ctx.enter_context(nc.psum_tensor(f"bank{i}", [P, 512], F32)) for i in range(8)]

        def heads_of(b, n=P, m=P):
            return bank[b][:, :].rearrange("p (h c) -> p h c", h=4)[0:n, :, 0:m]

        def view(off, shape):
            n = 1
            for s in shape:
                n *= s
            v = work[:, off:off + n]
            if len(shape) == 2:
                v = v.rearrange("p (a b) -> p a b", a=shape[0])
            elif len(shape) == 3:
                v = v.rearrange("p (a b c) -> p a b c", a=shape[0], b=shape[1])
            return v

        W0 = [view(2048 * s, (KD, 256)) for s in range(4)]
        QKV = view(8192, (NCHUNK, T))
        Z = view(15104, (NH, T))
        U = view(17408, (NH, UE))
        gB = view(20252, (NH, T))
        INV = view(22556, (8, T))
        SS = view(22556, (NS * NH, P))
        chist_rows = work[:, 22556:22556 + 1536]
        phist_rows = work[:, 24092:24092 + 512]
        par_rows = work[:, 24604:24604 + P]
        wab_in = view(24732, (KD, 8))
        wab = view(24796, (KD, 68))
        EXTB = [work[:, 27164 + EXT * s:27164 + EXT * (s + 1)] for s in range(3)]
        CV = view(28973, (2, T))
        SQ = view(30125, (2, T))
        PT_ = view(31277, (2, UE))
        POOLED = view(32699, (NH, T))
        chistT = view(31277, (NCHUNK, 24))
        RT, RA, RB, keep = (work[:, 15104 + T * i:15104 + T * i + T] for i in range(4))
        slot = [view(512 * s, (NH, P)) for s in range(16)] + \
               [view(27164 + 512 * s, (NH, P)) for s in range(8)]
        kbg0, kd0, vb0, Pa, Pb, PTa, PTb, aT0, TT, Noff0, TB, Yo, nwT, un = slot[0:14]
        after_u = [view(17408 + 512 * s, (NH, P)) for s in range(4)]
        kbg, kd, vb, aT, Noff = ((kbg0, after_u[0]), (kd0, after_u[1]), (vb0, after_u[2]), (aT0, after_u[3]),
                                 (Noff0, slot[14]))
        dif, dmx, Dbd, egB, _, SP_ = slot[16:22]
        dmn, DTm, Doff = dif, dif, dmx
        UB = [view(27164 + 512 * 6, (NS, P)), view(512 * 3, (NS, P))]
        WG = view(26652, (NH, P))
        WO_HEADS, WO_U, WO_SUMS, WO_RING = view(0, (NH, D)), view(17408, (2, D)), view(31277, (1, D)), view(7168, (1, D))
        WO_A = [WO_HEADS[:, k, :] for k in range(NH)] + [WO_U[:, 0, :], WO_U[:, 1, :], WO_SUMS[:, 0, :], WO_RING[:, 0, :]]
        WO1 = view(0, (KD, D))
        WO_B = [WO1[:, k, :] for k in range(KD)]
        tails = view(35003, (27, NCHUNK))
        utail = view(30125, (NH, NS * HIST))
        rows_out = LNP[:, 1, :, :].rearrange("p n d -> p (n d)")
        W1 = W0
        WRI = view(8192, (2, 8, 256))
        YB = view(12288, (KD, T))
        XC = view(16896, (KD, T))
        R_ = view(21504, (KD, T))
        GI = view(26112, (KD, T))
        EXT1 = [work[:, 30720 + EXT * s:30720 + EXT * (s + 1)] for s in range(3)]
        TMP = view(32529, (2, T))
        lhistT = view(33681, (KD, 24))
        lstateT = view(33873, (KD, NS))
        lhist_rows = work[:, 26112:26112 + D]
        lstate_rows = work[:, 27136:27136 + D]
        par_rows1 = work[:, 28160:28160 + P]
        tails1 = view(34073, (27, KD))
        lru_last = work[:, 33937:33937 + 72]
        lru_init = work[:, 34009:34009 + 64].rearrange("p (c s) -> p c s", c=KD)
        WGT = [view(8192 + 4096 * s, (KD, FF)) for s in range(2)]
        WUP = [view(16384 + 4096 * s, (KD, FF)) for s in range(2)]
        WDN = [view(4096 * s, (FF // P, D)) for s in range(2)]
        XG = [work[:, 24576 + D * s:24576 + D * (s + 1)] for s in range(2)]
        XGT = view(26624, (KD, P))
        SG = [work[:, 27648 + FF * s:27648 + FF * (s + 1)] for s in range(2)]
        HB = [work[:, 28672 + FF * s:28672 + FF * (s + 1)] for s in range(2)]
        HT = view(29696, (FF // P, P))
        def placed(name, at, off, shape):
            return nc.alloc_sbuf_tensor_at(name, [P, *shape], F32R, offset=at + 4 * off)

        HT_HIGH, HT_LOW = placed("HT_HIGH", WORK_AT, 32256, (FF // P, P)), placed("HT_LOW", WORK_AT, 29696, (FF // P, P))
        WDN_HIGH = placed("WDN_HIGH", XT_AT, 0, (FF // P, D))
        WDN_LOW = [placed(f"WDN_LOW{s}", WORK_AT, 4096 * s, (FF // P, D)) for s in range(2)]
        XT_HIGH, XT_LOW = (placed(name, WORK_AT, off, (KD, T)) for name, off in (("XT_HIGH", 21504), ("XT_LOW", 26112)))
        W1_HIGH = [placed(f"W1_HIGH{s}", WORK_AT, off, (KD, P)) for s, off in enumerate((32536, 34296))]
        W1_LOW = [placed(f"W1_LOW{s}", WORK_AT, 2048 * s, (KD, 256)) for s in range(4)]
        YO = [work[:, 30208 + D * s:30208 + D * (s + 1)] for s in range(2)]
        rt = view(30208, (12, NT * NE))
        oh = view(31168, (2, NT * NE)).rearrange("p k (t e) -> p k t e", t=NT)
        pairs_of4 = [view(31328 + 16 * 4 * NT * i, (4 * NT, 4, 4)) for i in range(2)]
        Y1, Y2 = ([work[:, 12288 + D * (2 * t + k):13312 + D * (2 * t + k)] for t in range(NT)]
                  for k in range(2))
        own = {e: sem(f"{e}_own") for e in ("dve", "pool")}

        class Own:

            def __init__(self, engine, s):
                self.engine, self.s, self.n = engine, s, 0

            def __call__(self, instruction):
                self.n += 1
                return instruction.then_inc(self.s, 1)

            def settle(self):
                self.engine.wait_ge(self.s, self.n)

        x_in, hist_in, gates_in, wab_sem = sem("x_in"), sem("hist_in"), sem("gates_in"), sem("wab_in_s")
        w_in = [sem(f"w_in{s}") for s in range(4)]
        w1_in = [sem(f"w1_in{s}") for s in range(4)]
        lnp_in = [sem(f"lnp_in{s}") for s in range(2)]
        router_in, lists_zeroed = sem("router_in"), sem("lists_zeroed")
        ss_in, wg_in, wo_in, wri_in, hist1_in = sem("ss_in"), sem("wg_in"), sem("wo_in"), sem("wri_in"), sem("hist1_in")
        wo_early_in = sem("wo_early_in")
        state_out, y_out = sem("state_out"), sem("y_out")
        xrows_out, tok_scattered, idx_in = sem("xrows_out"), sem("tok_scattered"), sem("idx_in")
        consts_ready = sem("consts_ready")
        xt_ps, xt_lo, xt_hi = sem("xt_ps"), sem("xt_lo"), sem("xt_hi")
        hist_ps, hist_out, ab_ps, rows_ready = sem("hist_ps"), sem("hist_out"), sem("ab_ps"), sem("rows_ready")
        wab_ready, gate_act, gate_dve = sem("wab_ready"), sem("gate_act"), sem("gate_dve")
        proj_ps, proj_out, conv_done, silu_done = sem("proj_ps"), sem("proj_out"), sem("conv_done"), sem("silu_done")
        sq_done, ssq_ps, inv_done, tail_done = sem("sq_done"), sem("ssq_ps"), sem("inv_done"), sem("tail_done")
        gcb_ps, gcb_out, col_ps, col_out, egl_done = sem("gcb_ps"), sem("gcb_out"), sem("col_ps"), sem("col_out"), sem("egl_done")
        roots_done, q_scaled, k_scaled = sem("roots_done"), sem("q_scaled"), sem("k_scaled")
        psum_done, pooled_done = sem("pool_sum_done"), sem("pooled_done")
        gained = sem("gained")
        utail_done = sem("utail_done")
        strow_ps, strow_out = sem("strow_ps"), sem("strow_out")
        front = ("ktr", "vtr", "gram", "qk")
        d_pe = steps("delta_pe", ["p1", "pt1", "x1", "p2", "pt2", "x2", *front, "p3", "pt3", "x3", "p4", "pt4", "x4",
                                  "p5", "x5", "tb", "y", "x6", "nw", "pt", "un", "o", "sn"], NT - 1, (*front, "pt"))
        d_dve = steps("delta_dve", ["tt0", "p1", "dif", "tt1", "p2", "tt2", "p3", "kbg", "kd", "tt3", "p4", "off", "a",
                                    "tt4", "p5", "tt5", "y", "tt6", "p0", "un", "s"],
                      NT - 1, ("dif", "kbg", "kd", "off", "a", "p0"))
        d_act = steps("delta_act", ["pt0", "pt1", "dbd", "dt", "pt2", "eg", "pt3", "vb", "pt4", "tb", "nw", "o"],
                      NT - 1, ("dbd", "dt", "eg", "vb"))
        d_pool = steps("delta_pool", ["qd", "max", "min", "bd", "off", "incl"], NT - 1,
                       ("max", "min", "bd", "off", "incl"))
        e_pe = steps("sample_pe", ["ktr", "vtr", "gram", "qk", "pt", "p1", "pt1", "x1", "p2", "x2", "nw", "ut", "un",
                                   "o"] + [f"sn{h}" for h in range(NH)])
        e_dve = steps("sample_dve", ["dif", "kbg", "kd", "a", "p0", "tt0", "p1", "tt1", "p2", "tt2", "un", "o"] +
                      [f"s{h}" for h in range(NH)])
        e_act = steps("sample_act", ["dbd", "dt", "eg", "vb", "pt0", "pt1", "nw", "ut"])
        e_pool = steps("sample_pool", ["max", "min", "bd", "incl", "qd"] + [f"ub{h}" for h in range(NH)])
        s_zeroed = sem("s_zeroed")
        rms_sq, rms_ps, rms_eps, rms_root, rms_inv = sem("rms_sq"), sem("rms_ps"), sem("rms_eps"), sem("rms_root"), sem("rms_inv")
        rmsb_ps, rmsb_out, mix_a, group_ps, mix_b = sem("rmsb_ps"), sem("rmsb_out"), sem("mix_a"), sem("group_ps"), sem("mix_b")
        out_ps = sem("out_ps")
        norm_sum, norm_stats, norm_coef = sem("norm_sum"), sem("norm_stats"), sem("norm_coef")
        norm_root, norm_scaled, norm_done = sem("norm_root"), sem("norm_scaled"), sem("norm_done")
        logits_ps, scores_done, onehot_ready, rank_ps, pos_ready = \
            sem("logits_ps"), sem("scores_done"), sem("onehot_ready"), sem("rank_ps"), sem("pos_ready")
        gate_in, up_in, down_in, xg_in, y_stored = (
            [sem(f"{n}{u}") for u in range(2)] for n in ("gate_in", "up_in", "down_in", "xg_in", "y_stored"))
        ysel_in = [sem(f"ysel_in{t}") for t in range(NT)]
        xg_ps, xgt_ready, gate_ps, up_ps, sg_done, h_ready = \
            sem("xg_ps"), sem("xgt_ready"), sem("gate_ps"), sem("up_ps"), sem("sg_done"), sem("h_ready")
        h_ps, ht_ready, y1_ps, y0_ps, y1_out, y0_out = \
            sem("h_ps"), sem("ht_ready"), sem("y1_ps"), sem("y0_ps"), sem("y1_out"), sem("y0_out")
        ysel_scaled, down_split = sem("ysel_scaled"), sem("down_split")
        down_rounded = sem("down_rounded")
        operands = ["w0"] + [f"x{t}" for t in range(NT)] + [f"w{c}" for c in range(1, 16)]
        rounded1, split1 = steps("rounded1", operands), steps("split1", operands)
        OV = {"x_ps": ("pe", 4, 1), "gu_ps": ("pe", 4, 2), "h_ps": ("pe", 4, 3), "y_ps": ("pe", 4, 4),
              "sg": ("act", 3, 1), "ht": ("act", 3, 2), "y_a": ("act", 3, 3),
              "xgt": ("dve", 3, 1), "h": ("dve", 3, 2), "y_d": ("dve", 3, 3),
              "w": ("w", 48, 48), "xg": ("xg", 16, 16), "stored": ("stored", 16, 16)}
        ov = [{n: sem(f"ov{l}_{n}") for n in ("pe", "act", "dve", "w", "xg", "stored")} for l in range(2)]

        def ov_wait(engine, l, n, part):
            who, per_step, at = OV[part]
            start = 4 if who == "pe" else 0
            engine.wait_ge(ov[l][who], n * per_step + (at - per_step + start))

        def ov_buffers_free(engine, l, n):
            engine.wait_ge(ov[l]["pe"], n * 4)

        lru_gate_ps, lru_gates_done = sem("lru_gate_ps"), sem("lru_gates_done")
        lru_hist_ps, lru_hist_out, lru_par = sem("lru_hist_ps"), sem("lru_hist_out"), sem("lru_par")
        proj1_ps, proj1_out, conv1_done, tail1_done = sem("proj1_ps"), sem("proj1_out"), sem("conv1_done"), sem("tail1_done")
        lru_a, lru_a2, lru_t, lru_w, lru_root, lru_x, lru_h, ext1_zeroed = (
            sem(f"lru_{n}") for n in ("a", "a2", "t", "w", "root", "x", "h", "ext_zeroed"))
        st1_ps, st1_out = sem("st1_ps"), sem("st1_out")

        def tile_cols(t):
            return slice(P * t, P * t + ROWS[t])

        def bc(ap, shape):
            return ap.broadcast_to(shape)

        def xrow_dram(t, prompt, sample):
            return prompt[0, P * t:P * t + P, :] if t < TP // P else sample.rearrange("s l d -> (s l) d")

        ext_prompt = slice(CONV - 1, EXT_P)

        def ext_samples(buf):
            return buf[:, EXT_P:EXT].rearrange("p (s l) -> p s l", s=NS)

        def samples(ap):
            return ap[:, TP:T].rearrange("p (s l) -> p s l", s=NS)

        def at_least(engine, s, value):
            if not isinstance(value, int) or value > 0:
                engine.wait_ge(s, value)

        def arrivals(l, pairs):
            return pairs * 16 + P * l if not isinstance(pairs, int) else 16 * pairs + P * l

        block = ctx.enter_context(nc.Block())
        TILE_BANK = lambda t: 4 + 2 * (t % 2)

        @block.sync
        def _(sp):
            def lnp(slot_, l, gains, biases):
                for n, src in enumerate((gains, biases)):
                    sp.dma_start(LNP[:, slot_, n, :], src[l, :].partition_broadcast(P)).then_inc(lnp_in[slot_], 16)

            def gate(l, e, u):
                sp.dma_start(WGT[u], moe_w_gate[l, e].rearrange("(k p) f -> p k f", p=P)).then_inc(gate_in[u], 16)

            def up(l, e, u):
                sp.dma_start(WUP[u], moe_w_up[l, e].rearrange("(k p) f -> p k f", p=P)).then_inc(up_in[u], 16)

            def down(l, e, u):
                sp.dma_start(WDN[u], moe_w_down[l, e].rearrange("(k p) d -> p k d", p=P)).then_inc(down_in[u], 16)

            def store_rows(l, q, t):
                sp.wait_ge(norm_done, q * NT + t + 1)
                sp.dma_start(x_rows[l][P * t:P * t + ROWS[t], :], X[0:ROWS[t], t, :]).then_inc(xrows_out, 16)

            def experts(l):
                sp.wait_ge(mix_a, NH + KD * l)
                sp.wait_ge(mix_b, NH)
                for u in range(2):
                    gate(l, u, u)
                for t in range(NT - 1):
                    store_rows(l, 2 * l, t)
                sp.wait_ge(out_ps, NT * (l + 1))
                up(l, 0, 0)
                store_rows(l, 2 * l, NT - 1)
                down(l, 0, 0)
                up(l, 1, 1)
                down(l, 1, 1)
                sp.wait_ge(tok_scattered, 160 * (l + 1))
                sp.dma_start(idx_all[:, :, :], slot_list[l].rearrange("(b s e) o -> s b (e o)", b=BLOCKS, s=P))\
                  .then_inc(idx_in, 16)
                base = NE * l
                with sp.Fori(0, NE // 2 - 1) as i:
                    for u in range(2):
                        sp.wait_ge(gate_ps, i * 2 + (base + u + 1))
                        sp.dma_start(WGT[u], moe_w_gate[l, bass.ds(i * 2 + (2 + u), 1)]
                                     .rearrange("o (k p) f -> p (o k) f", p=P)).then_inc(gate_in[u], 16)
                        sp.wait_ge(up_ps, i * 2 + (base + u + 1))
                        sp.dma_start(WUP[u], moe_w_up[l, bass.ds(i * 2 + (2 + u), 1)]
                                     .rearrange("o (k p) f -> p (o k) f", p=P)).then_inc(up_in[u], 16)
                        sp.wait_ge(y0_ps, i * 2 + (base + u + 1))
                        sp.dma_start(WDN[u], moe_w_down[l, bass.ds(i * 2 + (2 + u), 1)]
                                     .rearrange("o (k p) d -> p (o k) d", p=P)).then_inc(down_in[u], 16)
                sp.wait_ge(y0_ps, base + NE)
                overflow(l)

            def overflow(l):
                s = ov[l]
                sp.wait_ge(pos_ready, l + 1)
                most = sp.value_load(over_i[0:1, 0:1], min_val=0, max_val=T)
                with sp.If(most > P):
                    with sp.Fori(1, BLOCKS) as b:
                        with sp.Fori(0, NE) as e:
                            ov_buffers_free(sp, l, b * NE + e - (NE - 1))
                            for buf, w in ((WGT, moe_w_gate), (WUP, moe_w_up), (WDN, moe_w_down)):
                                sp.dma_start(buf[0], w[l, bass.ds(e, 1)].rearrange("o (k p) f -> p (o k) f", p=P))\
                                  .then_inc(s["w"], 16)
                    ov_buffers_free(sp, l, (BLOCKS - 1) * NE + 1)

            def mixer1():
                sp.wait_ge(ysel_in[3], 32)
                lnp(0, 1, ln_mix_g, ln_mix_b)
                sp.dma_start(lhist_rows[0:24, :], state_lru_conv[0].rearrange("s j c -> (s j) c")).then_inc(hist1_in, 16)
                sp.dma_start(lstate_rows[0:NS, :], state_lru[0]).then_inc(hist1_in, 16)
                sp.dma_start(par_rows1[0:32, :], c_conv_w[0].rearrange("j (c p) -> (j c) p", p=P)).then_inc(hist1_in, 16)
                for n, src in enumerate((c_conv_b, c_b_r, c_b_i, c_lambda)):
                    sp.dma_start(par_rows1[32 + 8 * n:40 + 8 * n, :], src[0].rearrange("(c p) -> c p", p=P))\
                      .then_inc(hist1_in, 16)
                for n, src in enumerate((c_w_r, c_w_i)):
                    sp.dma_start(WRI[:, n, :, :], src[0].rearrange("h (k p) j -> p (h k) j", p=P)).then_inc(wri_in, 16)
                win = c_w_in[0].rearrange("(k p) c -> p k c", p=P)
                for n in range(8):
                    if n >= 4:
                        sp.wait_ge(proj1_ps, 2 * (n - 4) + 2)
                    sp.dma_start(W0[n % 4], win[:, :, 256 * n:256 * n + 256]).then_inc(w1_in[n % 4], 16)
                sp.wait_ge(proj1_ps, 16)
                sp.dma_start(WO1, c_w_out[0].rearrange("(k p) d -> p k d", p=P)).then_inc(wo_in, 16)
                sp.wait_ge(st1_out, 1)
                sd = s_lconv[0].rearrange("s j (c p) -> (s j c) p", p=P)
                sp.dma_start(p_lconv[0, 0].rearrange("j (c p) -> (j c) p", p=P), rows_out[0:24, 0:128])\
                  .then_inc(state_out, 16)
                sp.dma_start(sd[0:84, :], rows_out[24:108, 0:128]).then_inc(state_out, 16)
                sp.dma_start(sd[84:192, :], rows_out[0:108, 128:256]).then_inc(state_out, 16)
                sp.wait_ge(st1_out, 2)
                sp.dma_start(p_lru[0, 0].rearrange("(c p) -> c p", p=P), rows_out[0:8, 256:384]).then_inc(state_out, 16)
                sp.dma_start(s_lru[0].rearrange("s (c p) -> (s c) p", p=P), rows_out[8:72, 256:384]).then_inc(state_out, 16)
            sp.dma_start(X[:, 0:4, :], x_prompt[0].rearrange("(t p) d -> p t d", p=P)).then_inc(x_in, 16)
            sp.dma_start(X[0:TS, 4, :], x_sample.rearrange("s l d -> (s l) d")).then_inc(x_in, 16)
            lnp(0, 0, ln_mix_g, ln_mix_b)
            sp.dma_start(rw[:, :, :], router_w.rearrange("(k p) e -> p k e", p=P)).then_inc(router_in, 16)
            sp.dma_start(rbias[:, :], router_bias.partition_broadcast(P)).then_inc(router_in, 16)
            win = ab_w_in[0].rearrange("(k p) c -> p k c", p=P)
            sp.dma_start(wab_in, win[:, :, 2048:2056]).then_inc(wab_sem, 16)
            sp.dma_start(chist_rows[0:24, :], state_delta_conv[0].rearrange("s j c -> (s j) c")).then_inc(hist_in, 16)
            sp.dma_start(phist_rows[0:120, :], state_pool[0].rearrange("s j c -> (s j) c")).then_inc(hist_in, 16)
            sp.dma_start(par_rows[0:48, :], a_conv_w[0].rearrange("j (c p) -> (j c) p", p=P)).then_inc(hist_in, 16)
            sp.dma_start(par_rows[48:52, :], b_scale[0].rearrange("(c p) -> c p", p=P)).then_inc(hist_in, 16)
            sp.dma_start(par_rows[52:53, :], a_norm_w).then_inc(hist_in, 16)
            cols = [256 * i for i in range(6)] + [2056, 2312] + [1536, 1792]
            for n, c in enumerate(cols):
                if n >= 4:
                    sp.wait_ge(proj_ps, 2 * (n - 4) + 2)
                sp.dma_start(W0[n % 4], win[:, :, c:c + 256]).then_inc(w_in[n % 4], 16)
                if n == 3:
                    sp.wait_ge(consts_ready, 1)
                    for l in range(2):
                        sp.dma_start(slot_list[l].rearrange("(p n) o -> p (n o)", p=P), zero_i[:, :])\
                          .then_inc(lists_zeroed, 16)
            sp.wait_ge(q_scaled, 4)
            sp.wait_ge(k_scaled, 4)
            sp.dma_start(SS, state_delta[0].rearrange("s h k v -> k (s h) v")).then_inc(ss_in, 16)
            sp.dma_start(WG, b_w_group[0].rearrange("g c d -> c g d")).then_inc(wg_in, 16)
            sp.wait_ge(strow_out, 1)
            sp.dma_start(p_pool[0, 0].rearrange("j c -> j c"), rows_out[0:HIST, 0:512]).then_inc(state_out, 16)
            sp.dma_start(s_pool[0].rearrange("s j c -> (s j) c"), rows_out[0:120, 512:1024]).then_inc(state_out, 16)
            sd = s_dconv[0].rearrange("s j (c p) -> (s j c) p", p=P)
            sp.dma_start(p_dconv[0, 0].rearrange("j (c p) -> (j c) p", p=P), rows_out[0:36, 1024:1152])\
              .then_inc(state_out, 16)
            for g, (lo, hi) in enumerate(((36, 108), (0, 108), (0, 108))):
                at = 108 * g + lo - 36
                sp.dma_start(sd[at:at + hi - lo, :], rows_out[lo:hi, 1024 + P * g:1152 + P * g]).then_inc(state_out, 16)
            wout = ab_w_out[0].rearrange("(k p) d -> p k d", p=P)
            sp.dma_start(WO_SUMS, wout[:, NH + 2:NH + 3, :]).then_inc(wo_early_in, 16)
            sp.wait_ge(state_out, 16 * 6)
            lnp(1, 0, ln_ffn_g, ln_ffn_b)
            d_dve.wait(sp, 3, "s")
            sp.dma_start(p_delta[0, 0].rearrange("h k v -> k h v"), SP_).then_inc(state_out, 16)
            for k, to in ((NH, WO_U), (NH + 3, WO_RING)):
                sp.dma_start(to, wout[:, k:k + to.shape[1], :]).then_inc(wo_early_in, 16)
            e_pe.wait(sp, 0, "sn3")
            sp.dma_start(WO_HEADS, wout[:, 0:NH, :]).then_inc(wo_in, 16)
            e_dve.wait(sp, 0, "s3")
            sp.dma_start(s_delta[0].rearrange("s h k v -> k (s h) v"), SS).then_inc(state_out, 16)
            sp.wait_ge(state_out, 16 * 8)
            experts(0)
            mixer1()
            sp.wait_ge(state_out, 16 * 13)
            lnp(1, 1, ln_ffn_g, ln_ffn_b)
            experts(1)
            for t in range(NT):
                sp.wait_ge(norm_done, 3 * NT + t + 1)
                dst = xrow_dram(t, y_prompt, y_sample)
                sp.dma_start(dst, X[0:ROWS[t], t, :]).then_inc(y_out, 16)
            sp.wait_ge(y_out, 16 * NT)
            sp.wait_ge(state_out, 16 * 13)

        @block.tensor
        def _(pe):
            mm, tr = nc.tensor.matmul, nc.tensor.transpose

            def to_channels(n, tiles=range(NT)):
                for t in tiles:
                    r, b = ROWS[t], TILE_BANK(t)
                    if n:
                        pe.wait_ge(norm_done, (n - 1) * NT + t + 1)
                    elif t == 0:
                        pe.wait_ge(x_in, 32)
                        pe.wait_ge(consts_ready, 1)
                    if n == 3 and t == 0:
                        pe.wait_ge(st1_out, 2)
                    if n * NT + t >= 2:
                        pe.wait_ge(xt_lo, n * NT + t - 1)
                        pe.wait_ge(xt_hi, n * NT + t - 1)
                    for k in range(KD):
                        last = tr(heads_of(b + k // 4, P, r)[:, k % 4, :], X[0:r, t, P * k:P * k + P], ident[0:r, 0:r])
                    last.then_inc(xt_ps, 1)

            def project(c, arrived, done, out_done):
                pe.wait_ge(arrived[(c // 2) % 4], 16 * (c // 8 + 1))
                if c >= 3:
                    pe.wait_ge(out_done, c - 2)
                w = W0[(c // 2) % 4][:, :, P * (c % 2):P * (c % 2) + P]
                for k in range(KD):
                    mm(bank[c % 3][:, :], w[:, k, :], XT[:, k, 0:TP], start=(k == 0), stop=(k == KD - 1))
                    last = mm(bank[(3, 6, 7)[c % 3]][:, 0:TS], w[:, k, :], XT[:, k, TP:T],
                              start=(k == 0), stop=(k == KD - 1))
                last.then_inc(done, 1)

            def project_split(c):
                split1.wait(pe, 0, f"w{c}")
                if c >= 3:
                    pe.wait_ge(proj1_out, c - 2)
                w_high, w_low = W1_HIGH[c % 2], W1_LOW[(c // 2) % 4][:, :, P * (c % 2):P * (c % 2) + P]
                parts = ((w_high, XT_HIGH), (w_high, XT_LOW), (w_low, XT_HIGH))
                for k in range(KD):
                    for n, (w, x) in enumerate(parts):
                        ends = dict(start=(k == n == 0), stop=(k == KD - 1 and n == 2))
                        mm(bank[c % 3][:, 0:TH], w[:, k, :], x[:, k, 0:TH], **ends)
                        last = mm(bank[(3, 6, 7)[c % 3]][:, 0:TH], w[:, k, :], x[:, k, TH:T], **ends)
                last.then_inc(proj1_ps, 1)

            def delta_front(b):
                cols = tile_cols(b)
                kT, qT, vT = (lambda h, o=o: QKV[:, o + h, cols] for o in (4, 0, 8))
                if b:
                    d_dve.wait(pe, b - 1, "kd")
                for h in range(NH):
                    last = tr(heads_of(0)[:, h, :], kT(h), ident[:, :])
                d_pe.end(last, b, "ktr")
                if b:
                    d_act.wait(pe, b - 1, "vb")
                for h in range(NH):
                    last = tr(heads_of(1)[:, h, :], vT(h), ident[:, :])
                d_pe.end(last, b, "vtr")
                if b:
                    d_dve.wait(pe, b - 1, "p0")
                for h in range(NH):
                    last = mm(heads_of(2)[:, h, :], kT(h), kT(h), start=True, stop=True)
                d_pe.end(last, b, "gram")
                if b:
                    d_dve.wait(pe, b - 1, "a")
                for h in range(NH):
                    last = mm(heads_of(3)[:, h, :], kT(h), qT(h), start=True, stop=True)
                d_pe.end(last, b, "qk")

            def power_transposed(b):
                d_dve.wait(pe, b, "p0")
                if b:
                    d_act.wait(pe, b - 1, "tb")
                for h in range(NH):
                    last = tr(heads_of(4)[:, h, :], Pa[:, h, :], ident[:, :])
                d_pe.end(last, b, "pt")

            def delta_prompt(b):
                cols, u = tile_cols(b), b % 2
                qT = lambda h: QKV[:, h, cols]
                pw, pwt = (Pa, Pb), (PTa, PTb)
                for r in range(1, 6):
                    a, o = (r - 1) % 2, r % 2
                    d_act.wait(pe, b, f"pt{r - 1}")
                    d_dve.wait(pe, b, f"p{r - 1}")
                    if r == 1 and b:
                        d_dve.wait(pe, b - 1, "un")
                    for h in range(NH):
                        last = mm(heads_of(5)[:, h, :], pwt[a][:, h, :], pw[a][:, h, :], start=True, stop=True)
                    d_pe.end(last, b, f"p{r}")
                    if r == 1 and b:
                        d_dve.wait(pe, b - 1, "s")
                    if r < 5:
                        for h in range(NH):
                            last = mm(heads_of(6)[:, h, :], pw[a][:, h, :], pwt[a][:, h, :], start=True, stop=True)
                        d_pe.end(last, b, f"pt{r}")
                    d_dve.wait(pe, b, f"p{r}")
                    d_dve.wait(pe, b, f"tt{r - 1}")
                    if r == 1 and b:
                        d_act.wait(pe, b - 1, "o")
                    for h in range(NH):
                        last = mm(heads_of(7)[:, h, :], pw[o][:, h, :], TT[:, h, :], start=True, stop=True)
                    d_pe.end(last, b, f"x{r}")
                    if r == 2:
                        if b + 1 < NT - 1:
                            delta_front(b + 1)
                        else:
                            samples_front()
                d_dve.wait(pe, b, "tt5")
                for h in range(NH):
                    last = tr(heads_of(4)[:, h, :], TT[:, h, :], ident[:, :])
                d_pe.end(last, b, "tb")
                for h in range(NH):
                    last = mm(heads_of(5)[:, h, :], Noff[u][:, h, :], TT[:, h, :], start=True, stop=True)
                d_pe.end(last, b, "y")
                d_act.wait(pe, b, "tb")
                d_dve.wait(pe, b, "y")
                for h in range(NH):
                    last = mm(heads_of(7)[:, h, :], TB[:, h, :], Yo[:, h, :], start=True, stop=True)
                d_pe.end(last, b, "x6")
                d_dve.wait(pe, b, "tt6")
                for h in range(NH):
                    last = mm(heads_of(6)[:, h, :], kbg[u][:, h, :], TT[:, h, :], start=True, stop=True)
                d_pe.end(last, b, "nw")
                if b + 1 < NT - 1:
                    power_transposed(b + 1)
                d_act.wait(pe, b, "nw")
                if b == 0:
                    pe.wait_ge(s_zeroed, 1)
                else:
                    d_dve.wait(pe, b - 1, "s")
                for h in range(NH):
                    mm(heads_of(5)[:, h, :], TT[:, h, :], vb[u][:, h, :], start=True, stop=False)
                    last = mm(heads_of(5)[:, h, :], nwT[:, h, :], SP_[:, h, :], start=False, stop=True)
                d_pe.end(last, b, "un")
                d_dve.wait(pe, b, "un")
                d_pool.wait(pe, b, "qd")
                for h in range(NH):
                    mm(heads_of(7)[:, h, :], SP_[:, h, :], qT(h), start=True, stop=False)
                    last = mm(heads_of(7)[:, h, :], un[:, h, :], aT[u][:, h, :], start=False, stop=True)
                d_pe.end(last, b, "o")
                for h in range(NH):
                    last = mm(heads_of(6)[:, h, :], kd[u][:, h, :], un[:, h, :], start=True, stop=True)
                d_pe.end(last, b, "sn")

            def samples_front():
                b, n = NT - 1, TS
                cols = tile_cols(b)
                kT, qT, vT = (lambda h, o=o: QKV[:, o + h, cols] for o in (4, 0, 8))
                d_dve.wait(pe, 3, "kd")
                for h in range(NH):
                    last = tr(heads_of(0, n)[:, h, :], kT(h), ident[:, :])
                e_pe.end(last, 0, "ktr")
                d_act.wait(pe, 3, "vb")
                for h in range(NH):
                    last = tr(heads_of(1, n)[:, h, :], vT(h), ident[:, :])
                e_pe.end(last, 0, "vtr")
                d_dve.wait(pe, 3, "p0")
                for h in range(NH):
                    last = mm(heads_of(2, n, n)[:, h, :], kT(h), kT(h), start=True, stop=True)
                e_pe.end(last, 0, "gram")
                for h in range(NH):
                    last = mm(heads_of(3, n, n)[:, h, :], kT(h), qT(h), start=True, stop=True)
                e_pe.end(last, 0, "qk")

            def delta_samples():
                b, n = NT - 1, TS
                e_dve.wait(pe, 0, "p0")
                for h in range(NH):
                    last = tr(heads_of(4, n, n)[:, h, :], Pa[0:n, h, 0:n], ident[0:n, 0:n])
                e_pe.end(last, 0, "pt")
                pw, pwt = (Pa, Pb), (PTa, PTb)
                for r in (1, 2):
                    a, o = (r - 1) % 2, r % 2
                    e_act.wait(pe, 0, f"pt{r - 1}")
                    if r == 1:
                        d_dve.wait(pe, 3, "s")
                        d_act.wait(pe, 3, "o")
                    for h in range(NH):
                        last = mm(heads_of(5, n, n)[:, h, :], pwt[a][0:n, h, 0:n], pw[a][0:n, h, 0:n],
                                  start=True, stop=True)
                    e_pe.end(last, 0, f"p{r}")
                    if r < 2:
                        for h in range(NH):
                            last = mm(heads_of(6, n, n)[:, h, :], pw[a][0:n, h, 0:n], pwt[a][0:n, h, 0:n],
                                      start=True, stop=True)
                        e_pe.end(last, 0, f"pt{r}")
                    e_dve.wait(pe, 0, f"p{r}")
                    for h in range(NH):
                        last = mm(heads_of(7, n, n)[:, h, :], pw[o][0:n, h, 0:n], TT[0:n, h, 0:n],
                                  start=True, stop=True)
                    e_pe.end(last, 0, f"x{r}")
                e_dve.wait(pe, 0, "tt2")
                for h in range(NH):
                    last = mm(heads_of(6, P, n)[:, h, :], kbg[0][0:n, h, :], TT[0:n, h, 0:n], start=True, stop=True)
                e_pe.end(last, 0, "nw")
                e_act.wait(pe, 0, "nw")
                pe.wait_ge(ss_in, 16)
                pe.wait_ge(rms_sq, 1)
                for h in range(NH):
                    last = mm(bank[4][0:NH, :], ms_col[:, h, :], gB[:, h, 0:TP], start=(h == 0), stop=(h == 3))
                last.then_inc(rms_ps, 1)
                pe.wait_ge(wg_in, 16)
                pe.wait_ge(pooled_done, NH)
                for g in range(NH):
                    if g >= 2:
                        pe.wait_ge(mix_b, g - 1)
                    b5, b7 = ((5, 7), (2, 3))[g % 2]
                    mm(bank[b5][:, :], WG[:, g, :], POOLED[:, g, 0:TP], start=True, stop=True)
                    mm(bank[b7][:, 0:TS], WG[:, g, :], POOLED[:, g, TP:T], start=True, stop=True).then_inc(group_ps, 1)
                e_pool.wait(pe, 0, "qd")
                for h in range(NH):
                    both, nwq = (x.rearrange("p (a c) -> p a c", a=2) for x in (heads_of(0)[:, h, :], nwT[:, h, :]))
                    for s in range(NS):
                        c = slice(LS * s, LS * s + LS)
                        mm(both[:, :, c], SS[:, NH * s + h, :], nwq[:, :, c], start=(h == s == 0), stop=False)
                for h in range(NH):
                    last = mm(heads_of(0)[:, h, 0:n], vb[0][0:n, h, :], TT[0:n, h, 0:n], start=False, stop=(h == NH - 1))
                e_pe.end(last, 0, "ut")
                e_act.wait(pe, 0, "ut")
                pe.wait_ge(rms_eps, 1)
                for h in range(NH):
                    last = tr(heads_of(4, n)[:, h, :], Yo[:, h, 0:n], ident[:, :])
                e_pe.end(last, 0, "un")
                e_dve.wait(pe, 0, "un")
                for h in range(NH):
                    last = mm(heads_of(1, P, n)[:, h, :], un[0:n, h, :], aT[0][0:n, h, 0:n], start=True, stop=True)
                e_pe.end(last, 0, "o")
                pe.wait_ge(mix_b, NH)

                def state_update(h):
                    e_pool.wait(pe, 0, f"ub{h}")
                    if h >= 2:
                        e_dve.wait(pe, 0, f"s{h - 2}")
                    for half, bb in enumerate(((2, 3), (5, 6))[h % 2]):
                        last = mm(heads_of(bb)[:, :, :], kd[0][0:n, h, :], UB[h % 2][0:n, 4 * half:4 * half + 4, :],
                                  start=True, stop=True)
                    e_pe.end(last, 0, f"sn{h}")

                def root_spread(h):
                    if h >= 2:
                        pe.wait_ge(rmsb_out, h - 1)
                    b4, b7 = ((4, 7), (0, 1))[h % 2]
                    mm(bank[b4][:, :], sel_row[:, h, :], gB[0:NH, 0, 0:TP], start=True, stop=True)
                    mm(bank[b7][:, 0:TS], sel_row[:, h, :], gB[0:NH, 0, TP:T], start=True, stop=True)\
                        .then_inc(rmsb_ps, 1)

                state_update(0)
                pe.wait_ge(rms_sq, 2)
                for h in range(NH):
                    last = mm(bank[7][0:NH, 0:TS], ms_col[:, h, :], gB[:, h, TP:T], start=(h == 0), stop=(h == 3))
                last.then_inc(rms_ps, 1)
                state_update(1)
                pe.wait_ge(rms_inv, 2)
                root_spread(0)
                root_spread(1)
                state_update(2)
                root_spread(2)
                state_update(3)
                root_spread(3)

            def mixer0():
                pe.wait_ge(hist_in, 16 * 5)
                for c in range(NCHUNK):
                    last = tr(bank[0][:, 24 * c:24 * c + 24], chist_rows[0:24, P * c:P * c + P], ident[0:24, 0:24])
                last.then_inc(hist_ps, 1)
                for g in range(NH):
                    last = tr(bank[1][:, 120 * g:120 * g + 120], phist_rows[0:120, P * g:P * g + P],
                              ident[0:120, 0:120])
                last.then_inc(hist_ps, 1)
                tr(bank[2][:, 0:53], par_rows[0:53, :], ident[0:53, 0:53]).then_inc(hist_ps, 1)
                pe.wait_ge(xt_lo, NT)
                pe.wait_ge(xt_hi, NT)
                pe.wait_ge(wab_ready, 1)
                for k in range(KD):
                    mm(bank[4][0:68, :], wab[:, k, :], XT[:, k, 0:TP], start=(k == 0), stop=(k == KD - 1))
                    last = mm(bank[5][0:68, 0:TS], wab[:, k, :], XT[:, k, TP:T], start=(k == 0), stop=(k == KD - 1))
                last.then_inc(ab_ps, 1)
                pe.wait_ge(hist_out, 3)
                for c in range(NPROJ):
                    project(c, w_in, proj_ps, proj_out)
                    if 3 <= c < 11:
                        n = c - 3
                        pe.wait_ge(sq_done, n + 1)
                        if n:
                            pe.wait_ge(inv_done, n)
                        else:
                            pe.wait_ge(rows_ready, 1)
                        mm(bank[4][:, :], ones[:, :], SQ[:, n % 2, 0:TP], start=True, stop=True)
                        mm(bank[5][:, 0:TS], ones[:, :], SQ[:, n % 2, TP:T], start=True, stop=True).then_inc(ssq_ps, 1)
                    if 11 <= c < 15:
                        h = c - 11
                        if h:
                            pe.wait_ge(gcb_out, h)
                        else:
                            pe.wait_ge(inv_done, 8)
                        mm(bank[4][:, :], sel_gc[:, h, :], RT[0:68, 0:TP], start=True, stop=True)
                        mm(bank[5][:, 0:TS], sel_gc[:, h, :], RT[0:68, TP:T], start=True, stop=True).then_inc(gcb_ps, 1)
                    if c == 15:
                        pe.wait_ge(gcb_out, 4)
                        for t in range(NT):
                            last = tr(bank[4][0:ROWS[t], 68 * t:68 * t + 68], RT[0:68, tile_cols(t)], ident[0:68, 0:68])
                        last.then_inc(col_ps, 1)
                pe.wait_ge(proj_out, NPROJ)
                pe.wait_ge(col_out, 1)
                pe.wait_ge(tail_done, NCHUNK)
                pe.wait_ge(utail_done, 1)
                for g in range(NH):
                    tr(bank[4][0:HIST, P * g:P * g + P], U[:, g, TP:TP + HIST], ident[:, :])
                for g in range(NH):
                    tr(bank[5][0:120, P * g:P * g + P], utail[:, g, :], ident[:, :])
                for g in range(3):
                    last = tr(bank[6][0:108, P * g:P * g + P], tails[:, 9 * g:9 * g + 9, :].rearrange("p j c -> p (j c)"), ident[:, :])
                last.then_inc(strow_ps, 1)
                pe.wait_ge(q_scaled, NH)
                pe.wait_ge(k_scaled, NH)
                pe.wait_ge(silu_done, NCHUNK)
                pe.wait_ge(strow_out, 1)
                delta_front(0)
                power_transposed(0)
                for b in range(NT - 1):
                    delta_prompt(b)
                delta_samples()

            def out_part(l, t, ks, ends):
                for half in range(2):
                    for k in ks:
                        last = mm(bank[2 * (t % 2) + half][0:ROWS[t], :], XT[:, k, tile_cols(t)],
                                  (WO_A, WO_B)[l][k][:, 512 * half:512 * half + 512], start=(k == ks[0] and not ends),
                                  stop=(k == ks[-1] and ends))
                if ends:
                    last.then_inc(out_ps, 1)

            def out_projection(l, tiles):
                for t in tiles:
                    if t >= 2:
                        pe.wait_ge(norm_sum, 2 * l * NT + t - 1)
                    for half in range(2):
                        for k in range(KD):
                            last = mm(bank[2 * (t % 2) + half][0:ROWS[t], :], XT[:, k, tile_cols(t)],
                                      (WO_A, WO_B)[l][k][:, 512 * half:512 * half + 512], start=(k == 0), stop=(k == KD - 1))
                    last.then_inc(out_ps, 1)

            def logits(l, tiles):
                n = 1 + 2 * l
                for t in tiles:
                    pe.wait_ge(xt_lo, n * NT + t + 1)
                    pe.wait_ge(xt_hi, n * NT + t + 1)
                    for k in range(KD):
                        last = mm(bank[2][0:ROWS[t], NE * t:NE * t + NE], XT[:, k, tile_cols(t)], rw[:, k, :],
                                  start=(k == 0), stop=(k == KD - 1))
                return last

            def out_and_route(l):
                n, most = 1 + 2 * l, NT - 1
                if l == 0:
                    pe.wait_ge(wo_early_in, 16 * 3)
                    pe.wait_ge(rmsb_out, NH)
                    e_dve.wait(pe, 0, "s2")
                    early, late = range(NH, KD), range(NH)
                else:
                    pe.wait_ge(wo_in, 16 * 2)
                    pe.wait_ge(mix_a, NH + NH)
                    early, late = range(NH), range(NH, KD)
                for t in range(2):
                    out_part(l, t, early, False)
                if l == 1:
                    pe.wait_ge(lru_h, KD)
                    tr(bank[5][0:72, 0:P], lru_last, ident[:, :]).then_inc(st1_ps, 1)
                pe.wait_ge(mix_a, NH + KD * l)
                pe.wait_ge(wo_in, 16 * (l + 1))
                for t in range(2):
                    out_part(l, t, late, True)
                out_projection(l, range(2, most))
                to_channels(n, (0, 1))
                out_projection(l, (most,))
                to_channels(n, (2, 3))
                pe.wait_ge(router_in, 32)
                pe.wait_ge(norm_sum, 2 * l * NT + most)
                logits(l, range(most))
                to_channels(n, (most,))
                logits(l, (most,)).then_inc(logits_ps, 1)
                pe.wait_ge(norm_sum, 2 * l * NT + NT)
                pe.wait_ge(onehot_ready, l + 1)
                hot = rt[:, 11, :]
                mm(bank[1][:, 0:80], m_before[:, :], hot, start=True, stop=True)
                mm(bank[0][:, 0:80], ones[:, :], hot, start=True, stop=True).then_inc(rank_ps, 1)

            def gather_transposed(l, pairs, u, g):
                pe.wait_ge(xg_in[u], arrivals(l, pairs))
                at_least(pe, xgt_ready, g * 2)
                for k in range(KD):
                    last = tr(heads_of(4 + k // 4)[:, k % 4, :], XG[u][:, P * k:P * k + P], ident[:, :])
                last.then_inc(xg_ps, 1)

            def gate(l, pairs, u, g):
                pe.wait_ge(xgt_ready, g * 2 + 2)
                pe.wait_ge(gate_in[u], arrivals(l, pairs))
                at_least(pe, sg_done, g - 1)
                for k in range(KD):
                    last = mm(bank[u][:, :], XGT[:, k, :], WGT[u][:, k, :], start=(k == 0), stop=(k == KD - 1))
                last.then_inc(gate_ps, 1)

            def up(l, pairs, u, g):
                pe.wait_ge(up_in[u], arrivals(l, pairs))
                at_least(pe, h_ready, g - 1)
                for k in range(KD):
                    last = mm(bank[2 + u][:, :], XGT[:, k, :], WUP[u][:, k, :], start=(k == 0), stop=(k == KD - 1))
                last.then_inc(up_ps, 1)

            def h_transposed(u, g):
                pe.wait_ge(h_ready, g + 1)
                at_least(pe, y0_out, g)
                for f in range(4):
                    last = tr(heads_of(7)[:, f, :], HB[u][:, P * f:P * f + P], ident[:, :])
                last.then_inc(h_ps, 1)

            def down(l, u, g):
                pe.wait_ge(down_split, g + (1 - l))
                at_least(pe, y1_out, g)
                for half, done in ((1, y1_ps), (0, y0_ps)):
                    cols = slice(512 * half, 512 * half + 512)
                    for f in range(4):
                        for n, (x, w) in enumerate(((HT_HIGH, WDN_HIGH), (HT_HIGH, WDN_LOW[u]), (HT_LOW, WDN_HIGH))):
                            last = mm(bank[7 - half][:, :], x[:, f, :], w[:, f, cols],
                                      start=(f == n == 0), stop=(f == 3 and n == 2))
                    last.then_inc(done, 1)

            def last_down(l, g):
                pe.wait_ge(ht_ready, g + 1)
                pe.wait_ge(down_in[1], arrivals(l, NE // 2))
                pe.wait_ge(y1_out, g)
                for half, done in ((1, y1_ps), (0, y0_ps)):
                    for f in range(4):
                        last = mm(bank[7 - half][:, :], HT[:, f, :], WDN[1][:, f, 512 * half:512 * half + 512],
                                  start=(f == 0), stop=(f == 3))
                    last.then_inc(done, 1)

            def experts(l):
                base = NE * l

                def step(i, v):
                    u, g = (1 + v) % 2, i * 2 + (base + 1 + v)
                    gate(l, i + (v + 1), u, g)
                    h_transposed(1 - u, g - 1)
                    up(l, i + (v + 1), u, g)
                    gather_transposed(l, i + 2, 1 - u, g + 1)
                    down(l, 1 - u, g - 1)

                pe.wait_ge(pos_ready, l + 1)
                pe.wait_ge(xt_hi, (2 * l + 2) * NT)
                gather_transposed(l, 1, 0, base)
                gate(l, 1, 0, base)
                up(l, 1, 0, base)
                gather_transposed(l, 1, 1, base + 1)
                step(0, 0)
                step(0, 1)
                with pe.Fori(1, NE // 2 - 1) as i:
                    step(i, 0)
                    step(i, 1)
                gate(l, 8, 1, base + 15)
                h_transposed(0, base + 14)
                up(l, 8, 1, base + 15)
                down(l, 0, base + 14)
                h_transposed(1, base + 15)
                last_down(l, base + 15)
                overflow(l)

            def overflow(l):
                s = ov[l]
                most = pe.value_load(over_i[0:1, 0:1], min_val=0, max_val=T)
                with pe.If(most > P):
                    pe.wait_ge(y0_out, NE * (l + 1))
                    pe.wait_ge(y1_out, NE * (l + 1))
                    pe.sem_inc(s["pe"], 4)
                    with pe.Fori(1, BLOCKS) as b:
                        with pe.Fori(0, NE) as e:
                            n = b * NE + e - (NE - 1)
                            ov_wait(pe, l, n, "xg")
                            for k in range(KD):
                                last = tr(heads_of(4 + k // 4)[:, k % 4, :], XG[0][:, P * k:P * k + P], ident[:, :])
                            last.then_inc(s["pe"], 1)
                            ov_wait(pe, l, n, "xgt")
                            ov_wait(pe, l, n, "w")
                            for to, w in ((0, WGT), (2, WUP)):
                                for k in range(KD):
                                    last = mm(bank[to][:, :], XGT[:, k, :], w[0][:, k, :],
                                              start=(k == 0), stop=(k == KD - 1))
                            last.then_inc(s["pe"], 1)
                            ov_wait(pe, l, n, "h")
                            for f in range(4):
                                last = tr(heads_of(7)[:, f, :], HB[0][:, P * f:P * f + P], ident[:, :])
                            last.then_inc(s["pe"], 1)
                            ov_wait(pe, l, n, "ht")
                            for half in (1, 0):
                                for f in range(4):
                                    last = mm(bank[7 - half][:, :], HT[:, f, :],
                                              WDN[0][:, f, 512 * half:512 * half + 512],
                                              start=(f == 0), stop=(f == 3))
                            last.then_inc(s["pe"], 1)

            def mixer1():
                pe.wait_ge(hist1_in, 16 * 7)
                pe.wait_ge(y0_out, NE)
                for c in range(KD):
                    last = tr(bank[0][:, 24 * c:24 * c + 24], lhist_rows[0:24, P * c:P * c + P], ident[0:24, 0:24])
                last.then_inc(lru_hist_ps, 1)
                for c in range(KD):
                    last = tr(bank[1][:, NS * c:NS * c + NS], lstate_rows[0:NS, P * c:P * c + P], ident[0:NS, 0:NS])
                last.then_inc(lru_hist_ps, 1)
                tr(bank[2][:, 0:64], par_rows1[0:64, :], ident[0:64, 0:64]).then_inc(lru_hist_ps, 1)
                pe.wait_ge(lru_hist_out, 3)
                split1.wait(pe, 0, f"x{NT - 1}")
                for c in range(16):
                    project_split(c)
                pe.wait_ge(wri_in, 32)
                pe.wait_ge(proj1_out, 16)
                for m in range(KD):
                    for n in range(2):
                        j = 2 * m + n
                        pe.wait_ge(conv1_done, 2 * (m // 2) + 2)
                        at_least(pe, lru_gates_done, j - 3)
                        b0 = (4, 0, 2, 6)[j % 4]
                        for k in range(2):
                            w = WRI[:, n, 2 * (m // 2) + k, P * (m % 2):P * (m % 2) + P]
                            x = XC[:, 2 * (m // 2) + k, :]
                            mm(bank[b0][:, :], w, x[:, 0:TP], start=(k == 0), stop=(k == 1))
                            last = mm(bank[b0 + 1][:, 0:TS], w, x[:, TP:T], start=(k == 0), stop=(k == 1))
                        last.then_inc(lru_gate_ps, 1)
                pe.wait_ge(lru_gates_done, 16)
                pe.wait_ge(tail1_done, KD)
                for g in range(2):
                    last = tr(bank[4][0:108, P * g:P * g + P], tails1[:, :, :]
                              .rearrange("p j c -> p (j c)")[:, 108 * g:108 * g + 108], ident[:, :])
                last.then_inc(st1_ps, 1)

            to_channels(0)
            mixer0()
            for l in range(2):
                out_and_route(l)
                experts(l)
                if l == 0:
                    to_channels(2)
                    mixer1()

        @block.scalar
        def _(act):
            def copy(out, in_, scale=1.0):
                return nc.scalar.activation(out, in_, ACT.Copy, scale=scale)

            def to_channels(n, tiles=range(NT)):
                for t in tiles:
                    act.wait_ge(xt_ps, n * NT + t + 1)
                    copy(XT[:, 4:8, tile_cols(t)], heads_of(TILE_BANK(t) + 1, P, ROWS[t])).then_inc(xt_hi, 1)

            def gates():
                act.wait_ge(consts_ready, 1)
                act.wait_ge(ab_ps, 1)
                nc.scalar.activation(RT[0:4, 0:TP], bank[4][0:4, :], ACT.Sigmoid).then_inc(gate_act, 1)
                nc.scalar.activation(RT[0:4, TP:T], bank[5][0:4, 0:TS], ACT.Sigmoid).then_inc(gate_act, 1)
                act.wait_ge(gates_in, 32)
                nc.scalar.activation(gpar[32:36, 1:2], gpar[32:36, 1:2], ACT.Exp).then_inc(gate_act, 1)
                act.wait_ge(gate_dve, 1)
                nc.scalar.activation(RB[32:36, :], RB[32:36, :], ACT.Exp).then_inc(gate_act, 1)
                act.wait_ge(gate_act, 4)
                nc.scalar.activation(RB[32:36, :], RB[32:36, :], ACT.Ln, bias=ones[32:36, 0:1]).then_inc(gate_act, 1)

            def decays(b):
                d_pool.wait(act, b, "max")
                d_act.end(nc.scalar.activation(dmx, dmx, ACT.Exp, scale=-1.0), b, "dbd")
                d_pool.wait(act, b, "min")
                d_act.end(nc.scalar.activation(dmn, dmn, ACT.Exp), b, "dt")

            def chunk_decay(b):
                d_act.end(nc.scalar.activation(egB, gB[:, :, tile_cols(b)], ACT.Exp), b, "eg")

            def weighted_v(b):
                d_pe.wait(act, b, "vtr")
                for h in range(NH):
                    last = copy(vb[b % 2][:, h, :], heads_of(1)[:, h, :], COL[:, b, h:h + 1])
                d_act.end(last, b, "vb")

            def delta_prompt(b):
                for r in range(5):
                    d_pe.wait(act, b, "pt" if r == 0 else f"pt{r}")
                    d_act.end(copy((PTa, PTb)[r % 2], heads_of(4 if r == 0 else 6)), b, f"pt{r}")
                    if r == 0:
                        continue
                    if b + 1 < NT - 1:
                        (None, decays, chunk_decay, weighted_v, lambda b: None)[r](b + 1)
                    else:
                        (None, samples_decays, samples_chunk_decay, samples_v, lambda: None)[r]()
                d_pe.wait(act, b, "tb")
                d_act.end(copy(TB, heads_of(4)), b, "tb")
                d_pe.wait(act, b, "nw")
                d_act.end(copy(nwT, heads_of(6), -1.0), b, "nw")
                d_pe.wait(act, b, "o")
                d_act.end(copy(QKV[:, 8:12, tile_cols(b)], heads_of(7)), b, "o")

            def samples_decays():
                n = TS
                e_pool.wait(act, 0, "max")
                e_act.end(nc.scalar.activation(dmx[0:n, :, 0:n], dmx[0:n, :, 0:n], ACT.Exp, scale=-1.0), 0, "dbd")
                e_pool.wait(act, 0, "min")
                e_act.end(nc.scalar.activation(dmn[0:n, :, 0:n], dmn[0:n, :, 0:n], ACT.Exp), 0, "dt")

            def samples_chunk_decay():
                e_act.end(nc.scalar.activation(egB[:, :, 0:TS], gB[:, :, tile_cols(NT - 1)], ACT.Exp), 0, "eg")

            def samples_v():
                b, n = NT - 1, TS
                e_pe.wait(act, 0, "vtr")
                for h in range(NH):
                    last = copy(vb[0][0:n, h, :], heads_of(1, n)[:, h, :], COL[0:n, b, h:h + 1])
                e_act.end(last, 0, "vb")

            def delta_samples():
                n = TS
                for r in range(2):
                    e_pe.wait(act, 0, "pt" if r == 0 else "pt1")
                    e_act.end(copy((PTa, PTb)[r][0:n, :, 0:n], heads_of(4 if r == 0 else 6, n, n)), 0, f"pt{r}")
                d_act.wait(act, 3, "o")
                nc.scalar.activation(gB[:, :, 0:TP], QKV[:, 8:12, 0:TP], ACT.Square).then_inc(rms_sq, 1)
                e_pe.wait(act, 0, "nw")
                e_act.end(copy(nwT[:, :, 0:n], heads_of(6, P, n), -1.0), 0, "nw")
                for g in range(NH):
                    act.wait_ge(group_ps, g + 1)
                    b5, b7 = ((5, 7), (2, 3))[g % 2]
                    sc = par[:, 48 + g:49 + g]
                    copy(XT[:, NH + g, 0:TP], bank[b5][:, :], sc)
                    copy(XT[:, NH + g, TP:T], bank[b7][:, 0:TS], sc).then_inc(mix_b, 1)
                act.wait_ge(rms_eps, 1)
                nc.scalar.activation(gB[0:NH, 0, 0:TP], gB[0:NH, 0, 0:TP], ACT.Sqrt).then_inc(rms_root, 1)
                e_pe.wait(act, 0, "ut")
                e_act.end(copy(Yo[:, :, 0:n], heads_of(0)[:, :, 0:n]), 0, "ut")

            def mixer0():
                gates()
                for c in range(NPROJ):
                    pb, sbk = bank[c % 3], bank[(3, 6, 7)[c % 3]]
                    act.wait_ge(proj_ps, c + 1)
                    if c < NCHUNK:
                        if c >= 3:
                            act.wait_ge(conv_done, c - 2)
                            act.wait_ge(tail_done, c - 2)
                        buf = EXTB[c % 3]
                        copy(buf[:, CONV - 1:EXT_P], pb[:, :])
                        copy(ext_samples(buf)[:, :, CONV - 1:], sbk[:, 0:TS].rearrange("p (s l) -> p s l", s=NS))\
                            .then_inc(proj_out, 1)
                    elif c < 16:
                        g = c - NCHUNK
                        copy(U[:, g, HIST:UEP], pb[:, :])
                        copy(U[:, g, UEP:UE].rearrange("p (s l) -> p s l", s=NS)[:, :, HIST:],
                             sbk[:, 0:TS].rearrange("p (s l) -> p s l", s=NS)).then_inc(proj_out, 1)
                    else:
                        nc.scalar.activation(Z[:, c - 16, 0:TP], pb[:, :], ACT.Silu)
                        nc.scalar.activation(Z[:, c - 16, TP:T], sbk[:, 0:TS], ACT.Silu).then_inc(proj_out, 1)
                    if 1 <= c <= NCHUNK:
                        n = c - 1
                        act.wait_ge(conv_done, n + 1)
                        nc.scalar.activation(QKV[:, n, :], CV[:, n % 2, :], ACT.Silu).then_inc(silu_done, 1)
                        if n < 8:
                            if n >= 2:
                                act.wait_ge(ssq_ps, n - 1)
                            act.wait_ge(silu_done, n + 1)
                            nc.scalar.activation(SQ[:, n % 2, :], QKV[:, n, :], ACT.Square).then_inc(sq_done, 1)
                    if 11 <= c < 15:
                        h = c - 11
                        act.wait_ge(gcb_ps, h + 1)
                        copy(gB[:, h, 0:TP], bank[4][:, :])
                        copy(gB[:, h, TP:T], bank[5][:, 0:TS]).then_inc(gcb_out, 1)
                    if c == 13:
                        act.wait_ge(inv_done, 8)
                        for n in range(2):
                            nc.scalar.activation(INV[:, 4 * n:4 * n + 4, :], INV[:, 4 * n:4 * n + 4, :], ACT.Sqrt)\
                                .then_inc(roots_done, 1)
                act.wait_ge(gcb_out, 4)
                act.wait_ge(col_out, 1)
                nc.scalar.activation(ecol[:, :, :], COL[:, :, 32:36], ACT.Exp).then_inc(egl_done, 1)
                nc.scalar.activation(kdc[:, :, :], COL[:, :, 64:68], ACT.Exp).then_inc(egl_done, 1)
                nc.scalar.activation(egl[:, :, 0:4], gB[:, :, 0:TP].rearrange("p h (c l) -> p h c l", l=P)[:, :, :, P - 1],
                                     ACT.Exp).then_inc(egl_done, 1)
                nc.scalar.activation(egl[:, :, 4:12], gB[:, :, TP:T].rearrange("p h (c l) -> p h c l", l=LS)[:, :, :, LS - 1],
                                     ACT.Exp).then_inc(egl_done, 1)
                decays(0)
                chunk_decay(0)
                weighted_v(0)
                for b in range(NT - 1):
                    delta_prompt(b)
                delta_samples()
                e_dve.wait(act, 0, "o")
                nc.scalar.activation(gB[:, :, TP:T], QKV[:, 8:12, TP:T], ACT.Square).then_inc(rms_sq, 1)
                act.wait_ge(rms_eps, 2)
                nc.scalar.activation(gB[0:NH, 0, TP:T], gB[0:NH, 0, TP:T], ACT.Sqrt).then_inc(rms_root, 1)

            def norm(q):
                def weighted(t):
                    act.wait_ge(ysel_in[t], 32 * (q // 2 + 1))
                    copy(Y1[t][0:ROWS[t], :], Y1[t][0:ROWS[t], :], wsel[0:ROWS[t], 0, t:t + 1])\
                        .then_inc(ysel_scaled, 1)

                def root(t):
                    act.wait_ge(norm_stats, q * NT + t + 1)
                    r = ROWS[t]
                    nc.scalar.activation(lnw[0:r, t, 14:15], lnw[0:r, t, 13:14], ACT.Sqrt).then_inc(norm_root, 1)

                def scaled(t):
                    act.wait_ge(norm_coef, q * NT + t + 1)
                    r = ROWS[t]
                    nc.scalar.activation(X[0:r, t, :], X[0:r, t, :], ACT.Identity, bias=lnw[0:r, t, 15:16],
                                         scale=lnw[0:r, t, 14:15]).then_inc(norm_scaled, 1)

                if q % 2 == 0:
                    for t in range(NT - 1):
                        root(t)
                        scaled(t)
                    to_channels(q + 1, (0, 1))
                    root(NT - 1)
                    to_channels(q + 1, (2,))
                    scaled(NT - 1)
                    to_channels(q + 1, (3, 4))
                    return
                weighted(0)
                for t in range(NT):
                    if t + 1 < NT:
                        weighted(t + 1)
                    root(t)
                    if t:
                        scaled(t - 1)
                scaled(NT - 1)

            def route(l):
                act.wait_ge(logits_ps, l + 1)
                nc.scalar.activation(scores[:, 0:4, :], bank[2][:, 0:64].rearrange("p (t e) -> p t e", t=4), ACT.Sigmoid)
                nc.scalar.activation(scores[0:TS, 4, :], bank[2][0:TS, 64:80], ACT.Sigmoid).then_inc(scores_done, 1)

            def y_view(l):
                return y_rows[l].rearrange("(b s e) d -> b s e d", b=BLOCKS, s=P)

            def experts(l):
                base = NE * l

                def h_copied(g):
                    act.wait_ge(h_ps, g + 1)
                    copy(HT_HIGH[:, :, :], heads_of(7))
                    copy(HT, heads_of(7)).then_inc(ht_ready, 1)

                def round_down(pairs, u, g):
                    act.wait_ge(down_in[u], arrivals(l, pairs))
                    at_least(act, y0_ps, g)
                    for f in range(4):
                        last = copy(WDN_HIGH[:, f, :], WDN[u][:, f, :])
                    last.then_inc(down_rounded, 1)

                def silu(u, g):
                    act.wait_ge(gate_ps, g + 1)
                    at_least(act, h_ready, g - 1)
                    nc.scalar.activation(SG[u], bank[u][:, :], ACT.Silu).then_inc(sg_done, 1)

                def result(pairs, u, g, e):
                    act.wait_ge(y0_ps, g + 1)
                    at_least(act, y_stored[u], arrivals(l, pairs - 1))
                    copy(YO[u][:, 0:512], bank[7][:, :]).then_inc(y0_out, 1)
                    act.wait_ge(y0_out, g + 1)
                    act.wait_ge(y1_out, g + 1)
                    act.dma_start(y_view(l)[0, :, bass.ds(e, 1), :].rearrange("s o d -> s (o d)"), YO[u])\
                       .then_inc(y_stored[u], 16)

                def step(i, v):
                    u, g = (1 + v) % 2, i * 2 + (base + 1 + v)
                    silu(u, g)
                    h_copied(g - 1)
                    result(i + 1, 1 - u, g - 1, i * 2 + v)
                    round_down(i + (v + 1), u, g)

                silu(0, base)
                round_down(1, 0, base)
                step(0, 0)
                step(0, 1)
                with act.Fori(1, NE // 2 - 1) as i:
                    step(i, 0)
                    step(i, 1)
                silu(1, base + 15)
                h_copied(base + 14)
                result(8, 0, base + 14, 14)
                h_copied(base + 15)
                result(8, 1, base + 15, 15)
                overflow(l)

            def overflow(l):
                s = ov[l]
                act.wait_ge(pos_ready, l + 1)
                most = act.value_load(over_i[0:1, 0:1], min_val=0, max_val=T)
                with act.If(most > P):
                    for u in range(2):
                        act.wait_ge(y_stored[u], arrivals(l, 8))
                    with act.Fori(1, BLOCKS) as b:
                        with act.Fori(0, NE) as e:
                            n = b * NE + e - (NE - 1)
                            ov_wait(act, l, n, "gu_ps")
                            nc.scalar.activation(SG[0], bank[0][:, :], ACT.Silu).then_inc(s["act"], 1)
                            ov_wait(act, l, n, "h_ps")
                            copy(HT, heads_of(7)).then_inc(s["act"], 1)
                            ov_wait(act, l, n, "y_ps")
                            copy(YO[0][:, 0:512], bank[7][:, :]).then_inc(s["act"], 1)
                            ov_wait(act, l, n, "y_a")
                            ov_wait(act, l, n, "y_d")
                            act.dma_start(y_view(l)[bass.ds(b, 1), :, bass.ds(e, 1), :]
                                          .rearrange("q s o d -> (q s) (o d)"), YO[0]).then_inc(s["stored"], 16)
                            ov_wait(act, l, n, "stored")

            def mixer1():
                act.wait_ge(lru_par, 1)
                nc.scalar.activation(par[:, 80:88], par[:, 80:88], ACT.Exp).then_inc(lru_par, 1)
                act.wait_ge(lru_par, 2)
                nc.scalar.activation(par[:, 80:88], par[:, 80:88], ACT.Ln, bias=ones[:, 0:1]).then_inc(lru_par, 1)
                def round_w(c):
                    act.wait_ge(w1_in[(c // 2) % 4], 16 * (c // 8 + 1))
                    rounded1.end(copy(W1_HIGH[c % 2][:, :, :], W0[(c // 2) % 4][:, :, P * (c % 2):P * (c % 2) + P]),
                                 0, f"w{c}")

                round_w(0)
                act.wait_ge(lru_hist_out, 3)
                for t in range(NT):
                    act.wait_ge(xt_lo, 2 * NT + t + 1)
                    act.wait_ge(xt_hi, 2 * NT + t + 1)
                    rounded1.end(copy(XT_HIGH[:, :, tile_cols(t)], XT[:, :, tile_cols(t)]), 0, f"x{t}")
                round_w(1)
                for c in range(16):
                    pb, sbk = bank[c % 3], bank[(3, 6, 7)[c % 3]]
                    act.wait_ge(proj1_ps, c + 1)
                    if c + 2 < 16:
                        round_w(c + 2)
                    if c < KD:
                        nc.scalar.activation(YB[:, c, 0:TH], pb[:, 0:TH], ACT.Gelu_apprx_tanh)
                        nc.scalar.activation(YB[:, c, TH:T], sbk[:, 0:TH], ACT.Gelu_apprx_tanh).then_inc(proj1_out, 1)
                    else:
                        m = c - KD
                        if m >= 3:
                            act.wait_ge(conv1_done, m - 2)
                            act.wait_ge(tail1_done, m - 2)
                        buf = EXT1[m % 3]
                        copy(buf[:, CONV - 1:CONV - 1 + TH], pb[:, 0:TH])
                        copy(buf[:, CONV - 1 + TH:EXT_P], sbk[:, 0:TP - TH])
                        copy(ext_samples(buf)[:, :, CONV - 1:], sbk[:, TP - TH:TH].rearrange("p (s l) -> p s l", s=NS))\
                            .then_inc(proj1_out, 1)
                act.wait_ge(lru_par, 4)
                for ms in (range(KD // 2), range(KD // 2, KD)):
                    for m in ms:
                        for n, (to, b_at) in enumerate(((R_, 40), (GI, 48))):
                            j = 2 * m + n
                            act.wait_ge(lru_gate_ps, j + 1)
                            b0 = (4, 0, 2, 6)[j % 4]
                            bias = par[:, b_at + m:b_at + m + 1]
                            nc.scalar.activation(to[:, m, 0:TP], bank[b0][:, :], ACT.Sigmoid, bias=bias)
                            nc.scalar.activation(to[:, m, TP:T], bank[b0 + 1][:, 0:TS], ACT.Sigmoid, bias=bias)\
                                .then_inc(lru_gates_done, 1)
                    act.wait_ge(lru_gates_done, 2 * ms[-1] + 2)
                    for m in ms:
                        nc.scalar.activation(XT[:, m, :], R_[:, m, :], ACT.Exp, scale=par[:, 72 + m:73 + m])\
                            .then_inc(lru_a, 1)
                        act.wait_ge(lru_a, m + 1)
                        nc.scalar.activation(R_[:, m, :], R_[:, m, :], ACT.Tanh, scale=par[:, 64 + m:65 + m])\
                            .then_inc(lru_t, 1)
                    for m in ms:
                        act.wait_ge(lru_w, m + 1)
                        nc.scalar.activation(R_[:, m, :], R_[:, m, :], ACT.Sqrt).then_inc(lru_root, 1)

            to_channels(0)
            mixer0()
            for l in range(2):
                norm(2 * l)
                route(l)
                experts(l)
                norm(2 * l + 1)
                if l == 0:
                    to_channels(2)
                    mixer1()

        @block.vector
        def _(dve):
            mine = Own(dve, own["dve"])
            V = nc.vector

            def to_channels(n, tiles=range(NT)):
                for t in tiles:
                    dve.wait_ge(xt_ps, n * NT + t + 1)
                    V.tensor_copy(XT[:, 0:4, tile_cols(t)], heads_of(TILE_BANK(t), P, ROWS[t])).then_inc(xt_lo, 1)

            def gates():
                g = slice(32, 36)
                dve.wait_ge(gates_in, 32)
                dve.wait_ge(ab_ps, 1)
                dve.wait_ge(gate_act, 2)
                mine(V.tensor_scalar(RA[g, 0:TP], bank[4][g, :], gpar[g, 0:1], None, ALU.add))
                mine(V.tensor_scalar(RA[g, TP:T], bank[5][g, 0:TS], gpar[g, 0:1], None, ALU.add))
                mine.settle()
                V.scalar_tensor_tensor(RB[g, :], RA[g, :], -1.0, RA[g, :], ALU.mult, ALU.min).then_inc(gate_dve, 1)
                dve.wait_ge(gate_dve, 1)
                mine(V.tensor_scalar(RA[g, :], RA[g, :], 0.0, None, ALU.max))
                dve.wait_ge(gate_act, 5)
                mine.settle()
                mine(V.tensor_tensor(RB[g, :], RB[g, :], RA[g, :], ALU.add))
                mine.settle()
                mine(V.tensor_scalar(RB[g, :], RB[g, :], gpar[g, 1:2], -1.0, ALU.mult, ALU.mult))
                mine.settle()
                mine(V.tensor_tensor_scan(RT[g, :], keep[g, :], RB[g, :], 0.0, ALU.mult, ALU.add))
                mine.settle()
                for lo, n, l in ((0, TP // P, P), (TP, NS, LS)):
                    gc = RT[g, lo:lo + n * l].rearrange("p (c l) -> p c l", l=l)
                    last = V.tensor_tensor(RT[64:68, lo:lo + n * l].rearrange("p (c l) -> p c l", l=l),
                                           gc[:, :, l - 1:l].broadcast_to([4, n, l]), gc, ALU.subtract)
                last.then_inc(rows_ready, 1)

            def conv(c, buf, hist, out, taps, bias):
                mine(V.tensor_copy(ext_samples(buf)[:, :, 0:CONV - 1], hist.rearrange("p (s j) -> p s j", s=NS)))
                mine.settle()
                for j in range(CONV):
                    w = par[:, taps * j + c:taps * j + c + 1]
                    srcs = ((out[:, 0:TP], buf[:, j:j + TP]), (samples(out), ext_samples(buf)[:, :, j:j + LS]))
                    for dst, src in srcs:
                        if j == 0 and bias is not None:
                            last = V.tensor_scalar(dst, src, w, bias, ALU.mult, ALU.add)
                        elif j == 0:
                            last = V.tensor_scalar(dst, src, w, None, ALU.mult)
                        else:
                            last = V.scalar_tensor_tensor(dst, src, w, dst, ALU.mult, ALU.add)
                        if j < CONV - 1:
                            mine(last)
                    if j < CONV - 1:
                        mine.settle()
                return last

            def differences(b):
                for h in range(NH):
                    last = V.tensor_scalar(dif[:, h, :], gB[:, h, tile_cols(b)], COL[:, b, 32 + h:33 + h], None,
                                           ALU.subtract)
                d_dve.end(last, b, "dif")

            def scaled_k(b):
                d_pe.wait(dve, b, "ktr")
                for name, to, by in (("kbg", kbg, kbgc), ("kd", kd, kdc)):
                    for h in range(NH):
                        last = V.tensor_scalar(to[b % 2][:, h, :], heads_of(0)[:, h, :], by[:, b, h:h + 1], None, ALU.mult)
                    d_dve.end(last, b, name)

            def key_products(b, name, to, mask, ready):
                d_pe.wait(dve, b, "gram")
                d_pool.wait(dve, b, ready)
                for h in range(NH):
                    last = V.scalar_tensor_tensor(to[:, h, :], heads_of(2)[:, h, :], COL[:, b, h:h + 1],
                                                  mask[:, h, :], ALU.mult, ALU.mult)
                d_dve.end(last, b, name)

            def off_and_attention(b):
                key_products(b, "off", Noff[b % 2], Doff, "off")
                d_pe.wait(dve, b, "qk")
                d_pool.wait(dve, b, "incl")
                d_dve.end(V.tensor_tensor(aT[b % 2], heads_of(3), DTm, ALU.mult), b, "a")

            def delta_prompt(b):
                more = b + 1 < NT - 1
                d_act.wait(dve, b, "pt0")
                if b:
                    d_pe.wait(dve, b - 1, "sn")
                d_dve.end(V.tensor_tensor(TT, PTa, ident[:, :].unsqueeze(1).broadcast_to([P, NH, P]), ALU.add), b, "tt0")
                for r in range(1, 6):
                    d_pe.wait(dve, b, f"p{r}")
                    d_dve.end(V.tensor_copy((Pa, Pb)[r % 2], heads_of(5)), b, f"p{r}")
                    if r == 1:
                        differences(b + 1) if more else samples_differences()
                    if r == 3:
                        scaled_k(b + 1) if more else samples_k()
                    if r == 4:
                        off_and_attention(b + 1) if more else samples_attention()
                    d_pe.wait(dve, b, f"x{r}")
                    d_dve.wait(dve, b, f"tt{r - 1}")
                    d_dve.end(V.tensor_tensor(TT, TT, heads_of(7), ALU.add), b, f"tt{r}")
                d_pe.wait(dve, b, "y")
                d_dve.end(V.tensor_copy(Yo, heads_of(5)), b, "y")
                d_pe.wait(dve, b, "x6")
                d_dve.wait(dve, b, "tt5")
                d_dve.end(V.tensor_tensor(TT, TT, heads_of(7), ALU.add), b, "tt6")
                key_products(b + 1, "p0", Pa, Dbd, "bd") if more else samples_key_products()
                d_pe.wait(dve, b, "un")
                d_dve.end(V.tensor_copy(un, heads_of(5)), b, "un")
                d_pe.wait(dve, b, "sn")
                if b:
                    d_dve.wait(dve, b - 1, "s")
                for h in range(NH):
                    last = V.scalar_tensor_tensor(SP_[:, h, :], SP_[:, h, :], egl[:, h, b:b + 1], heads_of(6)[:, h, :],
                                                  ALU.mult, ALU.add)
                d_dve.end(last, b, "s")

            def samples_differences():
                b, n = NT - 1, TS
                for h in range(NH):
                    last = V.tensor_scalar(dif[0:n, h, 0:n], gB[0:n, h, tile_cols(b)], COL[0:n, b, 32 + h:33 + h], None,
                                           ALU.subtract)
                e_dve.end(last, 0, "dif")

            def samples_k():
                b, n = NT - 1, TS
                e_pe.wait(dve, 0, "ktr")
                for name, to, by in (("kbg", kbg, kbgc), ("kd", kd, kdc)):
                    for h in range(NH):
                        last = V.tensor_scalar(to[0][0:n, h, :], heads_of(0, n)[:, h, :], by[0:n, b, h:h + 1], None,
                                               ALU.mult)
                    e_dve.end(last, 0, name)

            def samples_attention():
                n = TS
                e_pe.wait(dve, 0, "qk")
                e_pool.wait(dve, 0, "incl")
                e_dve.end(V.tensor_tensor(aT[0][0:n, :, 0:n], heads_of(3, n, n), DTm[0:n, :, 0:n], ALU.mult), 0, "a")

            def samples_key_products():
                b, n = NT - 1, TS
                e_pe.wait(dve, 0, "gram")
                e_pool.wait(dve, 0, "bd")
                for h in range(NH):
                    last = V.scalar_tensor_tensor(Pa[0:n, h, 0:n], heads_of(2, n, n)[:, h, :], COL[0:n, b, h:h + 1],
                                                  Dbd[0:n, h, 0:n], ALU.mult, ALU.mult)
                e_dve.end(last, 0, "p0")

            def delta_samples():
                b, n = NT - 1, TS
                cols = tile_cols(b)
                e_act.wait(dve, 0, "pt0")
                tt = TT[0:n, :, 0:n]
                e_dve.end(V.tensor_tensor(tt, PTa[0:n, :, 0:n], ident[0:n, 0:n].unsqueeze(1).broadcast_to([n, NH, n]),
                                          ALU.add), 0, "tt0")
                for r in (1, 2):
                    e_pe.wait(dve, 0, f"p{r}")
                    e_dve.end(V.tensor_copy((Pa, Pb)[r % 2][0:n, :, 0:n], heads_of(5, n, n)), 0, f"p{r}")
                    e_pe.wait(dve, 0, f"x{r}")
                    e_dve.wait(dve, 0, f"tt{r - 1}")
                    e_dve.end(V.tensor_tensor(tt, tt, heads_of(7, n, n), ALU.add), 0, f"tt{r}")
                dve.wait_ge(rms_ps, 1)
                V.tensor_scalar(gB[0:NH, 0, 0:TP], bank[4][0:NH, :], RMS_EPS, None, ALU.add).then_inc(rms_eps, 1)
                dve.wait_ge(rms_root, 1)
                V.reciprocal(gB[0:NH, 0, 0:TP], gB[0:NH, 0, 0:TP]).then_inc(rms_inv, 1)
                e_pe.wait(dve, 0, "un")
                e_dve.end(V.tensor_copy(un[0:n, :, :], heads_of(4, n)), 0, "un")
                mine(V.tensor_copy(QKV[:, 8:12, cols], heads_of(0)[:, :, n:2 * n]))
                e_pe.wait(dve, 0, "o")
                mine.settle()
                e_dve.end(V.tensor_tensor(QKV[:, 8:12, cols], QKV[:, 8:12, cols], heads_of(1, P, n), ALU.add), 0, "o")

                def new_states(h):
                    e_pe.wait(dve, 0, f"sn{h}")
                    for s in range(NS):
                        st = SS[:, NH * s + h, :]
                        bb = ((2, 3), (5, 6))[h % 2][s // 4]
                        last = V.scalar_tensor_tensor(st, st, egl[:, h, 4 + s:5 + s], heads_of(bb)[:, s % 4, :],
                                                      ALU.mult, ALU.add)
                    e_dve.end(last, 0, f"s{h}")

                def normed(h):
                    dve.wait_ge(rmsb_ps, h + 1)
                    (b4, b7), o = ((4, 7), (0, 1))[h % 2], QKV[:, 8 + h, :]
                    V.scalar_tensor_tensor(XT[:, h, 0:TP], o[:, 0:TP], par[:, 52:53], bank[b4][:, :], ALU.mult, ALU.mult)
                    V.scalar_tensor_tensor(XT[:, h, TP:T], o[:, TP:T], par[:, 52:53], bank[b7][:, 0:TS], ALU.mult,
                                           ALU.mult).then_inc(rmsb_out, 1)

                new_states(0)
                dve.wait_ge(rms_ps, 2)
                V.tensor_scalar(gB[0:NH, 0, TP:T], bank[7][0:NH, 0:TS], RMS_EPS, None, ALU.add).then_inc(rms_eps, 1)
                new_states(1)
                dve.wait_ge(rms_root, 2)
                V.reciprocal(gB[0:NH, 0, TP:T], gB[0:NH, 0, TP:T]).then_inc(rms_inv, 1)
                normed(0)
                normed(1)
                new_states(2)
                normed(2)
                new_states(3)
                normed(3)

            def mixer0():
                dve.wait_ge(consts_ready, 1)
                V.reciprocal(inv_cnt[:, :], inv_cnt[:, :])
                dve.wait_ge(wab_sem, 16)
                V.tensor_copy(wab[:, :, 0:4], wab_in[:, :, 0:4])
                V.tensor_copy(wab[:, :, 32:36], wab_in[:, :, 4:8]).then_inc(wab_ready, 1)
                dve.wait_ge(hist_ps, 1)
                V.tensor_copy(chistT, bank[0][:, 0:288].rearrange("p (c j) -> p c j", c=NCHUNK)).then_inc(hist_out, 1)
                dve.wait_ge(hist_ps, 2)
                V.tensor_copy(U[:, :, UEP:UE].rearrange("p g (s l) -> p g s l", s=NS)[:, :, :, 0:HIST],
                              bank[1][:, 0:480].rearrange("p (g s l) -> p g s l", g=NH, s=NS)).then_inc(hist_out, 1)
                dve.wait_ge(hist_ps, 3)
                V.tensor_copy(par[:, 0:53], bank[2][:, 0:53]).then_inc(hist_out, 1)
                gates()
                dve.wait_ge(hist_out, 3)
                for c in range(NCHUNK):
                    dve.wait_ge(proj_out, c + 1)
                    if c >= 2:
                        dve.wait_ge(silu_done, c - 1)
                    conv(c, EXTB[c % 3], chistT[:, c, :], CV[:, c % 2, :], NCHUNK, None).then_inc(conv_done, 1)
                    if 3 <= c < 11:
                        n = c - 3
                        dve.wait_ge(ssq_ps, n + 1)
                        mine(V.tensor_scalar(INV[:, n, 0:TP], bank[4][:, :], L2_EPS, None, ALU.add))
                        mine(V.tensor_scalar(INV[:, n, TP:T], bank[5][:, 0:TS], L2_EPS, None, ALU.add))
                        mine.settle()
                        V.reciprocal(INV[:, n, :], INV[:, n, :]).then_inc(inv_done, 1)
                dve.wait_ge(roots_done, 2)
                dve.wait_ge(silu_done, NCHUNK)
                for h in range(NH):
                    V.scalar_tensor_tensor(QKV[:, h, :], QKV[:, h, :], float(P) ** -0.5, INV[:, h, :], ALU.mult,
                                           ALU.mult).then_inc(q_scaled, 1)
                dve.wait_ge(col_ps, 1)
                V.tensor_copy(COL[:, 0:4, :], bank[4][:, 0:272].rearrange("p (t c) -> p t c", t=4))
                V.tensor_copy(COL[0:TS, 4, :], bank[4][0:TS, 272:340]).then_inc(col_out, 1)
                for g, w in enumerate(WINDOWS):
                    dve.wait_ge(psum_done, g + 1)
                    s, u = PT_[:, g % 2, :], U[:, g, :]
                    mine(V.scalar_tensor_tensor(POOLED[:, g, w:TP], s[:, HIST + w:UEP], 1.0 / w, u[:, HIST + w:UEP],
                                                ALU.mult, ALU.subtract))
                    ss, us = (x[:, UEP:UE].rearrange("p (s l) -> p s l", s=NS)[:, :, HIST:] for x in (s, u))
                    mine(V.scalar_tensor_tensor(samples(POOLED[:, g, :]), ss, 1.0 / w, us, ALU.mult, ALU.subtract))
                    mine(V.tensor_tensor(POOLED[:, g, 0:w], s[:, HIST:HIST + w], inv_cnt[:, 0:w], ALU.mult))
                    mine.settle()
                    V.tensor_tensor(POOLED[:, g, 0:w], POOLED[:, g, 0:w], u[:, HIST:HIST + w], ALU.subtract)\
                        .then_inc(pooled_done, 1)
                dve.wait_ge(strow_ps, 1)
                V.tensor_copy(rows_out[0:HIST, 0:512], bank[4][0:HIST, :])
                V.tensor_copy(rows_out[0:120, 512:1024], bank[5][0:120, :])
                V.tensor_copy(rows_out[0:108, 1024:1408], bank[6][0:108, 0:384]).then_inc(strow_out, 1)
                dve.wait_ge(egl_done, 4)
                mine(V.tensor_tensor(kbgc[:, :, :], COL[:, :, 0:4], ecol[:, :, :], ALU.mult))
                mine.settle()
                dve.wait_ge(tail_done, NCHUNK)
                differences(0)
                dve.wait_ge(proj_ps, NPROJ)
                scaled_k(0)
                off_and_attention(0)
                key_products(0, "p0", Pa, Dbd, "bd")
                for b in range(NT - 1):
                    delta_prompt(b)
                delta_samples()

            def norm(q):
                l = q // 2

                def stats(t):
                    r, n = ROWS[t], q * NT + t
                    x, w = X[0:r, t, :], lnw[0:r, t, :]
                    if q % 2 == 0:
                        dve.wait_ge(out_ps, l * NT + t + 1)
                        for half in range(2):
                            c = slice(512 * half, 512 * half + 512)
                            last = V.scalar_tensor_tensor(x[:, c], x[:, c], ALPHA, bank[2 * (t % 2) + half][0:r, :],
                                                          ALU.mult, ALU.add)
                    else:
                        dve.wait_ge(ysel_scaled, l * NT + t + 1)
                        y1, y2 = Y1[t][0:r, :], Y2[t][0:r, :]
                        mine(V.scalar_tensor_tensor(y1, y2, wsel[0:r, 1, t:t + 1], y1, ALU.mult, ALU.add))
                        mine.settle()
                        last = V.scalar_tensor_tensor(x, x, ALPHA, y1, ALU.mult, ALU.add)
                    last.then_inc(norm_sum, 1)
                    dve.wait_ge(norm_sum, n + 1)
                    for half in range(2):
                        mine(V.bn_stats(w[:, 6 * half:6 * half + 6], x[:, 512 * half:512 * half + 512]))
                    mine.settle()
                    mine(V.bn_aggr(w[:, 12:14], w[:, 0:12]))
                    mine.settle()
                    V.tensor_scalar(w[:, 13:14], w[:, 13:14], LN_EPS, None, ALU.add).then_inc(norm_stats, 1)

                def coefficients(t):
                    w = lnw[0:ROWS[t], t, :]
                    dve.wait_ge(norm_root, q * NT + t + 1)
                    mine(V.reciprocal(w[:, 14:15], w[:, 14:15]))
                    mine.settle()
                    V.scalar_tensor_tensor(w[:, 15:16], w[:, 12:13], -1.0, w[:, 14:15], ALU.mult, ALU.mult)\
                        .then_inc(norm_coef, 1)

                def finish(t):
                    r = ROWS[t]
                    gain, bias = LNP[0:r, q % 2, 0, :], LNP[0:r, q % 2, 1, :]
                    dve.wait_ge(norm_scaled, q * NT + t + 1)
                    last = V.tensor_tensor(X[0:r, t, :], X[0:r, t, :], gain, ALU.mult)
                    if q % 2 and t < NT - 1:
                        last.then_inc(gained, 1)
                        return
                    mine(last)
                    if q % 2:
                        dve.wait_ge(norm_done, q * NT + t)
                    mine.settle()
                    V.tensor_tensor(X[0:r, t, :], X[0:r, t, :], bias, ALU.add).then_inc(norm_done, 1)

                dve.wait_ge(lnp_in[q % 2], 32 * (l + 1))
                if q % 2 == 0:
                    for t in range(NT - 1):
                        stats(t)
                        coefficients(t)
                        finish(t)
                    to_channels(q + 1, (0, 1))
                    stats(NT - 1)
                    to_channels(q + 1, (2,))
                    coefficients(NT - 1)
                    to_channels(q + 1, (3,))
                    finish(NT - 1)
                    to_channels(q + 1, (4,))
                    return
                dve.wait_ge(xrows_out, 16 * NT * (l + 1))
                stats(0)
                for t in range(NT):
                    if t + 1 < NT:
                        stats(t + 1)
                    coefficients(t)
                    if t:
                        finish(t - 1)
                finish(NT - 1)

            def route(l):
                def do(instruction):
                    mine(instruction)
                    mine.settle()

                def per(i, n):
                    return rt[:, i, 0:NT * n].rearrange("p (t g) -> p t g", t=NT)

                def places(values, out):
                    n = values.shape[1]
                    more, same = (x[:, 0:n] for x in pairs_of4)
                    other = values.unsqueeze(2).broadcast_to([P, n, 4, 4])
                    own_value = values.unsqueeze(3).broadcast_to([P, n, 4, 4])
                    mine(V.tensor_tensor(more, other, own_value, ALU.is_gt))
                    do(V.tensor_tensor(same, other, own_value, ALU.is_equal))
                    do(V.tensor_tensor(same, same, m_lower4[:, :, :].unsqueeze(1).broadcast_to([P, n, 4, 4]), ALU.mult))
                    do(V.tensor_tensor(more, more, same, ALU.add))
                    do(V.tensor_reduce(out, more, AX.X, ALU.add))

                dve.wait_ge(router_in, 32)
                dve.wait_ge(scores_done, l + 1)
                do(V.tensor_tensor(per(0, NE), scores[:, :, :], rbias[:, :].unsqueeze(1).broadcast_to([P, NT, NE]),
                                   ALU.add))
                biased, place, best = (rt[:, i, :].rearrange("p (g e) -> p g e", e=4) for i in (0, 1, 2))
                places(biased, place)
                do(V.scalar_tensor_tensor(best, place, 2.0, biased, ALU.is_lt, ALU.mult))
                group_score, group_place = per(5, 4), per(6, 4)
                do(V.tensor_reduce(rt[:, 5, 0:4 * NT], best, AX.X, ALU.add))
                places(group_score, group_place)
                do(V.tensor_scalar(rt[:, 7, 0:4 * NT], rt[:, 6, 0:4 * NT], 0.0, None, ALU.is_equal))
                group = rt[:, 7, 0:4 * NT].unsqueeze(2).broadcast_to([P, 4 * NT, 4])
                for k in range(2):
                    last = V.scalar_tensor_tensor(oh[:, k, :, :].rearrange("p t (g e) -> p (t g) e", e=4), place, float(k),
                                                  group, ALU.is_equal, ALU.mult)
                    mine(last)
                mine.settle()
                for k in range(2):
                    mine(V.tensor_tensor(per(3 + k, NE), scores[:, :, :], oh[:, k, :, :], ALU.mult))
                mine.settle()
                for k in range(2):
                    mine(V.tensor_reduce(wsel[:, k, :], per(3 + k, NE), AX.X, ALU.add))
                do(V.memset(oh[TS:P, :, NT - 1, :], 0.0))
                V.tensor_tensor(per(11, NE), oh[:, 0, :, :], oh[:, 1, :, :], ALU.add).then_inc(onehot_ready, 1)
                do(V.tensor_tensor(wsel[:, 2, :], wsel[:, 0, :], wsel[:, 1, :], ALU.add))
                do(V.reciprocal(wsel[:, 3, :], wsel[:, 2, :]))
                for k in range(2):
                    mine(V.tensor_tensor(wsel[:, k, :], wsel[:, k, :], wsel[:, 3, :], ALU.mult))
                dve.wait_ge(rank_ps, l + 1)
                do(V.tensor_copy(rt[:, 2, :], bank[0][:, 0:80]))
                before, total = per(3, NE), per(2, NE)
                do(V.memset(before[:, 0, :], 0.0))
                for t in range(1, NT):
                    do(V.tensor_tensor(before[:, t, :], before[:, t - 1, :], total[:, t - 1, :], ALU.add))
                do(V.tensor_tensor(rt[:, 4, 0:NE], before[:, NT - 1, :], total[:, NT - 1, :], ALU.add))
                do(V.tensor_reduce(rt[:, 5, 0:1], rt[:, 4, 0:NE], AX.X, ALU.max))
                do(V.tensor_copy(over_i[:, :], rt[0:1, 5, 0:1]))
                do(V.tensor_tensor(rt[:, 3, :], rt[:, 3, :], bank[1][:, 0:80], ALU.add))
                do(V.scalar_tensor_tensor(per(3, NE), per(3, NE), float(NE),
                                          iota16[:, :].unsqueeze(1).broadcast_to([P, NT, NE]), ALU.mult, ALU.add))
                for k in range(2):
                    mine(V.tensor_tensor(per(8 + k, NE), per(3, NE), oh[:, k, :, :], ALU.mult))
                mine.settle()
                for k in range(2):
                    mine(V.tensor_reduce(rt[:, 6 + k, 0:NT], per(8 + k, NE), AX.X, ALU.add))
                mine.settle()
                V.tensor_copy(pos_i[:, :, :], rt[:, 6:8, 0:NT]).then_inc(pos_ready, 1)

            def experts(l):
                base = NE * l

                def x_copied(g):
                    dve.wait_ge(xg_ps, g + 1)
                    V.tensor_copy(XGT[:, 0:4, :], heads_of(4)).then_inc(xgt_ready, 1)
                    V.tensor_copy(XGT[:, 4:8, :], heads_of(5)).then_inc(xgt_ready, 1)

                def h_product(u, g):
                    dve.wait_ge(up_ps, g + 1)
                    dve.wait_ge(sg_done, g + 1)
                    at_least(dve, h_ps, g - 1)
                    V.tensor_tensor(HB[u], SG[u], bank[2 + u][:, :], ALU.mult).then_inc(h_ready, 1)

                def result(pairs, u, g):
                    dve.wait_ge(y1_ps, g + 1)
                    at_least(dve, y_stored[u], arrivals(l, pairs - 1))
                    V.tensor_copy(YO[u][:, 512:1024], bank[6][:, :]).then_inc(y1_out, 1)

                def split_down(u, g):
                    dve.wait_ge(down_rounded, g + (1 - l))
                    for f in range(4):
                        if f == 2:
                            dve.wait_ge(ht_ready, g + 1)
                            V.tensor_tensor(HT_LOW[:, :, :], HT, HT_HIGH[:, :, :].bitcast(F32), ALU.subtract)
                        last = V.tensor_tensor(WDN_LOW[u][:, f, :], WDN[u][:, f, :], WDN_HIGH[:, f, :].bitcast(F32),
                                               ALU.subtract)
                    last.then_inc(down_split, 1)

                def step(i, v):
                    u, g = (1 + v) % 2, i * 2 + (base + 1 + v)
                    h_product(u, g)
                    x_copied(g + 1)
                    result(i + 1, 1 - u, g - 1)
                    split_down(u, g)

                x_copied(base)
                h_product(0, base)
                x_copied(base + 1)
                split_down(0, base)
                step(0, 0)
                step(0, 1)
                with dve.Fori(1, NE // 2 - 1) as i:
                    step(i, 0)
                    step(i, 1)
                h_product(1, base + 15)
                result(8, 0, base + 14)
                result(8, 1, base + 15)
                overflow(l)

            def overflow(l):
                s = ov[l]
                dve.wait_ge(pos_ready, l + 1)
                most = dve.value_load(over_i[0:1, 0:1], min_val=0, max_val=T)
                with dve.If(most > P):
                    with dve.Fori(1, BLOCKS) as b:
                        with dve.Fori(0, NE) as e:
                            n = b * NE + e - (NE - 1)
                            ov_wait(dve, l, n, "x_ps")
                            V.tensor_copy(XGT[:, 0:4, :], heads_of(4))
                            V.tensor_copy(XGT[:, 4:8, :], heads_of(5)).then_inc(s["dve"], 1)
                            ov_wait(dve, l, n, "gu_ps")
                            ov_wait(dve, l, n, "sg")
                            V.tensor_tensor(HB[0], SG[0], bank[2][:, :], ALU.mult).then_inc(s["dve"], 1)
                            ov_wait(dve, l, n, "y_ps")
                            V.tensor_copy(YO[0][:, 512:1024], bank[6][:, :]).then_inc(s["dve"], 1)

            def mixer1():
                dve.wait_ge(lru_hist_ps, 1)
                V.tensor_copy(lhistT, bank[0][:, 0:192].rearrange("p (c j) -> p c j", c=KD)).then_inc(lru_hist_out, 1)
                dve.wait_ge(lru_hist_ps, 2)
                V.tensor_copy(lstateT, bank[1][:, 0:64].rearrange("p (c s) -> p c s", c=KD)).then_inc(lru_hist_out, 1)
                dve.wait_ge(lru_hist_ps, 3)
                V.tensor_copy(par[:, 0:64], bank[2][:, 0:64]).then_inc(lru_hist_out, 1)
                dve.wait_ge(lru_hist_out, 3)
                lam, c, nc_, tmp = par[:, 56:64], par[:, 64:72], par[:, 72:80], par[:, 80:88]
                V.scalar_tensor_tensor(tmp, lam, -1.0, lam, ALU.mult, ALU.min).then_inc(lru_par, 1)
                mine(V.tensor_scalar(c, lam, -1.0, 0.0, ALU.mult, ALU.max))
                dve.wait_ge(lru_par, 3)
                mine.settle()
                mine(V.tensor_tensor(c, c, tmp, ALU.add))
                mine.settle()
                mine(V.tensor_scalar(nc_, c, -8.0, None, ALU.mult))
                mine.settle()
                V.tensor_scalar(c, c, 8.0, None, ALU.mult).then_inc(lru_par, 1)
                def split_w(c):
                    rounded1.wait(dve, 0, f"w{c}")
                    cols = slice(P * (c % 2), P * (c % 2) + P)
                    split1.end(V.tensor_tensor(W1_LOW[(c // 2) % 4][:, :, cols], W0[(c // 2) % 4][:, :, cols],
                                               W1_HIGH[c % 2][:, :, :].bitcast(F32), ALU.subtract), 0, f"w{c}")

                split_w(0)
                for t in range(NT):
                    rounded1.wait(dve, 0, f"x{t}")
                    split1.end(V.tensor_tensor(XT_LOW[:, :, tile_cols(t)], XT[:, :, tile_cols(t)],
                                               XT_HIGH[:, :, tile_cols(t)].bitcast(F32), ALU.subtract), 0, f"x{t}")
                for c in range(1, KD + 2):
                    split_w(c)
                for m in range(KD):
                    if m + KD + 2 < 16:
                        split_w(m + KD + 2)
                    dve.wait_ge(proj1_out, KD + m + 1)
                    if m < 3:
                        dve.wait_ge(ext1_zeroed, 1)
                    conv(m, EXT1[m % 3], lhistT[:, m, :], XC[:, m, :], KD, par[:, 32 + m:33 + m]).then_inc(conv1_done, 1)
                def root_input(m):
                    dve.wait_ge(lru_t, m + 1)
                    dve.wait_ge(lru_a2, m + 1)
                    V.scalar_tensor_tensor(R_[:, m, :], TMP[:, m % 2, :], 1.0, R_[:, m, :], ALU.add, ALU.mult)\
                        .then_inc(lru_w, 1)

                def recurrence(m):
                    a, bt, h = XT[:, m, :], GI[:, m, :], XC[:, m, :]
                    dve.wait_ge(lru_root, m + 1)
                    dve.wait_ge(lru_x, m + 1)
                    mine(V.tensor_tensor(bt, R_[:, m, :], bt, ALU.mult))
                    mine(V.tensor_tensor(lru_init[:, m, :], samples(a)[:, :, 0], lstateT[:, m, :], ALU.mult))
                    mine.settle()
                    mine(V.tensor_tensor(samples(bt)[:, :, 0], samples(bt)[:, :, 0], lru_init[:, m, :], ALU.add))
                    mine(V.memset(samples(a)[:, :, 0], 0.0))
                    mine.settle()
                    mine(V.tensor_tensor_scan(h, a, bt, 0.0, ALU.mult, ALU.add))
                    mine.settle()
                    V.tensor_copy(lru_last[:, m:m + 1], h[:, TP - 1:TP])
                    V.tensor_copy(lru_last[:, 8:72].rearrange("p (s c) -> p s c", s=NS)[:, :, m],
                                  samples(h)[:, :, LS - 1]).then_inc(lru_h, 1)

                for ms in (range(KD // 2), range(KD // 2, KD)):
                    for m in ms:
                        root_input(m)
                    for m in ms:
                        recurrence(m)
                dve.wait_ge(norm_done, 2 * NT)
                dve.wait_ge(st1_ps, 1)
                V.tensor_copy(rows_out[0:108, 0:256], bank[4][0:108, 0:256]).then_inc(st1_out, 1)
                dve.wait_ge(st1_ps, 2)
                V.tensor_copy(rows_out[0:72, 256:384], bank[5][0:72, 0:128]).then_inc(st1_out, 1)

            to_channels(0)
            mixer0()
            for l in range(2):
                norm(2 * l)
                route(l)
                experts(l)
                norm(2 * l + 1)
                if l == 0:
                    to_channels(2)
                    mixer1()

        @block.gpsimd
        def _(pool):
            mine = Own(pool, own["pool"])
            G = nc.gpsimd

            def do(instruction):
                mine(instruction)
                mine.settle()

            def keep_where(m, pattern, base, mult, fill=0.0, op=ALU.is_ge):
                do(G.affine_select(out=m, in_=m, compare_op=op, fill=fill, base=base, pattern=pattern,
                                   channel_multiplier=mult))

            def constants():
                for m, v in ((ident, 0.0), (ones, 1.0), (m_strict_bd, -1.0), (m_strict_off, -1.0), (m_strict_s, -1.0),
                             (m_incl, 1.0), (m_incl_s, 1.0), (m_before, 1.0), (own_sample, 1.0), (ms_col, 0.0),
                             (m_lower4, 1.0), (sel_gc, 0.0), (sel_row, 0.0), (COL, 0.0), (scores, 0.5)):
                    mine(G.memset(m[:], v))
                mine(G.memset(zero_i[:, :], 0))
                mine(G.memset(RT, 0.0))
                mine(G.memset(keep, 1.0))
                mine(G.memset(wab, 0.0))
                mine(G.memset(U[:, :, 0:HIST], 0.0))
                for buf in EXTB:
                    mine(G.memset(buf[:, 0:CONV - 1], 0.0))
                do(G.iota(tok_id[:, :], pattern=[[P, NT]], base=0, channel_multiplier=1))
                mine(G.memset(keep[:, 0:TP].rearrange("p (c l) -> p c l", l=P)[:, :, 0], 0.0))
                mine(G.memset(keep[:, TP:T].rearrange("p (c l) -> p c l", l=LS)[:, :, 0], 0.0))
                keep_where(ident[:, :], [[-1, P]], 0, 1, 1.0, ALU.not_equal)
                keep_where(m_strict_bd[:, :], [[-1, P]], -1, 1)
                keep_where(m_strict_bd[:, :].rearrange("p (b c) -> p b c", b=2), [[-64, 2], [0, 64]], 0, 1)
                keep_where(m_strict_bd[:, :].rearrange("p (b c) -> p b c", b=2), [[64, 2], [0, 64]], 63, -1)
                keep_where(m_strict_off[:, :], [[0, P]], -64, 1)
                keep_where(m_strict_off[:, :], [[-1, P]], 63, 0)
                by_sample = m_strict_s[:, :].rearrange("p (s l) -> p s l", s=NS)
                keep_where(m_strict_s[:, :], [[-1, TS]], -1, 1)
                keep_where(by_sample, [[-LS, NS], [0, LS]], 0, 1)
                keep_where(by_sample, [[LS, NS], [0, LS]], LS - 1, -1)
                by_sample = m_incl_s[:, :].rearrange("p (s l) -> p s l", s=NS)
                keep_where(m_incl[:, :], [[1, P]], 0, -1)
                keep_where(m_incl_s[:, :], [[1, TS]], 0, -1)
                keep_where(by_sample, [[-LS, NS], [0, LS]], 0, 1)
                keep_where(by_sample, [[LS, NS], [0, LS]], LS - 1, -1)
                keep_where(m_before[:, :], [[1, P]], -1, -1)
                keep_where(own_sample[:, :], [[-LS, NS]], 0, 1)
                keep_where(own_sample[:, :], [[LS, NS]], LS - 1, -1)
                keep_where(sel_gc[:, :, :], [[-1, NH], [0, P]], -32, 1, 1.0, ALU.not_equal)
                keep_where(sel_row[:, :, :], [[-1, NH], [0, P]], 0, 1, 1.0, ALU.not_equal)
                keep_where(ms_col[:, :, :], [[1, NH], [-1, NH]], 0, 0, 1.0 / P, ALU.not_equal)
                keep_where(m_lower4[:, :, :], [[1, 4], [-1, 4]], -1, 0)
                do(G.iota(iota_i[:, :], pattern=[[1, NE]], base=0, channel_multiplier=0))
                do(G.tensor_copy(iota16[:, :], iota_i[:, :]))
                do(G.iota(iota_i[:, :], pattern=[[1, 16]], base=1, channel_multiplier=0))
                G.tensor_copy(inv_cnt[:, :], iota_i[:, :]).then_inc(consts_ready, 1)

            def tail(ready, n, buf, to, c, done):
                pool.wait_ge(ready, n)
                G.tensor_copy(to[:, 0:3, c], buf[:, TP:TP + 3])
                G.tensor_copy(to[:, 3:27, c].rearrange("p (s j) -> p s j", s=NS), ext_samples(buf)[:, :, LS:LS + 3])\
                    .then_inc(done, 1)

            def spread(mask, n):
                return mask[0:n, 0:n].unsqueeze(1).broadcast_to([n, NH, n])

            def decays(st, n, dv, ac, i, strict, incl, off):
                cut = lambda x: x[0:n, :, 0:n]
                dv.wait(pool, i, "dif")
                st.end(G.tensor_scalar(cut(dmx), cut(dif), 0.0, None, ALU.max), i, "max")
                st.end(G.tensor_scalar(cut(dmn), cut(dif), 0.0, None, ALU.min), i, "min")
                ac.wait(pool, i, "dbd")
                st.end(G.tensor_tensor(cut(Dbd), cut(dmx), spread(strict, n), ALU.mult), i, "bd")
                if off is not None:
                    st.end(G.tensor_tensor(cut(Doff), cut(dmx), spread(off, n), ALU.mult), i, "off")
                ac.wait(pool, i, "dt")
                st.end(G.tensor_tensor(cut(DTm), cut(dmn), spread(incl, n), ALU.mult), i, "incl")

            def decayed_q(st, b, n, ac, pe_, i, off):
                cols = tile_cols(b)
                ac.wait(pool, i, "eg")
                pe_.wait(pool, i, "qk")
                if off is None:
                    d_pe.wait(pool, NT - 2, "un")
                to = QKV[:, 0:4, cols] if off is not None else nwT[:, :, n:2 * n]
                st.end(G.tensor_tensor(to, QKV[:, 0:4, cols], egB[:, :, 0:n], ALU.mult), i, "qd")

            def mixer0():
                for n, src in enumerate((a_dt_bias, a_log_decay)):
                    pool.dma_start(gpar[32:36, n:n + 1], src.rearrange("o h -> h o")).then_inc(gates_in, 16)
                for c in range(NCHUNK):
                    tail(proj_out, c + 1, EXTB[c % 3], tails, c, tail_done)
                pool.wait_ge(conv_done, NCHUNK)
                for g in range(NH):
                    pool.wait_ge(proj_out, NCHUNK + g + 1)
                    if g:
                        pool.wait_ge(pooled_done, g)
                    src = U[:, g, :]
                    for k in range(g + 1):
                        sh, lo = 1 << k, (2 << k) - 1
                        last = G.tensor_tensor(PT_[:, k % 2, lo:UE], src[:, lo:UE], src[:, lo - sh:UE - sh], ALU.add)
                        if k < g:
                            do(last)
                        src = PT_[:, k % 2, :]
                    last.then_inc(psum_done, 1)
                pool.wait_ge(ssq_ps, 8)
                for g in range(NH):
                    last = G.tensor_copy(utail[:, g, :].rearrange("p (s l) -> p s l", s=NS),
                                         U[:, g, UEP:UE].rearrange("p (s l) -> p s l", s=NS)[:, :, LS:LS + HIST])
                last.then_inc(utail_done, 1)
                pool.wait_ge(roots_done, 2)
                for h in range(NH):
                    G.tensor_tensor(QKV[:, 4 + h, :], QKV[:, 4 + h, :], INV[:, 4 + h, :], ALU.mult).then_inc(k_scaled, 1)
                pool.wait_ge(silu_done, NCHUNK)
                pool.wait_ge(strow_out, 1)
                G.memset(SP_, 0.0).then_inc(s_zeroed, 1)
                decays(d_pool, P, d_dve, d_act, 0, m_strict_bd, m_incl, m_strict_off)
                for b in range(NT - 1):
                    decayed_q(d_pool, b, P, d_act, d_pe, b, m_strict_off)
                    if b + 1 < NT - 1:
                        decays(d_pool, P, d_dve, d_act, b + 1, m_strict_bd, m_incl, m_strict_off)
                decays(e_pool, TS, e_dve, e_act, 0, m_strict_s, m_incl_s, None)
                decayed_q(e_pool, NT - 1, TS, e_act, e_pe, 0, None)
                e_dve.wait(pool, 0, "un")
                for h in range(NH):
                    if h >= 2:
                        e_pe.wait(pool, 0, f"sn{h - 2}")
                    e_pool.end(G.tensor_tensor(UB[h % 2][0:TS, :, :], un[0:TS, h, :].unsqueeze(1).broadcast_to([TS, NS, P]),
                                               own_sample[:, :].unsqueeze(2).broadcast_to([TS, NS, P]), ALU.mult),
                               0, f"ub{h}")
                for h in range(NH):
                    pool.wait_ge(rmsb_out, h + 1)
                    G.tensor_tensor(XT[:, h, :], XT[:, h, :], Z[:, h, :], ALU.mult).then_inc(mix_a, 1)

            def select_and_bias(l):
                def select(rows):
                    for t in range(NT):
                        for k, to in enumerate((Y1, Y2)):
                            pool.indirect_dma_start(
                                out=to[t][0:ROWS[t], :], out_offset=None, in_=rows,
                                in_offset=bass.IndirectOffsetOnAxis(ap=pos_i[0:ROWS[t], k, t:t + 1], axis=0),
                            ).then_inc(ysel_in[t], 16)

                for u in range(2):
                    pool.wait_ge(y_stored[u], arrivals(l, 8))
                with pool.If(most_tokens() > P):
                    overflow(l)
                    select(y_rows[l])
                with pool.Else():
                    select(y_rows[l][0:P * NE, :])
                pool.wait_ge(lnp_in[1], 32 * (l + 1))
                for t in range(NT - 1):
                    pool.wait_ge(gained, l * (NT - 1) + t + 1)
                    G.tensor_tensor(X[:, t, :], X[:, t, :], LNP[:, 1, 1, :], ALU.add).then_inc(norm_done, 1)

            def experts(l):
                base = NE * l

                def gather(u, g, e):
                    at_least(pool, xg_ps, g - 1)
                    G.tensor_copy(idx_cur[:, u:u + 1], idx_all[:, 0, bass.ds(e, 1)])
                    pool.drain()
                    pool.indirect_dma_start(
                        out=XG[u], out_offset=None, in_=x_rows[l],
                        in_offset=bass.IndirectOffsetOnAxis(ap=idx_cur[:, u:u + 1], axis=0)).then_inc(xg_in[u], 16)

                pool.wait_ge(lists_zeroed, 32)
                pool.wait_ge(pos_ready, l + 1)
                for t in range(NT):
                    for k in range(2):
                        pool.indirect_dma_start(
                            out=slot_list[l], in_=tok_id[0:ROWS[t], t:t + 1], in_offset=None,
                            out_offset=bass.IndirectOffsetOnAxis(ap=pos_i[0:ROWS[t], k, t:t + 1], axis=0),
                        ).then_inc(tok_scattered, 16)
                pool.wait_ge(state_out, 16 * 8)
                pool.wait_ge(idx_in, 16 * (l + 1))
                pool.wait_ge(xrows_out, 16 * NT * (l + 1))
                gather(0, base, 0)
                gather(1, base + 1, 1)
                with pool.Fori(1, NE // 2) as i:
                    for u in range(2):
                        gather(u, i * 2 + (base + u), i * 2 + u)

            def most_tokens():
                return pool.value_load(over_i[0:1, 0:1], min_val=0, max_val=T)

            def overflow(l):
                s = ov[l]
                with pool.Fori(1, BLOCKS) as b:
                    with pool.Fori(0, NE) as e:
                        n = b * NE + e - (NE - 1)
                        ov_buffers_free(pool, l, n)
                        G.tensor_copy(idx_cur[:, 0:1], idx_all[:, bass.ds(b, 1), bass.ds(e, 1)]
                                      .rearrange("p b e -> p (b e)"))
                        pool.drain()
                        pool.indirect_dma_start(
                            out=XG[0], out_offset=None, in_=x_rows[l],
                            in_offset=bass.IndirectOffsetOnAxis(ap=idx_cur[:, 0:1], axis=0)).then_inc(s["xg"], 16)
                ov_wait(pool, l, NE * (BLOCKS - 1), "stored")

            def mixer1():
                for buf in EXT1:
                    last = G.memset(buf[:, 0:CONV - 1], 0.0)
                last.then_inc(ext1_zeroed, 1)
                for m in range(KD):
                    tail(proj1_out, KD + m + 1, EXT1[m % 3], tails1, m, tail1_done)
                pool.wait_ge(conv1_done, KD)

                def gated_input(m):
                    pool.wait_ge(lru_gates_done, 2 * m + 2)
                    G.tensor_tensor(GI[:, m, :], GI[:, m, :], XC[:, m, :], ALU.mult).then_inc(lru_x, 1)

                def squared(m):
                    pool.wait_ge(lru_a, m + 1)
                    if m >= 2:
                        pool.wait_ge(lru_w, m - 1)
                    G.tensor_tensor(TMP[:, m % 2, :], XT[:, m, :], XT[:, m, :], ALU.mult).then_inc(lru_a2, 1)

                def result(m):
                    pool.wait_ge(lru_h, m + 1)
                    G.tensor_tensor(XT[:, m, :], XC[:, m, :], YB[:, m, :], ALU.mult).then_inc(mix_a, 1)

                half = KD // 2
                for m in range(half):
                    gated_input(m)
                for m in range(half):
                    squared(m)
                for m in range(half):
                    gated_input(half + m)
                    result(m)
                for m in range(half):
                    squared(half + m)
                for m in range(half):
                    result(half + m)

            constants()
            mixer0()
            for l in range(2):
                experts(l)
                select_and_bias(l)
                if l == 0:
                    mixer1()


_INS = ['x_prompt', 'x_sample', 'state_delta', 'state_delta_conv', 'state_pool', 'state_lru', 'state_lru_conv',
        'ab_w_in', 'a_conv_w', 'a_log_decay', 'a_dt_bias', 'a_norm_w', 'b_w_group', 'b_scale', 'ab_w_out',
        'c_w_in', 'c_conv_w', 'c_conv_b', 'c_w_r', 'c_b_r', 'c_w_i', 'c_b_i', 'c_lambda', 'c_w_out',
        'ln_mix_g', 'ln_mix_b', 'ln_ffn_g', 'ln_ffn_b', 'router_w', 'router_bias',
        'moe_w_gate', 'moe_w_up', 'moe_w_down']
_OUTS = [(1, 512, 1024), (8, 8, 1024), (1, 1, 4, 128, 128), (1, 1, 3, 1536), (1, 1, 15, 512), (1, 1, 1024),
         (1, 1, 3, 1024), (1, 8, 4, 128, 128), (1, 8, 3, 1536), (1, 8, 15, 512), (1, 8, 1024), (1, 8, 3, 1024)]


def kernel(**inputs):
    import numpy as _np
    import concourse.bacc as _bacc
    from concourse import mybir as _mybir
    from concourse.bass_utils import run_bass_kernel_spmd as _run

    nc = _bacc.Bacc("TRN2", target_bir_lowering=False, num_devices=1)
    arrays, args = {}, []
    for name in _INS:
        a = _np.ascontiguousarray(inputs[name])
        arrays[f"in_{name}_dram"] = a
        args.append(nc.dram_tensor(f"in_{name}_dram", a.shape, _mybir.dt.from_np(a.dtype), kind="ExternalInput").ap())
    for i, shape in enumerate(_OUTS):
        args.append(nc.dram_tensor(f"out_{i}_dram", shape, _mybir.dt.float32, kind="ExternalOutput").ap())
    hybrid_trunk(nc, *args)
    r = _run(nc, [arrays], core_ids=[0])
    return tuple(r.results[0][f"out_{i}_dram"] for i in range(len(_OUTS)))
```
